# Optimizing a Trainium2 kernel written in Bass

```python
import math
import jax, jax.numpy as jnp
from jax import lax
import numpy as np

D_MODEL = 1024
BATCH = 1
SEQ = 512
DEPTH = 2

DA_HEADS = 4
DA_QK_DIM = 64
DA_V_DIM = 2 * DA_QK_DIM
DA_QK_WIDTH = DA_HEADS * 2 * DA_QK_DIM
DA_WIDTH = DA_HEADS * DA_V_DIM
ROPE_THETA = 500000.0
ROT_DIM = DA_QK_DIM // 4
Q_BLOCK = 128
HG_HEADS = 4
HG_K_DIM = 128
HG_V_DIM = 128
HG_K_WIDTH = HG_HEADS * HG_K_DIM
HG_V_WIDTH = HG_HEADS * HG_V_DIM
HG_CHUNK = 64
FFN_HIDDEN = -(-8 * D_MODEL // (3 * 256)) * 256
NORM_EPS = 1e-6
IN_SIZES = (DA_QK_WIDTH, DA_QK_WIDTH, DA_WIDTH,
            HG_K_WIDTH, HG_K_WIDTH, HG_K_WIDTH, HG_V_WIDTH, HG_V_WIDTH,
            D_MODEL, D_MODEL)
IN_WIDTH = sum(IN_SIZES)


def rmsnorm(x, gain):
    xf = x.astype(jnp.float32)
    y = xf * lax.rsqrt(jnp.mean(xf * xf, axis=-1, keepdims=True) + NORM_EPS)
    return (y * gain.astype(jnp.float32)).astype(x.dtype)

def split_columns(p):
    outs, start = [], 0
    for size in IN_SIZES:
        outs.append(p[..., start:start + size])
        start += size
    return outs

def rope_tables(positions):
    inv_freq = ROPE_THETA ** (-(jnp.arange(0, ROT_DIM, 2, dtype=jnp.float32) / ROT_DIM))
    ang = positions.astype(jnp.float32)[..., None] * inv_freq
    return jnp.cos(ang), jnp.sin(ang)

def apply_partial_rope(t, cos, sin):
    c = cos[:, :, None, None, :].astype(t.dtype)
    s = sin[:, :, None, None, :].astype(t.dtype)
    half = ROT_DIM // 2
    t1 = t[..., :half]
    t2 = t[..., half:ROT_DIM]
    rot = jnp.concatenate([t1 * c - t2 * s, t2 * c + t1 * s], axis=-1)
    return jnp.concatenate([rot, t[..., ROT_DIM:]], axis=-1)

def diff_attention(h_q, h_k, h_v, cos, sin, lam, norm_gain, layer):
    B, S, _ = h_q.shape
    q = h_q.reshape(B, S, DA_HEADS, 2, DA_QK_DIM)
    k = h_k.reshape(B, S, DA_HEADS, 2, DA_QK_DIM)
    v = h_v.reshape(B, S, DA_HEADS, DA_V_DIM)
    q = apply_partial_rope(q, cos, sin) * (DA_QK_DIM ** -0.5)
    k = apply_partial_rope(k, cos, sin)
    lam_init = 0.8 - 0.6 * math.exp(-0.3 * layer)
    l32 = lam.astype(jnp.float32)
    lam_full = (jnp.exp(jnp.sum(l32[0] * l32[1])) - jnp.exp(jnp.sum(l32[2] * l32[3]))
                + lam_init)
    nq = S // Q_BLOCK
    qb = q.reshape(B, nq, Q_BLOCK, DA_HEADS, 2, DA_QK_DIM).transpose(1, 0, 2, 3, 4, 5)

    def block(qi):
        s = jnp.einsum('bqhcd,bkhcd->bhcqk', qi, k).astype(jnp.float32)
        p = jax.nn.softmax(s, axis=-1)
        w = p[:, :, 0] - lam_full * p[:, :, 1]
        return jnp.einsum('bhqk,bkhv->bqhv', w.astype(v.dtype), v)

    o = lax.map(block, qb)
    o = o.transpose(1, 0, 2, 3, 4).reshape(B, S, DA_HEADS, DA_V_DIM)
    o = rmsnorm(o, norm_gain.reshape(DA_HEADS, DA_V_DIM)) * (1.0 - lam_init)
    return o.reshape(B, S, DA_WIDTH)

def hgrn_lower_bounds(lb_logits):
    p = jax.nn.softmax(lb_logits.astype(jnp.float32), axis=1)
    c = jnp.cumsum(p, axis=1)
    return c - c[:, :1]

def log_forget(z, lb):
    return jnp.logaddexp(jnp.log(lb), jnp.log1p(-lb) + jax.nn.log_sigmoid(z))

def chunk_scan(q, k, g, v):
    B, S, H, dk = q.shape
    dv = v.shape[-1]
    n = S // HG_CHUNK

    def to_chunks(t):
        return t.reshape(B, n, HG_CHUNK, H, t.shape[-1]).transpose(1, 0, 3, 2, 4)

    tril = jnp.tril(jnp.ones((HG_CHUNK, HG_CHUNK), dtype=bool))

    def step(state, inp):
        qc, kc, gc, vc = inp
        b = jnp.cumsum(gc, axis=2)
        inter = jnp.einsum('bhck,bhkv->bhcv', qc * jnp.exp(b), state)
        diff = b[:, :, :, None, :] - b[:, :, None, :, :]
        decay = jnp.exp(jnp.where(tril[:, :, None], diff, -jnp.inf))
        scores = jnp.einsum('bhtk,bhsk,bhtsk->bhts', qc, kc, decay)
        intra = jnp.einsum('bhts,bhsv->bhtv', scores, vc)
        b_last = b[:, :, -1, :]
        state = (jnp.exp(b_last)[..., None] * state
                 + jnp.einsum('bhck,bhcv->bhkv', kc * jnp.exp(b_last[:, :, None, :] - b), vc))
        return state, inter + intra

    s0 = jnp.zeros((B, H, dk, dv), jnp.float32)
    _, out = lax.scan(step, s0, (to_chunks(q), to_chunks(k), to_chunks(g), to_chunks(v)))
    return out.transpose(1, 0, 3, 2, 4).reshape(B, S, H, dv)

def hgrn2_bidirectional(h_q, h_ff, h_fb, h_i, h_g, lb_f, lb_b, norm_gain):
    B, S, _ = h_q.shape
    f32 = jnp.float32
    q = h_q.astype(f32).reshape(B, S, HG_HEADS, HG_K_DIM)
    v = h_i.astype(f32).reshape(B, S, HG_HEADS, HG_V_DIM)
    g_f = log_forget(h_ff.astype(f32).reshape(B, S, HG_HEADS, HG_K_DIM),
                     lb_f.reshape(HG_HEADS, HG_K_DIM))
    g_b = log_forget(h_fb.astype(f32).reshape(B, S, HG_HEADS, HG_K_DIM),
                     lb_b.reshape(HG_HEADS, HG_K_DIM))
    k_f = -jnp.expm1(g_f)
    k_b = -jnp.expm1(g_b)
    out_f = chunk_scan(q, k_f, g_f, v)
    out_b = chunk_scan(q[:, ::-1], k_b[:, ::-1], g_b[:, ::-1], v[:, ::-1])[:, ::-1]
    o = rmsnorm(out_f + out_b, norm_gain.reshape(HG_HEADS, HG_V_DIM))
    o = o * jax.nn.sigmoid(h_g.astype(f32).reshape(B, S, HG_HEADS, HG_V_DIM))
    return o.reshape(B, S, HG_V_WIDTH).astype(h_q.dtype)

def first_inputs(seed: int = 0) -> dict:
    key = jax.random.key(seed)
    ks = jax.random.split(key, 18)
    nrm = jax.random.normal
    f32 = jnp.float32
    x = nrm(ks[0], (BATCH, SEQ, D_MODEL), f32)
    offset = jax.random.randint(ks[1], (BATCH, 1), 0, 1024, dtype=jnp.int32)
    positions = offset + jnp.arange(SEQ, dtype=jnp.int32)[None, :]
    w_in = nrm(ks[2], (DEPTH, D_MODEL, IN_WIDTH), f32) * D_MODEL ** -0.5
    da_lambda = nrm(ks[3], (DEPTH, 4, DA_QK_DIM), f32) * 0.1
    da_norm = 1.0 + 0.02 * nrm(ks[4], (DEPTH, DA_WIDTH), f32)
    hg_lb_logits = 0.5 * nrm(ks[5], (2, DEPTH, HG_K_WIDTH), f32)
    hg_norm = 1.0 + 0.02 * nrm(ks[6], (DEPTH, HG_V_WIDTH), f32)
    w_a = nrm(ks[7], (DEPTH, DA_WIDTH, D_MODEL), f32) * DA_WIDTH ** -0.5
    w_b = nrm(ks[8], (DEPTH, HG_V_WIDTH, D_MODEL), f32) * HG_V_WIDTH ** -0.5
    w_o = nrm(ks[9], (DEPTH, D_MODEL, D_MODEL), f32) * D_MODEL ** -0.5
    attn_norm = 1.0 + 0.02 * nrm(ks[10], (DEPTH, D_MODEL), f32)
    ffn_norm = 1.0 + 0.02 * nrm(ks[11], (DEPTH, D_MODEL), f32)
    w_gate = nrm(ks[12], (DEPTH, D_MODEL, FFN_HIDDEN), f32) * D_MODEL ** -0.5
    w_up = nrm(ks[13], (DEPTH, D_MODEL, FFN_HIDDEN), f32) * D_MODEL ** -0.5
    w_down = nrm(ks[14], (DEPTH, FFN_HIDDEN, D_MODEL), f32) * FFN_HIDDEN ** -0.5
    final_norm = 1.0 + 0.02 * nrm(ks[15], (D_MODEL,), f32)
    return {"x": x, "positions": positions, "w_in": w_in, "da_lambda": da_lambda,
            "da_norm": da_norm, "hg_lb_logits": hg_lb_logits, "hg_norm": hg_norm,
            "w_a": w_a, "w_b": w_b, "w_o": w_o, "attn_norm": attn_norm,
            "ffn_norm": ffn_norm, "w_gate": w_gate, "w_up": w_up, "w_down": w_down,
            "final_norm": final_norm}

def first_block(x, positions, w_in, da_lambda, da_norm, hg_lb_logits, hg_norm, w_a, w_b,
              w_o, attn_norm, ffn_norm, w_gate, w_up, w_down, final_norm):
    cos, sin = rope_tables(positions)
    lbs = hgrn_lower_bounds(hg_lb_logits)
    for layer in range(DEPTH):
        h = rmsnorm(x, attn_norm[layer])
        proj = h @ w_in[layer]
        (a_q, a_k, a_v, b_q, b_ff, b_fb, b_i, b_g, gate_a, gate_b) = split_columns(proj)
        y_a = diff_attention(a_q, a_k, a_v, cos, sin, da_lambda[layer], da_norm[layer],
                             layer) @ w_a[layer]
        y_b = hgrn2_bidirectional(b_q, b_ff, b_fb, b_i, b_g,
                                  lbs[0, layer].astype(x.dtype).astype(jnp.float32),
                                  lbs[1, layer].astype(x.dtype).astype(jnp.float32),
                                  hg_norm[layer]) @ w_b[layer]
        merged = jax.nn.sigmoid(gate_a) * y_a + jax.nn.sigmoid(gate_b) * y_b
        x = x + merged @ w_o[layer]
        h = rmsnorm(x, ffn_norm[layer])
        x = x + (jax.nn.silu(h @ w_gate[layer]) * (h @ w_up[layer])) @ w_down[layer]
    return rmsnorm(x, final_norm)


D_MIX = D_MODEL
HEAD_DIM = 64
D_SC = D_MIX // 4
D_ATT = D_MIX // 2
D_CC = D_MIX // 4
N_Q_HEADS = D_ATT // HEAD_DIM
N_KV_HEADS = 2
GQA_GROUP = N_Q_HEADS // N_KV_HEADS
SC_WIDTH = 3
CC_WIDTH = 31
WINDOW = 128
BLOCK = 128
ROPE_THETA_2 = 10000.0
D_FF = 2816
LN_EPS = 1e-5
ALPHA = (2.0 * DEPTH) ** 0.25
BETA = (8.0 * DEPTH) ** -0.25
IN_SIZES_2 = (D_SC, D_SC, D_SC, N_Q_HEADS * HEAD_DIM, N_KV_HEADS * HEAD_DIM, N_KV_HEADS * HEAD_DIM, D_CC, D_CC)
D_IN = sum(IN_SIZES_2)
IN_OFFSETS = tuple(int(v) for v in np.cumsum(IN_SIZES_2)[:-1])


def layer_norm(x, g, b):
    xf = x.astype(jnp.float32)
    mu = jnp.mean(xf, axis=-1, keepdims=True)
    var = jnp.mean(jnp.square(xf - mu), axis=-1, keepdims=True)
    y = (xf - mu) * lax.rsqrt(var + LN_EPS)
    return (y * g.astype(jnp.float32) + b.astype(jnp.float32)).astype(x.dtype)

def swiglu(x, w_gu, w_down):
    g, u = jnp.split(x @ w_gu, 2, axis=-1)
    return (jax.nn.silu(g) * u) @ w_down

def depthwise_conv(x, w):
    k = w.shape[0]
    pad = (k - 1) // 2
    return lax.conv_general_dilated(
        x, w[:, None, :].astype(x.dtype), window_strides=(1,), padding=[(pad, pad)],
        dimension_numbers=("NWC", "WIO", "NWC"), feature_group_count=x.shape[-1])

def rope(x, positions):
    half = HEAD_DIM // 2
    inv_freq = ROPE_THETA_2 ** (-jnp.arange(half, dtype=jnp.float32) / half)
    ang = positions.astype(jnp.float32)[:, None] * inv_freq[None, :]
    cos = jnp.cos(ang)[None, :, None, :]
    sin = jnp.sin(ang)[None, :, None, :]
    xf = x.astype(jnp.float32)
    x1, x2 = xf[..., :half], xf[..., half:]
    return jnp.concatenate([x1 * cos - x2 * sin, x2 * cos + x1 * sin], axis=-1).astype(x.dtype)

def banded_window_attention(q, k, v, sink):
    b, s = q.shape[0], q.shape[1]
    nb = s // BLOCK
    qb = q.reshape(b, nb, BLOCK, N_KV_HEADS, GQA_GROUP, HEAD_DIM)

    def band(t):
        tp = jnp.pad(t, ((0, 0), (BLOCK, BLOCK), (0, 0), (0, 0)))
        parts = [tp[:, o * BLOCK:o * BLOCK + s].reshape(b, nb, BLOCK, N_KV_HEADS, HEAD_DIM) for o in range(3)]
        return jnp.concatenate(parts, axis=2)

    kb, vb = band(k), band(v)
    scores = jnp.einsum("bnqkgd,bnskd->bnkgqs", qb, kb).astype(jnp.float32) * (HEAD_DIM ** -0.5)
    qpos = jnp.arange(s).reshape(nb, BLOCK)
    kpos = jnp.arange(nb)[:, None] * BLOCK - BLOCK + jnp.arange(3 * BLOCK)[None, :]
    valid = (jnp.abs(qpos[:, :, None] - kpos[:, None, :]) <= WINDOW) \
        & (kpos >= 0)[:, None, :] & (kpos < s)[:, None, :]
    scores = jnp.where(valid[None, :, None, None], scores, -1e30)
    sink_f = sink.astype(jnp.float32).reshape(N_KV_HEADS, GQA_GROUP)[None, None, :, :, None]
    m = jnp.maximum(jnp.max(scores, axis=-1), sink_f)
    p = jnp.exp(scores - m[..., None])
    denom = jnp.sum(p, axis=-1) + jnp.exp(sink_f - m)
    o = jnp.einsum("bnkgqs,bnskd->bnqkgd", p.astype(v.dtype), vb).astype(jnp.float32)
    o = o / jnp.transpose(denom, (0, 1, 4, 2, 3))[..., None]
    return o.reshape(b, s, D_ATT).astype(q.dtype)

def hybrid_mixer(x, w_in, sc_conv_w, attn_sink, cc_conv_w, cc_conv_b, cc_ln_g, cc_ln_b, w_out):
    b, s, _ = x.shape
    positions = jnp.arange(s)
    z = x @ w_in
    sc_b, sc_c, sc_h, q, k, v, cc_a, cc_gate = jnp.split(z, IN_OFFSETS, axis=-1)
    y_sc = sc_b * depthwise_conv(sc_c * sc_h, sc_conv_w)
    q = rope(q.reshape(b, s, N_Q_HEADS, HEAD_DIM), positions)
    k = rope(k.reshape(b, s, N_KV_HEADS, HEAD_DIM), positions)
    v = v.reshape(b, s, N_KV_HEADS, HEAD_DIM)
    y_att = banded_window_attention(q, k, v, attn_sink)
    u = cc_a * jax.nn.sigmoid(cc_gate)
    u = depthwise_conv(u, cc_conv_w) + cc_conv_b
    y_cc = jax.nn.silu(layer_norm(u, cc_ln_g, cc_ln_b))
    return jnp.concatenate([y_sc, y_att, y_cc], axis=-1) @ w_out

def second_inputs(seed: int = 0) -> dict:
    key = jax.random.key(seed)
    ks = jax.random.split(key, 24)
    f32 = jnp.float32

    def nrm(k, shape, scale):
        return jax.random.normal(k, shape, f32) * scale

    def gain(k, n):
        return 1.0 + 0.02 * jax.random.normal(k, (DEPTH, n), f32)

    return {
        "x": jax.random.normal(ks[0], (BATCH, SEQ, D_MODEL), f32),
        "ffn1_w_gu": nrm(ks[1], (DEPTH, D_MODEL, 2 * D_FF), D_MODEL ** -0.5),
        "ffn1_w_down": nrm(ks[2], (DEPTH, D_FF, D_MODEL), BETA * D_FF ** -0.5),
        "ln1_g": gain(ks[3], D_MODEL),
        "ln1_b": nrm(ks[4], (DEPTH, D_MODEL), 0.02),
        "w_in": nrm(ks[5], (DEPTH, D_MODEL, D_IN), D_MODEL ** -0.5),
        "sc_conv_w": nrm(ks[6], (DEPTH, SC_WIDTH, D_SC), SC_WIDTH ** -0.5),
        "attn_sink": nrm(ks[7], (DEPTH, N_Q_HEADS), 0.5),
        "cc_conv_w": nrm(ks[8], (DEPTH, CC_WIDTH, D_CC), CC_WIDTH ** -0.5),
        "cc_conv_b": nrm(ks[9], (DEPTH, D_CC), 0.02),
        "cc_ln_g": gain(ks[10], D_CC),
        "cc_ln_b": nrm(ks[11], (DEPTH, D_CC), 0.02),
        "w_out": nrm(ks[12], (DEPTH, D_MIX, D_MODEL), BETA * D_MIX ** -0.5),
        "ln2_g": gain(ks[13], D_MODEL),
        "ln2_b": nrm(ks[14], (DEPTH, D_MODEL), 0.02),
        "ffn2_w_gu": nrm(ks[15], (DEPTH, D_MODEL, 2 * D_FF), D_MODEL ** -0.5),
        "ffn2_w_down": nrm(ks[16], (DEPTH, D_FF, D_MODEL), BETA * D_FF ** -0.5),
        "ln3_g": gain(ks[17], D_MODEL),
        "ln3_b": nrm(ks[18], (DEPTH, D_MODEL), 0.02),
    }

def second_block(x, ffn1_w_gu, ffn1_w_down, ln1_g, ln1_b, w_in, sc_conv_w, attn_sink, cc_conv_w,
              cc_conv_b, cc_ln_g, cc_ln_b, w_out, ln2_g, ln2_b, ffn2_w_gu, ffn2_w_down, ln3_g, ln3_b):
    for l in range(DEPTH):
        x = layer_norm(ALPHA * x + 0.5 * swiglu(x, ffn1_w_gu[l], ffn1_w_down[l]), ln1_g[l], ln1_b[l])
        x = layer_norm(ALPHA * x + hybrid_mixer(x, w_in[l], sc_conv_w[l], attn_sink[l], cc_conv_w[l],
                                                 cc_conv_b[l], cc_ln_g[l], cc_ln_b[l], w_out[l]),
                       ln2_g[l], ln2_b[l])
        x = layer_norm(ALPHA * x + 0.5 * swiglu(x, ffn2_w_gu[l], ffn2_w_down[l]), ln3_g[l], ln3_b[l])
    return x


def setup_inputs(seed=0):
    out = dict(first_inputs(seed))
    for name, value in second_inputs(seed + 1).items():
        if name != "x":
            out[name + "_2"] = value
    return out


def reference(
    x, positions, w_in, da_lambda, da_norm, hg_lb_logits, hg_norm, w_a, w_b, w_o, attn_norm,
    ffn_norm, w_gate, w_up, w_down, final_norm, ffn1_w_gu_2, ffn1_w_down_2, ln1_g_2, ln1_b_2,
    w_in_2, sc_conv_w_2, attn_sink_2, cc_conv_w_2, cc_conv_b_2, cc_ln_g_2, cc_ln_b_2, w_out_2,
    ln2_g_2, ln2_b_2, ffn2_w_gu_2, ffn2_w_down_2, ln3_g_2, ln3_b_2,
):
    x = first_block(
        x, positions, w_in, da_lambda, da_norm, hg_lb_logits, hg_norm, w_a, w_b, w_o, attn_norm,
        ffn_norm, w_gate, w_up, w_down, final_norm,
    )
    return second_block(
        x, ffn1_w_gu_2, ffn1_w_down_2, ln1_g_2, ln1_b_2, w_in_2, sc_conv_w_2, attn_sink_2,
        cc_conv_w_2, cc_conv_b_2, cc_ln_g_2, cc_ln_b_2, w_out_2, ln2_g_2, ln2_b_2, ffn2_w_gu_2,
        ffn2_w_down_2, ln3_g_2, ln3_b_2,
    )


_drawn_inputs = setup_inputs


def setup_inputs(seed=0):
    import zlib

    import numpy as np

    out = dict(_drawn_inputs(seed))
    spreads = {}
    factors = {'da_norm': 4.342,
     'hg_norm': 6.102,
     'ffn_norm': 2.739,
     'attn_sink_2': 8.0,
     'cc_conv_b_2': 8.0,
     'cc_ln_g_2': 8.0,
     'cc_ln_b_2': 8.0}
    for name, (base, spread) in spreads.items():
        noise = np.random.default_rng([zlib.crc32(name.encode()), seed]).standard_normal(out[name].shape)
        drawn = base * np.exp(spread * noise) if base else spread * noise
        out[name] = __import__('jax').numpy.asarray(drawn.astype(out[name].dtype))
    for name, factor in factors.items():
        out[name] = (out[name] * factor).astype(out[name].dtype)
    return out
```

```python
import math
from contextlib import ExitStack
import numpy as np
import concourse.bass as bass
from concourse import mybir

FP = mybir.dt.float32
FR = mybir.dt.float32r
BF = mybir.dt.bfloat16
U8 = mybir.dt.uint8
I32 = mybir.dt.int32
ALU = mybir.AluOpType
ACT = mybir.ActivationFunctionType
AX = mybir.AxisListType

T = 512
DEPTH = 2
EPS_RMS = 1e-6
EPS_LN = 1e-5
ALPHA = (2.0 * DEPTH) ** 0.25
BIG = 1e30

PCOL = {}
_n = 0
for _name, _k in (("attn_norm", 16), ("ffn_norm", 16), ("final_norm", 8), ("da_norm", 8), ("hg_norm", 8),
                  ("lb", 16), ("ln1_g", 16), ("ln1_b", 16), ("ln2_g", 16), ("ln2_b", 16), ("ln3_g", 16),
                  ("ln3_b", 16), ("sc_w", 12), ("cc_w", 124), ("cc_b", 4), ("cc_g", 4), ("cc_lb", 4),
                  ("invf", 1)):
    PCOL[_name] = _n
    _n += _k
NPRM = _n

ACT_SET = {ACT.Exp: "natural_log_exp_and_others", ACT.Ln: "natural_log_exp_and_others",
           ACT.Sigmoid: "sigmoid_and_others", ACT.Silu: "silu_and_others", ACT.Sin: "silu_and_others"}


class Sem:
    def __init__(self, h):
        self.h = h
        self.n = 0


class Queue:

    def __init__(self, sem):
        self.sem = sem
        self.ops = []
        self.seen = {}

    def do(self, fn, *after, sig=True):
        waits = {}
        stack = list(after)
        while stack:
            a = stack.pop()
            if a is None:
                continue
            if isinstance(a, list):
                stack.extend(a)
                continue
            s, v = a
            if self.seen.get(s, 0) < v:
                self.seen[s] = v
                waits[s] = v
        self.ops.append((list(waits.items()), fn, self.sem if sig else None, 1))
        if sig:
            self.sem.n += 1
            return (self.sem, self.sem.n)
        return None

    def dma(self, out, in_, sem, *after):
        self.do(lambda e: e.dma_start(out, in_), *after, sig=False)
        w, fn, _, _ = self.ops[-1]
        self.ops[-1] = (w, fn, sem, 16)
        sem.n += 16
        return (sem, sem.n)

    def last(self):
        return (self.sem, self.sem.n)

    def emit(self, e):
        for waits, fn, sem, inc in self.ops:
            for s, v in waits:
                e.wait_ge(s.h, v)
            ins = fn(e)
            if sem is not None:
                ins.then_inc(sem.h, inc)


class Buf:
    def __init__(self, ap, free=None):
        self.ap = ap
        self.free = free if free is not None else []


class Ring:

    def __init__(self, bufs):
        self.q = list(bufs)

    def get(self):
        assert self.q, "ring is empty"
        return self.q.pop(0)

    def put(self, buf, *toks):
        buf.free = list(toks)
        self.q.append(buf)


class Acts:

    def __init__(self, hi, lo):
        self.hi, self.lo = hi, lo
        self.th = [None] * len(hi)
        self.tl = [None] * len(lo)


class Prog:
    pass


def build_program(nc, a, stop=None):
    ctx = ExitStack()
    with ctx:
        P = Prog()
        nsem = [0]

        def sem():
            nsem[0] += 1
            return Sem(ctx.enter_context(nc.semaphore(f"s{nsem[0]}")))

        PE, AC, DV, PO = Queue(sem()), Queue(sem()), Queue(sem()), Queue(sem())
        SP = Queue(sem())
        base = BASE
        names = [0]

        def at(off, cols, dt=FP, name=None):
            names[0] += 1
            t = nc.alloc_sbuf_tensor_at(f"{name or 'm'}_{names[0]}", [128, cols], dt, offset=base + off)
            return t

        KB = 1024
        off = [0]

        def take(nbytes):
            o = off[0]
            off[0] += (nbytes + 31) // 32 * 32
            assert off[0] <= LIMIT - base, (off[0], LIMIT - base)
            return o

        def here(cols, dt=FP, size=4, name=None):
            return at(take(cols * size), cols, dt, name)

        prm = here(NPRM, name="prm")
        ident = here(128, name="ident")
        ones = here(128, name="ones")
        permT = here(128, name="permT")
        perm2 = here(128, name="perm2")
        identb = here(128, BF, 2, name="identb")
        wmask = here(256, BF, 2, name="wmask")
        sink = here(16, name="sink")
        M_f = here(1024, FR, name="Mf")
        M_b = here(1024, FR, name="Mb")
        R = here(512, name="R")
        msk = here(7 * 128, U8, 1, name="msk")
        lbt = here(48, name="lbt")
        nlam = here(8, name="nlam")
        small = here(64, name="small")
        tabs = [here(512, name=f"tab{i}") for i in range(4)]
        C_t, S_t, RC, RS = tabs
        NR = 3
        raw = [here(1024, name="raw") for _ in range(NR)]
        whi = [here(1024, FR, name="whi") for _ in range(NR)]
        wlo = [here(1024, FR, name="wlo") for _ in range(NR)]
        X_off = take(16 * KB)
        X = [at(X_off + 2 * KB * k, 512, name="X") for k in range(8)]
        Hh = [here(512, FR, name="Hh") for _ in range(8)]
        Hl = [here(512, FR, name="Hl") for _ in range(8)]
        B0 = off[0]
        BIGSZ = LIMIT - base - B0
        P.bigsz = BIGSZ

        def big(kb, cols, dt=FP, size=4, name=None):
            o = int(kb * KB)
            assert o + cols * size <= BIGSZ, (name, kb, BIGSZ / KB)
            return at(B0 + o, cols, dt, name)

        ps = [ctx.enter_context(nc.psum_tensor(f"ps{i}", [128, 512], FP)) for i in range(8)]
        main = Ring([Buf(ps[i]) for i in range(3)])
        sideb = Ring([Buf(ps[i]) for i in range(3, 8)])

        def fence():
            return [PE.last(), AC.last(), DV.last(), PO.last()]

        cur_set = [None]

        def act(out, in_, func, *after, bias=0.0, scale=1.0, accum=None):
            want = ACT_SET.get(func)
            if want is not None and cur_set[0] != want:
                cur_set[0] = want
                AC.do(lambda e: e.preload_act_table_set(want), sig=False)
            if accum is None:
                return AC.do(lambda e: e.activation(out, in_, func, bias=bias, scale=scale), *after)
            return AC.do(lambda e: e.activation(out, in_, func, bias=bias, scale=scale, accum_out=accum), *after)

        def tt(out, x, y, op, *after, q=None):
            return (q or DV).do(lambda e: e.tensor_tensor(out, x, y, op), *after)

        def ts(out, x, s1, s2, o1, o2, *after, q=None):
            if s2 is None:
                return (q or DV).do(lambda e: e.tensor_scalar(out, x, s1, None, o1), *after)
            return (q or DV).do(lambda e: e.tensor_scalar(out, x, s1, s2, o1, o2), *after)

        def stt(out, x, s, y, o1, o2, *after):
            return DV.do(lambda e: e.scalar_tensor_tensor(out=out, in0=x, scalar=s, in1=y, op0=o1, op1=o2), *after)

        def mm(out, l, r, start, stop, *after, sig=False, skip=False):
            if skip:
                return PE.do(lambda e: e.matmul(out, l, r, start=start, stop=stop, skip_group_check=True), *after, sig=sig)
            return PE.do(lambda e: e.matmul(out, l, r, start=start, stop=stop), *after, sig=sig)

        def tr(out, x, *after, sig=False):
            return PE.do(lambda e: e.transpose(out, x, ident[:, :]), *after, sig=sig)

        def mm3(out, Lh, Ll, Rh, Rl, start, stop, th, tl, *after, sig=False):
            mm(out, Lh, Rh, start, False, th, *after)
            mm(out, Lh, Rl, False, False, tl)
            return mm(out, Ll, Rh, False, stop, sig=sig)

        V4 = lambda t: t[:, :].rearrange("p (j c) -> p j c", j=4)

        class State:
            pass
        NS = State()
        NS.R_ready = False

        chunks = []
        s_raw = [sem() for _ in range(NR)]
        raw_free = [[] for _ in range(NR)]
        raw_tok = {}
        hi_tok, lo_tok, done = {}, {}, {}

        def load(c):
            if c >= len(chunks):
                return
            w, n = chunks[c]
            s = c % NR
            raw_tok[c] = SP.dma(raw[s][:, 0:n], w, s_raw[s], raw_free[s])

        def prep(c):
            if c >= len(chunks):
                return
            w, n = chunks[c]
            s = c % NR
            hi_tok[c] = act(whi[s][:, 0:n], raw[s][:, 0:n], ACT.Copy, raw_tok[c], done.get(c - NR))
            lo_tok[c] = tt(wlo[s][:, 0:n], raw[s][:, 0:n], whi[s][:, 0:n].bitcast(FP), ALU.subtract,
                           raw_tok[c], hi_tok[c], done.get(c - NR))
            raw_free[s] = [hi_tok[c], lo_tok[c]]
            load(c + NR)

        side = []
        pend = []

        def evacs():
            while pend and NS.R_ready:
                pend.pop(0)()

        def tick():
            evacs()
            for g in list(side):
                try:
                    next(g)
                except StopIteration:
                    side.remove(g)
            evacs()

        def spawn(g):
            side.append(g)
            return g

        def settle():
            while side or pend:
                tick()

        def wait_for(g):
            n = 0
            while g in side:
                tick()
                n += 1
            return n

        jobs = []

        def job(chs, nb, evac, before=None):
            ids = []
            for w, n, segs in chs:
                ids.append(len(chunks))
                chunks.append((w, n))
            jobs.append((ids, [c[2] for c in chs], nb, evac, before))

        def run_jobs():
            for ids, segs, nb, evac, before in jobs:
                if before is not None:
                    before()
                banks = None
                for c, sg in zip(ids, segs):
                    prep(c + 2)
                    s = c % NR
                    half = (len(sg) + 1) // 2
                    for part in (sg[:half], sg[half:]):
                        tick()
                        if banks is None:
                            banks = [main.get() for _ in range(nb)]
                            bfree = [b.free for b in banks]
                        for i, (k, A, kt, b, st, sp) in enumerate(part):
                            out = banks[b].ap[:, :]
                            wh = whi[s][:, 128 * k:128 * k + 128]
                            wl = wlo[s][:, 128 * k:128 * k + 128]
                            free = bfree[b] if st else None
                            mm(out, wh, A.hi[kt], st, False, hi_tok[c], A.th[kt], free)
                            mm(out, wh, A.lo[kt], False, False, A.tl[kt])
                            done[c] = mm(out, wl, A.hi[kt], False, sp, lo_tok[c], sig=(i == len(part) - 1))
                tok = done[ids[-1]]
                if evac is not None:
                    pend.append(lambda f=evac, b=banks, t=tok: f(b, t))

        s_c, s_x, s_p = sem(), [sem() for _ in range(8)], sem()
        stage = big(0, 2048, name="stage")
        mst = big(20, 896, name="mst")
        posi = big(8, 512, I32, name="posi")
        lamv = big(10, 512, name="lamv")
        for o, i in ((prm, a["prm"]), (ident, a["cst"][:, 0:128]), (ones, a["cst"][:, 128:256]),
                     (permT, a["cst"][:, 256:384]), (perm2, a["cst"][:, 384:512]), (mst, a["msk"]), (stage, a["mcst"])):
            t_c = SP.dma(o[:, :], i, s_c)
        for k in range(8):
            SP.dma(X[k][:, :], a["xT"][:, 512 * k:512 * k + 512], s_x[k])
        xt = [(s_x[k], 16) for k in range(8)]
        t_p = SP.dma(posi[:, :], a["pos"].broadcast_to([128, 512]), s_p)
        t_p = SP.dma(lamv[:, :], a["lam"].broadcast_to([128, 512]), s_p)
        t_p = SP.dma(sink[:, :], a["sink"].broadcast_to([128, 16]), s_p)
        wst = big(18, 384, name="wst")
        t_w = SP.dma(wst[:, :], a["wmask"], s_p)
        t_wm = [act(wmask[:, :], wst[:, 0:256], ACT.Copy, t_w), act(identb[:, :], ident[:, :], ACT.Copy, t_c)]
        t_msk = DV.do(lambda e: e.tensor_copy(msk[:, :], mst[:, :]), t_c)
        t_M = [act(M_f[:, :], stage[:, 0:1024], ACT.Copy, t_c), act(M_b[:, :], stage[:, 1024:2048], ACT.Copy, t_c)]

        def col(name, i):
            return prm[:, PCOL[name] + i:PCOL[name] + i + 1]

        lbraw = prm[:, PCOL["lb"]:PCOL["lb"] + 16].rearrange("p (d l h) -> p d l h", d=2, l=2)
        sc8 = lambda i: lbt[:, 8 * i:8 * i + 8].rearrange("p (d h) -> p d h", d=2)
        la, lc, lca, w0, w1, w2 = [sc8(i) for i in range(6)]
        t = tt(w0, lbraw[:, :, 0, :], lbraw[:, :, 1, :], ALU.max, t_c)
        t0 = tt(w1, lbraw[:, :, 0, :], w0, ALU.subtract, t)
        t1 = tt(w2, lbraw[:, :, 1, :], w0, ALU.subtract, t0)
        t0 = act(w1, w1, ACT.Exp, t1)
        t1 = act(w2, w2, ACT.Exp, t1)
        t = tt(w0, w1, w2, ALU.add, t1)
        t = DV.do(lambda e: e.reciprocal(lbt[:, 24:32], lbt[:, 24:32]), t)
        t0 = tt(w1, w1, w0, ALU.mult, t)
        t1 = tt(w2, w2, w0, ALU.mult, t0)
        t = tt(w0, w1, w2, ALU.add, t1)
        t = tt(w0, w0, w1, ALU.subtract, t)
        t = ts(w1, w0, -1.0, 1.0, ALU.mult, ALU.add, t)
        for src, dst in ((w0, la), (w1, lc)):
            t = ts(w2, src, 1e-18, None, ALU.max, None, t)
            t = act(dst, w2, ACT.Ln, t)
            t = ts(w2, src, 0.0, -BIG, ALU.is_le, ALU.mult, t)
            t = tt(dst, dst, w2, ALU.add, t)
        t_lb = tt(lca, lc, la, ALU.subtract, t)
        lam4 = lamv[:, :].rearrange("p (l r e) -> p l r e", l=2, r=4)
        prod = big(12, 256, name="prod")
        pr4 = prod[:, :].rearrange("p (l r e) -> p l r e", l=2, r=2)
        tt(pr4[:, :, 0, :], lam4[:, :, 0, :], lam4[:, :, 1, :], ALU.mult, t_p)
        t = tt(pr4[:, :, 1, :], lam4[:, :, 2, :], lam4[:, :, 3, :], ALU.mult, t_p)
        t = DV.do(lambda e: e.tensor_reduce(small[:, 0:4], prod[:, :].rearrange("p (a e) -> p a e", a=4), AX.X, ALU.add), t)
        t = act(small[:, 0:4], small[:, 0:4], ACT.Exp, t)
        for l in range(2):
            li = 0.8 - 0.6 * math.exp(-0.3 * l)
            t0 = tt(nlam[:, l:l + 1], small[:, 2 * l + 1:2 * l + 2], small[:, 2 * l:2 * l + 1], ALU.subtract, t)
            t_lam = ts(nlam[:, l:l + 1], nlam[:, l:l + 1], -li, None, ALU.add, None, t0)
            c0 = PCOL["da_norm"] + 4 * l
            t_lam = ts(prm[:, c0:c0 + 4], prm[:, c0:c0 + 4], 1.0 - li, None, ALU.mult, None, t_lam, t_c)

        def tables():
            ang, n1, m1, m2 = [big(k, 512, name="rt") for k in (92, 94, 96, 98)]
            MAGIC = 12582912.0
            t = DV.do(lambda e: e.tensor_copy(ang[:, :], posi[:, :]), t_p)
            t = ts(ang[:, :], ang[:, :], col("invf", 0), None, ALU.mult, None, t, t_c)
            two_pi = 2.0 * math.pi
            c1 = 201.0 / 32.0
            r1 = two_pi - c1

            def top(v, bits):
                m, e = math.frexp(v)
                return math.ldexp(math.floor(m * 2 ** bits), e - bits)
            c2 = top(r1, 8)
            c3 = top(r1 - c2, 8)
            c4 = r1 - c2 - c3
            K = 65536.0
            d2 = top(r1 * K, 11)
            d3 = r1 * K - d2
            yield
            t = ts(n1[:, :], ang[:, :], 1.0 / (two_pi * K), MAGIC, ALU.mult, ALU.add, t)
            t = ts(n1[:, :], n1[:, :], MAGIC, None, ALU.subtract, None, t)
            for cc in (c1 * K, d2):
                t = stt(ang[:, :], n1[:, :], -cc, ang[:, :], ALU.mult, ALU.add, t)
            yield
            for rnd in range(2):
                t = ts(m1[:, :], ang[:, :], 1.0 / two_pi, MAGIC, ALU.mult, ALU.add, t)
                t = ts(m1[:, :], m1[:, :], MAGIC, None, ALU.subtract, None, t)
                for cc in (c1, c2, c3, c4):
                    t = stt(ang[:, :], m1[:, :], -cc, ang[:, :], ALU.mult, ALU.add, t)
                yield
                if rnd == 0:
                    t = stt(ang[:, :], n1[:, :], -d3, ang[:, :], ALU.mult, ALU.add, t)
            t = ts(ang[:, :], ang[:, :], 3.1415925, -3.1415925, ALU.min, ALU.max, t)
            t1 = act(S_t[:, :], ang[:, :], ACT.Sin, t)
            t2 = act(m1[:, :], ang[:, :], ACT.Sin, t, scale=0.5)
            t2 = act(m1[:, :], m1[:, :], ACT.Square, t2)
            yield
            t = ts(C_t[:, :], m1[:, :], -2.0, 1.0, ALU.mult, ALU.add, t2)
            P.t_tab = [t1, t]

        st_ring = Ring([Buf(small[:, 8 * i:8 * i + 8]) for i in range(1, 7)])

        def rstd(sq, t_sq, scale, eps, D, Dfree, out):
            b = sideb.get()
            for j in range(4):
                t = mm(b.ap[:, j:j + 1], sq[:, 128 * j:128 * j + 128], ones[:, 0:1], True, True, t_sq, t_c,
                       b.free, sig=(j == 3))
            s = st_ring.get()
            t = ts(s.ap[:, 0:4], b.ap[:, 0:4], scale, eps, ALU.mult, ALU.add, t, s.free)
            sideb.put(b, t)
            out["sq_done"] = t
            t = PO.do(lambda e: e.tensor_tensor(s.ap[:, 4:8], s.ap[:, 0:4], pm05[:, 0:4], ALU.pow), t, t_pm)
            yield
            t = tt(D[:, :].rearrange("p (j c) -> p j c", j=4), ident[:, None, :].broadcast_to([128, 4, 128]),
                   s.ap[:, 4:8][:, :, None].broadcast_to([128, 4, 128]), ALU.mult, t, t_c, Dfree)
            st_ring.put(s, t)
            yield
            b = sideb.get()
            t = mm(b.ap[:, :], ones[:, :], D[:, :], True, True, t, b.free, sig=True)
            out["D_done"] = t
            out["bank"], out["tok"] = b, t

        pm05 = nlam[:, 4:8]
        t_pm = PO.do(lambda e: e.memset(pm05, -0.5))


        slot = [[big(22 * s + 2 * i, 512, FR if i in (6, 7, 8, 9) else FP) for i in range(11)] for s in range(2)]
        E_t = [big(44, 2048), big(52, 2048)]
        E_free = [[], []]
        KQ = Ring([Buf((big(60 + 4 * i, 512), big(62 + 4 * i, 512))) for i in range(4)])
        AT = big(76, 2560)
        AT_free = [[]]
        tmps = [Buf(big(84 + 2 * i, 512)) for i in range(4)]
        TMP = Ring(tmps)
        nb_o, nb_sq, nb_D, nb_r = [big(92 + 2 * i, 512) for i in range(4)]
        g_off = [100, 102, 104, 106, 64, 66, 68, 70, 72, 74, 22, 24, 26, 28, 30, 32]
        gate = [big(o, 512) for o in g_off]
        gateR = [big(o, 512, FR) for o in g_off]
        oH = Acts([at(X_off + 2 * KB * h, 512, FR) for h in range(4)],
                  [at(X_off + 8 * KB + 2 * KB * h, 512, FR) for h in range(4)])
        oD = Acts([big(34 + 2 * h, 512, FR) for h in range(4)], [big(76 + 2 * h, 512, FR) for h in range(4)])
        daq = [big(2 * i, 512, FR) for i in range(6)]
        E4 = Ring([Buf(big(12 + 2 * i, 512)) for i in range(4)])
        WT = [big(44, 2048, FR), big(52, 2048, FR)]
        Wr = Ring([Buf(big(60 + 2 * i, 512)) for i in range(2)])
        hid = Acts([big(2 * i, 512, FR) for i in range(22)], [big(44 + 2 * i, 512, FR) for i in range(22)])
        FT = Ring([Buf(big(o, 512)) for o in (88, 90, 98, 100, 102, 104, 106)])
        H = Acts([t[:, :] for t in Hh], [t[:, :] for t in Hl])
        tv = lambda t: t[:, :]
        for A_ in (oH, oD, hid):
            A_.hi = [tv(t) for t in A_.hi]
            A_.lo = [tv(t) for t in A_.lo]

        def view(t, n, half):
            return t[:, :].rearrange("p (t b h e) -> p t b h e", t=4, h=2, e=n // 2)[:, :, :, half, :]

        def eview(t, j, n, half):
            return t[:, :].rearrange("p (t j b h e) -> p t j b h e", t=4, j=4, h=2, e=n // 2)[:, :, j, :, half, :]

        def prep_x(k, gname, gi, tok, hfree, sfree):
            H.th[k] = act(H.hi[k], X[k][:, :], ACT.Copy, tok, hfree, scale=col(gname, gi))
            if k == 0:
                NS.t = tt(nb_o[:, :], X[k][:, :], X[k][:, :], ALU.mult, tok, sfree, q=PO)
            else:
                t = tt(nb_sq[:, :], X[k][:, :], X[k][:, :], ALU.mult, tok, sfree, NS.t, q=PO)
                NS.t = tt(nb_o[:, :], nb_o[:, :], nb_sq[:, :], ALU.add, t, NS.t, q=PO)
            H.tl[k] = stt(H.lo[k], X[k][:, :], col(gname, gi), H.hi[k].bitcast(FP), ALU.mult, ALU.subtract,
                          H.th[k], hfree)

        def make_R(scale, eps):
            o = {}
            yield from rstd(nb_o, NS.t, scale, eps, nb_D, fence(), o)
            NS.tR = act(R[:, :], o["bank"].ap[:, :], ACT.Copy, o["tok"], fence())
            sideb.put(o["bank"], NS.tR)
            NS.R_ready = True

        class Head:
            pass

        def hg_gate(st, l, h, d, bank, tok):
            k_, g_, Gh, Gl = slot[st.s][d], slot[st.s][4 + d], slot[st.s][6 + 2 * d], slot[st.s][7 + 2 * d]
            z, w = TMP.get(), TMP.get()
            t = tt(z.ap[:, :], bank.ap[:, :], R[:, :], ALU.mult, tok, NS.tR, z.free, st.free)
            main.put(bank, t)
            t1 = act(w.ap[:, :], z.ap[:, :], ACT.Abs, t, w.free)
            t1 = act(w.ap[:, :], w.ap[:, :], ACT.Exp, t1, scale=-1.0)
            t1 = act(w.ap[:, :], w.ap[:, :], ACT.Ln, t1, bias=1.0)
            yield
            t2 = stt(g_[:, :], z.ap[:, :], 0.0, w.ap[:, :], ALU.min, ALU.subtract, t1)
            t3 = tt(z.ap[:, :], g_[:, :], z.ap[:, :], ALU.subtract, t2)
            if l == 0:
                tk = act(k_[:, :], z.ap[:, :], ACT.Exp, t3)
                tg = t2
            else:
                cc, aa, ca = (lbt[:, 8 * i + 4 * d + h:8 * i + 4 * d + h + 1] for i in (1, 0, 2))
                tk = act(k_[:, :], z.ap[:, :], ACT.Exp, t3, t_lb, bias=cc)
                t1 = act(w.ap[:, :], g_[:, :], ACT.Abs, t2, bias=ca)
                t1 = act(w.ap[:, :], w.ap[:, :], ACT.Exp, t1, scale=-1.0)
                t1 = act(w.ap[:, :], w.ap[:, :], ACT.Ln, t1, bias=1.0)
                yield
                t2 = ts(g_[:, :], g_[:, :], cc, aa, ALU.add, ALU.max, t1)
                tg = tt(g_[:, :], g_[:, :], w.ap[:, :], ALU.add, t2)
            TMP.put(z, tk)
            TMP.put(w, tg)
            yield
            b = sideb.get()
            for j in range(4):
                t = tr(b.ap[:, 128 * j:128 * j + 128], g_[:, 128 * j:128 * j + 128], tg, b.free, t_c, sig=(j == 3))
            t1 = act(Gh[:, :], b.ap[:, :], ACT.Copy, t, st.free)
            t2 = tt(Gl[:, :], b.ap[:, :], Gh[:, :].bitcast(FP), ALU.subtract, t1)
            sideb.put(b, t2)
            te = act(g_[:, :], g_[:, :], ACT.Exp, t)
            st.k[d], st.eg[d], st.G[d] = tk, te, [t1, t2]

        def hg_v(st, bank, tok):
            z = TMP.get()
            t = tt(z.ap[:, :], bank.ap[:, :], R[:, :], ALU.mult, tok, NS.tR, z.free)
            main.put(bank, t)
            yield
            b = sideb.get()
            for j in range(4):
                t1 = tr(b.ap[:, 128 * j:128 * j + 128], z.ap[:, 128 * j:128 * j + 128], t, b.free, t_c, sig=(j == 3))
            TMP.put(z, t1)
            st.v = act(slot[st.s][3][:, :], b.ap[:, :], ACT.Copy, t1, st.free_v)
            sideb.put(b, st.v)

        def hg_main(st, l, h, prev):
            sl = slot[st.s]
            kf, kb, q, V, egf, egb = sl[:6]
            bg = sl[10]
            while not st.ready or any(g in side for g in st.gens):
                yield
            if prev is not None:
                while not prev.passed_E:
                    yield

            def exps(d, grp):
                G, M, E = (sl[6 + 2 * d], sl[7 + 2 * d]), (M_f, M_b)[d], E_t[d]
                for j in range(4):
                    b = sideb.get()
                    for i in range(2):
                        t = mm(b.ap[:, :], G[i][:, 128 * j:128 * j + 128], M[:, 512 * grp:512 * grp + 512],
                               i == 0, i == 1, st.G[d], t_M, b.free, sig=(i == 1))
                    st.E[d] = act(E[:, 512 * j:512 * j + 512], b.ap[:, :], ACT.Exp, t, E_free[d])
                    sideb.put(b, st.E[d])

            def half(K, Q, j, n, d, free):
                E = E_t[d]
                kk = (kf, kb)[d]
                kh, qh = (0, 1) if d == 0 else (1, 0)
                t1 = tt(view(K, n, kh), view(kk, n, kh), eview(E, j, n, kh), ALU.mult, st.k[d], st.E[d], free)
                t2 = tt(view(Q, n, qh), view(q, n, qh), eview(E, j, n, qh), ALU.mult, st.q, st.E[d], free)
                E_free[d] = [t2]
                return [t1, t2]

            def pair(j, n):
                b = KQ.get()
                K, Q = b.ap
                b.t = [half(K, Q, j, n, d, b.free) for d in range(2)]
                return b

            ATd = AT[:, :].rearrange("p (i c) -> p i c", c=640)[:, :, 0:128]

            def scores(kq, K, Q, lev):
                b = sideb.get()
                for j in range(4):
                    s_ = slice(128 * j, 128 * j + 128)
                    t = mm(b.ap[:, s_], K[:, s_], Q[:, s_], True, True, kq.t, b.free, sig=(j == 3))
                KQ.put(kq, t)
                if lev == 0:
                    st.at = act(ATd, V4(b.ap), ACT.Copy, t, AT_free[0])
                else:
                    m_ = msk[:, 128 * (lev - 1):128 * lev]
                    st.at = DV.do(lambda e: e.copy_predicated(ATd, m_[:, None, :].broadcast_to([128, 4, 128]),
                                                              V4(b.ap)), t, st.at, t_msk)
                sideb.put(b, st.at)

            def offs(d):
                b = KQ.get()
                K, Q = b.ap
                E = E_t[d]
                kk = (kf, kb)[d]
                E5 = E[:, :].rearrange("p (t j c) -> p t j c", t=4, j=4)
                k4, q4, K4, Q4 = V4(kk), V4(q), V4(K), V4(Q)
                k_e = E5[:, :, 2, :]
                q_e = E5[:, :, 3, :]
                tot = lambda j: q_e[:, j, 127:128] if d == 0 else q_e[:, j, 0:1]
                w = [st.k[d], st.q, st.E[d], b.free]
                pr = lambda ap, o: ap.rearrange("p (a b) c -> p a b c", b=2)[:, :, o, :]
                if d == 0:
                    t = tt(K4[:, 0:3, :], k4[:, 0:3, :], k_e[:, 0:3, :], ALU.mult, w)
                    t1 = ts(K4[:, 3, :], K4[:, 0, :], tot(1), None, ALU.mult, None, t)
                    tt(Q4[:, 0:2, :], pr(q4, 1), pr(q_e, 1), ALU.mult, w)
                    t = tt(Q4[:, 2, :], q4[:, 2, :], q_e[:, 2, :], ALU.mult, w)
                    t2 = ts(Q4[:, 3, :], Q4[:, 1, :], tot(2), None, ALU.mult, None, t)
                else:
                    t = tt(K4[:, 0:3, :], k4[:, 1:4, :], k_e[:, 1:4, :], ALU.mult, w)
                    t1 = ts(K4[:, 3, :], K4[:, 2, :], tot(2), None, ALU.mult, None, t)
                    tt(Q4[:, 2:4, :], pr(q4, 0), pr(q_e, 0), ALU.mult, w)
                    t = tt(Q4[:, 1, :], q4[:, 1, :], q_e[:, 1, :], ALU.mult, w)
                    t2 = ts(Q4[:, 0, :], Q4[:, 2, :], tot(1), None, ALU.mult, None, t)
                E_free[d] = [t2]
                b.t = [t1, t2]
                return b

            def off_scores(kq, d):
                K, Q = kq.ap
                ba, bb = sideb.get(), sideb.get()
                c = lambda t_, i, n=1: t_[:, 128 * i:128 * (i + n)]
                w = [kq.t, ba.free, bb.free]
                if d == 0:
                    mm(c(ba.ap, 0), c(K, 0), c(Q, 0), True, True, w)
                    t = mm(c(ba.ap, 1, 2), c(K, 3), c(Q, 2, 2), True, True, sig=True)
                    mm(c(bb.ap, 0, 2), c(K, 1), c(Q, 2, 2), True, True)
                    t2 = mm(c(bb.ap, 2), c(K, 2), c(Q, 1), True, True, sig=True)
                    act(c(AT, 1, 3), c(ba.ap, 0, 3), ACT.Copy, t, AT_free[0])
                    sideb.put(ba, AC.last())
                    act(c(AT, 6, 2), c(bb.ap, 0, 2), ACT.Copy, t2, AT_free[0])
                    st.off[d] = act(c(AT, 11), c(bb.ap, 2), ACT.Copy, t2)
                else:
                    mm(c(ba.ap, 0, 2), c(K, 3), c(Q, 0, 2), True, True, w)
                    t = mm(c(ba.ap, 2), c(K, 2), c(Q, 3), True, True, sig=True)
                    mm(c(bb.ap, 0, 2), c(K, 1), c(Q, 0, 2), True, True)
                    t2 = mm(c(bb.ap, 2), c(K, 0), c(Q, 2), True, True, sig=True)
                    act(c(AT, 12, 3), c(ba.ap, 0, 3), ACT.Copy, t, AT_free[0])
                    sideb.put(ba, AC.last())
                    act(c(AT, 8, 2), c(bb.ap, 0, 2), ACT.Copy, t2, AT_free[0])
                    st.off[d] = act(c(AT, 4), c(bb.ap, 2), ACT.Copy, t2)
                KQ.put(kq, t2)
                sideb.put(bb, st.off[d])

            exps(0, 0)
            yield
            exps(1, 0)
            l128 = KQ.get()
            l128.t = [half(l128.ap[0], l128.ap[1], 0, 128, 0, l128.free)]
            of = offs(0)
            yield
            off_scores(of, 0)
            l128.t.append(half(l128.ap[0], l128.ap[1], 0, 128, 1, l128.free))
            ob = offs(1)
            yield
            scores(l128, l128.ap[0], l128.ap[1], 0)
            off_scores(ob, 1)
            l64 = pair(1, 64)
            yield
            scores(l64, l64.ap[0], l64.ap[1], 1)
            exps(0, 1)
            yield
            exps(1, 1)
            dg = KQ.get()
            dg.t = [tt(dg.ap[0][:, :], kf[:, :], kb[:, :], ALU.add, st.k, dg.free), st.q]
            l2 = KQ.get()
            K, Q = l2.ap
            l2.t = [DV.do(lambda e: e.tensor_copy(view(K, 2, 0), view(kf, 2, 0)), st.k, l2.free),
                    DV.do(lambda e: e.tensor_copy(view(K, 2, 1), view(kb, 2, 1)), st.k, l2.free),
                    tt(view(Q, 2, 1), view(q, 2, 1), view(egf, 2, 1), ALU.mult, st.q, st.eg, l2.free),
                    tt(view(Q, 2, 0), view(q, 2, 0), view(egb, 2, 0), ALU.mult, st.q, st.eg, l2.free)]
            l32 = KQ.get()
            l32.t = [half(l32.ap[0], l32.ap[1], 0, 32, 0, l32.free)]
            yield
            scores(dg, dg.ap[0], q, 7)
            scores(l2, l2.ap[0], l2.ap[1], 6)
            l32.t.append(half(l32.ap[0], l32.ap[1], 0, 32, 1, l32.free))
            l16 = pair(1, 16)
            yield
            scores(l32, l32.ap[0], l32.ap[1], 2)
            scores(l16, l16.ap[0], l16.ap[1], 3)
            l8 = pair(2, 8)
            l4 = pair(3, 4)
            st.passed_E = True
            yield
            scores(l8, l8.ap[0], l8.ap[1], 4)
            scores(l4, l4.ap[0], l4.ap[1], 5)
            st.last_a = fence()
            yield
            b = sideb.get()
            for i in range(4):
                t = mm(b.ap[:, :], V[:, 128 * i:128 * i + 128], AT[:, 512 * i:512 * i + 512], i == 0, i == 3,
                       st.at, st.off, st.v, b.free, sig=(i == 3))
            AT_free[0] = [t]
            st.last_v = [t]
            yield from norm_out(b, t, col("hg_norm", 4 * l + h), (bg, st.bg), oH, h, oH_free)
            st.last = fence()

        def norm_out(b, t, gcol, extra, O, h, ofree):
            to = act(nb_o[:, :], b.ap[:, :], ACT.Copy, t, NS.nfree)
            sideb.put(b, to)
            tq = act(nb_sq[:, :], nb_o[:, :], ACT.Square, to)
            yield
            o = {}
            yield from rstd(nb_sq, tq, 1.0 / 128.0, EPS_RMS, nb_D, NS.nfree, o)
            t = stt(nb_r[:, :], nb_o[:, :], gcol, o["bank"].ap[:, :], ALU.mult, ALU.mult, o["tok"], t_lam)
            sideb.put(o["bank"], t)
            if extra is not None:
                t = tt(nb_r[:, :], nb_r[:, :], extra[0][:, :], ALU.mult, t, extra[1])
            O.th[h] = act(O.hi[h], nb_r[:, :], ACT.Copy, t, ofree)
            yield
            O.tl[h] = tt(O.lo[h], nb_r[:, :], O.hi[h].bitcast(FP), ALU.subtract, O.th[h])
            NS.nfree = [O.tl[h]]

        def da_rope(st, which, bank, tok):
            z, w = TMP.get(), TMP.get()
            t = act(z.ap[:, :], bank.ap[:, :], ACT.Copy, tok, z.free)
            main.put(bank, t)
            yield
            b = sideb.get()
            t1 = mm(b.ap[:, :], permT[:, :], z.ap[:, :], True, True, t, b.free, t_c, sig=True)
            t2 = tt(w.ap[:, :], b.ap[:, :], RS[:, :], ALU.mult, t1, NS.tRC, w.free)
            sideb.put(b, t2)
            t3 = tt(z.ap[:, :], z.ap[:, :], RC[:, :], ALU.mult, t1)
            t4 = tt(z.ap[:, :], z.ap[:, :], w.ap[:, :], ALU.add, t3, t2)
            TMP.put(w, t4)
            th = act(daq[2 * which][:, :], z.ap[:, :], ACT.Copy, t4, st.free)
            yield
            tl = tt(daq[2 * which + 1][:, :], z.ap[:, :], daq[2 * which][:, :].bitcast(FP), ALU.subtract, th, st.free)
            TMP.put(z, tl)
            st.qk[which] = [th, tl]

        def da_v(st, bank, tok):
            z = TMP.get()
            t = tt(z.ap[:, :], bank.ap[:, :], R[:, :], ALU.mult, tok, NS.tR, z.free)
            main.put(bank, t)
            yield
            b = sideb.get()
            for j in range(4):
                t1 = tr(b.ap[:, 128 * j:128 * j + 128], z.ap[:, 128 * j:128 * j + 128], t, b.free, sig=(j == 3))
            TMP.put(z, t1)
            th = act(daq[4][:, :], b.ap[:, :], ACT.Copy, t1, st.free)
            tl = tt(daq[5][:, :], b.ap[:, :], daq[4][:, :].bitcast(FP), ALU.subtract, th)
            sideb.put(b, tl)
            st.v = [th, tl]

        def da_block(st, l, qt, WT_t):
            es, sm = [], st_ring.get()
            mx, ng, su, r_ = (sm.ap[:, 2 * i:2 * i + 2] for i in range(4))
            qs = slice(128 * qt, 128 * qt + 128)
            bs = []
            for c in range(2):
                p = slice(64 * c, 64 * c + 64)
                b = sideb.get()
                t = mm3(b.ap[:, :], daq[0][p, qs], daq[1][p, qs], daq[2][p, :], daq[3][p, :], True, True,
                        [st.qk[0], st.qk[1]], None, b.free, sig=True)
                bs.append((b, t))
            for c, (b, t) in enumerate(bs):
                tm = DV.do(lambda e, b=b, c=c: e.tensor_reduce(mx[:, c:c + 1], b.ap[:, :], AX.X, ALU.max), t, sm.free)
            tn = ts(ng, mx, -0.125, None, ALU.mult, None, tm)
            for c, (b, t) in enumerate(bs):
                e_ = E4.get()
                te = act(e_.ap[:, :], b.ap[:, :], ACT.Exp, tn, e_.free, bias=ng[:, c:c + 1], scale=0.125,
                         accum=su[:, c:c + 1])
                sideb.put(b, te)
                es.append(e_)
            yield
            t = DV.do(lambda e: e.reciprocal(r_, su), te)
            t = tt(r_[:, 1:2], r_[:, 1:2], nlam[:, l:l + 1], ALU.mult, t, t_lam)
            w = Wr.get()
            t1 = ts(w.ap[:, :], es[0].ap[:, :], r_[:, 0:1], None, ALU.mult, None, t, w.free)
            t2 = stt(w.ap[:, :], es[1].ap[:, :], r_[:, 1:2], w.ap[:, :], ALU.mult, ALU.add, t1)
            st_ring.put(sm, t2)
            E4.put(es[0], t2)
            E4.put(es[1], t2)
            yield
            b = sideb.get()
            for j in range(4):
                t = tr(b.ap[:, 128 * j:128 * j + 128], w.ap[:, 128 * j:128 * j + 128], t2, b.free, sig=(j == 3))
            Wr.put(w, t)
            dst = [V4(W_)[:, :, qs] for W_ in WT]
            th = act(dst[0], V4(b.ap), ACT.Copy, t, st.wfree)
            tl = tt(dst[1], V4(b.ap), dst[0].bitcast(FP), ALU.subtract, th, st.wfree)
            sideb.put(b, tl)
            WT_t += [th, tl]

        def da_main(st, l, h, prev):
            while not st.ready or any(g in side for g in st.gens):
                yield
            while prev is not None and prev.busy:
                yield
            WT_t = []
            subs = []
            for qt in range(4):
                subs.append(spawn(da_block(st, l, qt, WT_t)))
                yield
            st.scored = True
            while any(g in side for g in subs):
                yield
            b = sideb.get()
            for j in range(4):
                s_ = slice(128 * j, 128 * j + 128)
                t = mm3(b.ap[:, :], daq[4][:, s_], daq[5][:, s_], WT[0][:, 512 * j:512 * j + 512],
                        WT[1][:, 512 * j:512 * j + 512], j == 0, j == 3, [WT_t, st.v], None, b.free, sig=(j == 3))
            st.pv = t
            st.busy = False
            yield from norm_out(b, t, col("da_norm", 4 * l + h), None, oD, h, oD_free)

        oH_free, oD_free = [], []

        s_re = [sem() for _ in range(8)]
        s_sp = sem()
        scr = a["scr"]
        xtok = list(xt)

        def w1(name, l, n):
            return a[name][l, n]

        def in_job(l, n, evac, before=None):
            job([(a["win1"][l, n], 1024, [(k, H, k, 0, k == 0, k == 7) for k in range(8)])], 1, evac, before)

        def first_block(l):
            hs = [Head() for _ in range(4)]
            ds = [Head() for _ in range(4)]

            def start_layer():
                NS.nfree = []
                if l == 0:
                    for k in range(8):
                        H.th[k] = act(H.hi[k], X[k][:, :], ACT.Copy, xtok[k], t_c, scale=col("attn_norm", k))
                        H.tl[k] = stt(H.lo[k], X[k][:, :], col("attn_norm", k), H.hi[k].bitcast(FP),
                                      ALU.mult, ALU.subtract, H.th[k])
                    ta = tb = None
                    for k in range(4):
                        if k == 0:
                            ta = tt(nb_o[:, :], X[0][:, :], X[0][:, :], ALU.mult, xtok[0], q=PO)
                            tb = tt(nb_r[:, :], X[4][:, :], X[4][:, :], ALU.mult, xtok[4])
                        else:
                            t1 = tt(nb_sq[:, :], X[k][:, :], X[k][:, :], ALU.mult, xtok[k], ta, q=PO)
                            ta = tt(nb_o[:, :], nb_o[:, :], nb_sq[:, :], ALU.add, t1, q=PO)
                            t1 = tt(nb_D[:, :], X[4 + k][:, :], X[4 + k][:, :], ALU.mult, xtok[4 + k], tb)
                            tb = tt(nb_r[:, :], nb_r[:, :], nb_D[:, :], ALU.add, t1)
                    NS.t = tt(nb_o[:, :], nb_o[:, :], nb_r[:, :], ALU.add, ta, tb)
                    NS.xread = fence()

                for d in range(2):
                    E_free[d] = fence()
                AT_free[0] = fence()
                for b_ in KQ.q + TMP.q:
                    b_.free = fence()
                oH_free[:] = [NS.xread if l == 0 else [NS.spill, fence()]]

                def g():
                    if l == 0:
                        NS.R_ready = False
                        yield from make_R(1.0 / 1024.0, EPS_RMS)
                        yield from tables()
                    while not NS.R_ready:
                        yield
                    NS.nfree = [fence()]
                    t1 = tt(RC[:, :], C_t[:, :], R[:, :], ALU.mult, NS.tR, P.t_tab, fence(), q=PO)
                    t2 = tt(RS[:, :], S_t[:, :], R[:, :], ALU.mult, NS.tR, P.t_tab, q=PO)
                    NS.tRC = [t1, t2]
                spawn(g())

            for h in range(4):
                st = hs[h]
                st.s = h % 2
                st.k, st.eg, st.G, st.E, st.off = [None] * 2, [None] * 2, [None] * 2, [None] * 2, [None] * 2
                st.gens, st.ready, st.passed_E, st.last = [], False, False, None

                def bef(h=h, st=st):
                    if h == 0:
                        start_layer()
                    if h < 2:
                        st.free = st.free_v = st.free_g = fence()

                def ev_gate(b, t, h=h, st=st, d=0):
                    if h >= 2:
                        st.free = hs[h - 2].last_a
                    st.gens.append(spawn(hg_gate(st, l, h, d, b[0], t)))

                def ev_v(b, t, h=h, st=st):
                    if h >= 2:
                        st.free_v = hs[h - 2].last_v
                    st.gens.append(spawn(hg_v(st, b[0], t)))

                def ev_q(b, t, h=h, st=st):
                    st.q = tt(slot[st.s][2][:, :], b[0].ap[:, :], R[:, :], ALU.mult, t, NS.tR, st.free)
                    main.put(b[0], st.q)
                    st.ready = True
                    spawn(hg_main(st, l, h, hs[h - 1] if h else None))

                def ev_g(b, t, h=h, st=st):
                    if h >= 2:
                        st.free_g = hs[h - 2].last
                        assert st.free_g is not None
                    t1 = tt(slot[st.s][10][:, :], b[0].ap[:, :], R[:, :], ALU.mult, t, NS.tR, st.free_g)
                    main.put(b[0], t1)
                    st.bg = act(slot[st.s][10][:, :], slot[st.s][10][:, :], ACT.Sigmoid, t1)

                in_job(l, 16 + h, lambda b, t, f=ev_gate: f(b, t, d=0), bef)
                in_job(l, 20 + h, lambda b, t, f=ev_gate: f(b, t, d=1))
                in_job(l, 24 + h, ev_v)
                in_job(l, 12 + h, ev_q)
                in_job(l, 28 + h, ev_g)

            def gates(i0, n):
                for i in range(i0, i0 + n):
                    def ev(b, t, i=i, i0=i0, n=n):
                        fr = fence()
                        if i >= 4:
                            assert hs[2].last is not None
                        if i >= 10:
                            assert hs[3].last is not None
                        t1 = tt(gate[i][:, :], b[0].ap[:, :], R[:, :], ALU.mult, t, NS.tR, fr)
                        main.put(b[0], t1)
                        gt[i] = t1
                        if i == i0 + n - 1:
                            def sg():
                                yield
                                for m in range(i0, i0 + n):
                                    gt[m] = act(gate[m][:, :], gate[m][:, :], ACT.Sigmoid, gt[m])
                            spawn(sg())
                    in_job(l, (32 if i % 2 == 0 else 40) + i // 2, ev)

            gt = [None] * 16

            def da(h):
                st = ds[h]
                st.qk, st.gens, st.ready, st.busy, st.scored = [None, None], [], False, True, False

                def ev(b, t, w=0):
                    if w == 0:
                        if h == 0:
                            assert hs[2].last is not None
                            st.free = fence()
                        else:
                            assert ds[h - 1].scored, "q and k of the head before still in use"
                            st.free = fence()
                    if w == 2:
                        if h:
                            assert not ds[h - 1].busy
                        st.free = fence()
                        st.gens.append(spawn(da_v(st, b[0], t)))
                        st.ready = True
                        if h == 0:
                            st.wfree = None
                        else:
                            st.wfree = [ds[h - 1].pv]

                        def start():
                            if h == 0:
                                while hs[3].last is None:
                                    yield
                                st.wfree = fence()
                                oD_free[:] = st.wfree
                                for b_ in E4.q + Wr.q:
                                    b_.free = st.wfree
                            yield from da_main(st, l, h, ds[h - 1] if h else None)
                        st.main = spawn(start())
                    else:
                        st.gens.append(spawn(da_rope(st, w, b[0], t)))
                for w in range(3):
                    in_job(l, 4 * w + h, lambda b, t, w=w, ev=ev: ev(b, t, w))

            gates(0, 4)
            da(0)
            gates(4, 2)
            da(1)
            gates(6, 2)
            da(2)
            gates(8, 2)
            da(3)
            gates(10, 3)
            gates(13, 3)

            mg = Acts([g[:, :] for g in gateR[0::2]], [g[:, :] for g in gateR[1::2]])
            for n in range(8):
                def ev(b, t, n=n):
                    def g():
                        x_, y_ = TMP.get(), TMP.get()
                        t1 = tt(x_.ap[:, :], b[0].ap[:, :], gate[2 * n][:, :], ALU.mult, t, gt[2 * n], x_.free)
                        main.put(b[0], t1)
                        t2 = tt(y_.ap[:, :], b[1].ap[:, :], gate[2 * n + 1][:, :], ALU.mult, t, gt[2 * n + 1], y_.free)
                        main.put(b[1], t2)
                        t1 = tt(x_.ap[:, :], x_.ap[:, :], y_.ap[:, :], ALU.add, t1, t2)
                        TMP.put(y_, t1)
                        mg.th[n] = act(mg.hi[n], x_.ap[:, :], ACT.Copy, t1)
                        yield
                        mg.tl[n] = tt(mg.lo[n], x_.ap[:, :], mg.hi[n].bitcast(FP), ALU.subtract, mg.th[n])
                        TMP.put(x_, mg.tl[n])
                    spawn(g())

                def bef(n=n):
                    if n == 0:
                        while side:
                            tick()
                job([(a["wab"][l, n], 1024,
                      [(4 + k, oH, k, 1, k == 0, k == 3) for k in range(4)]
                      + [(k, oD, k, 0, k == 0, k == 3) for k in range(4)])], 2, ev, bef)

            src = a["xT"] if l == 0 else scr
            for n in range(8):
                def bef(n=n):
                    if n == 0:
                        tick()
                        tick()
                        for k in range(8):
                            xtok[k] = SP.dma(X[k][:, :], src[:, 512 * k:512 * k + 512], s_re[k], PE.last(),
                                             NS.spill if l else NS.xread)
                        NS.hfree = PE.last()
                        NS.sfree = fence()

                def ev(b, t, n=n):
                    xtok[n] = tt(X[n][:, :], X[n][:, :], b[0].ap[:, :], ALU.add, t, xtok[n])
                    main.put(b[0], xtok[n])
                    prep_x(n, "ffn_norm", 8 * l + n, xtok[n], NS.hfree, NS.sfree)
                    if n == 7:
                        NS.R_ready = False
                        spawn(make_R(1.0 / 1024.0, EPS_RMS))
                job([(a["wo"][l, n], 1024, [(k, mg, k, 0, k == 0, k == 7) for k in range(8)])], 1, ev, bef)

        def ffn(gu, dn, acc, useR, before=None):
            for n in range(22):
                stt_ = {}

                def ev_G(b, t, s=stt_, n=n):
                    x_ = FT.get()
                    if useR:
                        t1 = tt(x_.ap[:, :], b[0].ap[:, :], R[:, :], ALU.mult, t, NS.tR, x_.free)
                        main.put(b[0], t1)
                        s["t"] = act(x_.ap[:, :], x_.ap[:, :], ACT.Silu, t1)
                    else:
                        s["t"] = act(x_.ap[:, :], b[0].ap[:, :], ACT.Silu, t, x_.free)
                        main.put(b[0], s["t"])
                    s["g"] = x_

                def ev_U(b, t, s=stt_, n=n):
                    def g():
                        y_ = FT.get()
                        x_ = s["g"]
                        if useR:
                            t1 = tt(y_.ap[:, :], b[0].ap[:, :], R[:, :], ALU.mult, t, NS.tR, y_.free)
                            main.put(b[0], t1)
                            t1 = tt(y_.ap[:, :], y_.ap[:, :], x_.ap[:, :], ALU.mult, t1, s["t"])
                        else:
                            t1 = tt(y_.ap[:, :], b[0].ap[:, :], x_.ap[:, :], ALU.mult, t, s["t"], y_.free)
                            main.put(b[0], t1)
                        FT.put(x_, t1)
                        hid.th[n] = act(hid.hi[n], y_.ap[:, :], ACT.Copy, t1, NS.hidfree)
                        yield
                        hid.tl[n] = tt(hid.lo[n], y_.ap[:, :], hid.hi[n].bitcast(FP), ALU.subtract, hid.th[n])
                        FT.put(y_, hid.tl[n])
                    spawn(g())

                def bef(n=n):
                    if n == 0:
                        if before is not None:
                            before()
                        NS.hidfree = fence()
                        for b_ in FT.q:
                            b_.free = fence()
                job([(gu(n, 0), 1024, [(k, H, k, 0, k == 0, k == 7) for k in range(8)])], 1, ev_G, bef)
                job([(gu(n, 1), 1024, [(k, H, k, 0, k == 0, k == 7) for k in range(8)])], 1, ev_U)
            for n in range(8):
                w = dn(n)
                chs = []
                for c0, kn in ((0, 8), (8, 8), (16, 6)):
                    chs.append((w[:, 128 * c0:128 * (c0 + kn)], 128 * kn,
                                [(k, hid, c0 + k, 0, c0 + k == 0, c0 + k == 21) for k in range(kn)]))

                def bef(n=n):
                    if n == 0:
                        NS.hfree = PE.last()
                        NS.sfree = fence()
                job(chs, 1, lambda b, t, n=n: acc(n, b[0], t), bef)

        def ffn_a(l):
            def acc(n, b, t):
                xtok[n] = tt(X[n][:, :], X[n][:, :], b.ap[:, :], ALU.add, t, xtok[n])
                main.put(b, xtok[n])
                if l == 0:
                    prep_x(n, "attn_norm", 8 * (l + 1) + n, xtok[n], NS.hfree, NS.sfree)
                    NS.spill = SP.dma(scr[:, 512 * n:512 * n + 512], X[n][:, :], s_sp, xtok[n])
                else:
                    prep_x(n, "final_norm", n, xtok[n], NS.hfree, NS.sfree)
                if n == 7:
                    NS.R_ready = False
                    spawn(make_R(1.0 / 1024.0, EPS_RMS))
            ffn(lambda n, u: a["wgu1"][l, 2 * n + u], lambda n: a["wd1"][l, n], acc, True)

        L_m0, L_s1, L_s2, L_sq, L_DR, L_DC, L_C = [big(92 + 2 * i, 512) for i in range(7)]
        LN = State()

        def ln_acc(n, b, t, scale):
            t = stt(X[n][:, :], X[n][:, :], scale, b.ap[:, :], ALU.mult, ALU.add, t, xtok[n])
            main.put(b, t)
            if n == 0:
                s_ = sideb.get()
                t1 = mm(s_.ap[:, :], ones[:, :], X[0][:, :], True, True, t, s_.free, sig=True)
                LN.m0 = act(L_m0[:, :], s_.ap[:, :], ACT.Copy, t1, NS.sfree, scale=1.0 / 128.0)
                sideb.put(s_, LN.m0)
            t = tt(X[n][:, :], X[n][:, :], L_m0[:, :], ALU.subtract, t, LN.m0)
            xtok[n] = t
            if n == 0:
                LN.s1 = PO.do(lambda e: e.tensor_copy(L_s1[:, :], X[0][:, :]), t, NS.sfree)
                LN.s2 = act(L_s2[:, :], X[0][:, :], ACT.Square, t, NS.sfree)
            else:
                LN.s1 = tt(L_s1[:, :], L_s1[:, :], X[n][:, :], ALU.add, t, LN.s1, q=PO)
                t1 = act(L_sq[:, :], X[n][:, :], ACT.Square, t, LN.s2, NS.sfree)
                LN.s2 = tt(L_s2[:, :], L_s2[:, :], L_sq[:, :], ALU.add, t1, LN.s2, q=PO)

        def ln_finish(gn, bn, l, eps, final):
            b = sideb.get()
            for i, (S_, ts_) in enumerate(((L_s1, LN.s1), (L_s2, LN.s2))):
                for j in range(4):
                    t = mm(b.ap[:, 4 * i + j:4 * i + j + 1], S_[:, 128 * j:128 * j + 128], ones[:, 0:1], True, True,
                           ts_, b.free, sig=(i == 1 and j == 3))
            sa, sb_ = st_ring.get(), st_ring.get()
            md, v, r_, c_ = sa.ap[:, 0:4], sa.ap[:, 4:8], sb_.ap[:, 0:4], sb_.ap[:, 4:8]
            t1 = ts(md, b.ap[:, 0:4], 1.0 / 1024.0, None, ALU.mult, None, t, sa.free)
            t2 = ts(v, b.ap[:, 4:8], 1.0 / 1024.0, eps, ALU.mult, ALU.add, t)
            sideb.put(b, t2)
            t1 = tt(c_, md, md, ALU.mult, t1, sb_.free)
            t2 = tt(v, v, c_, ALU.subtract, t1, t2)
            t = PO.do(lambda e: e.tensor_tensor(r_, v, pm05[:, 0:4], ALU.pow), t2, t_pm)
            yield
            t = stt(c_, md, -1.0, r_, ALU.mult, ALU.mult, t)
            br, bc = sideb.get(), sideb.get()
            tb = []
            for D_, s_, bb in ((L_DR, r_, br), (L_DC, c_, bc)):
                t1 = tt(D_[:, :].rearrange("p (j c) -> p j c", j=4), ident[:, None, :].broadcast_to([128, 4, 128]),
                        s_[:, :, None].broadcast_to([128, 4, 128]), ALU.mult, t, NS.sfree)
                tb.append(mm(bb.ap[:, :], ones[:, :], D_[:, :], True, True, t1, bb.free, sig=True))
            st_ring.put(sa, t1)
            st_ring.put(sb_, t1)
            tc = act(L_C[:, :], bc.ap[:, :], ACT.Copy, tb[1])
            sideb.put(bc, tc)
            for k in range(8):
                t = tt(X[k][:, :], X[k][:, :], br.ap[:, :], ALU.mult, tb[0], xtok[k], LN.s1, LN.s2)
                if k == 7:
                    sideb.put(br, t)
                t = tt(X[k][:, :], X[k][:, :], L_C[:, :], ALU.add, t, tc, q=PO if k % 2 else DV)
                t = act(X[k][:, :], X[k][:, :], ACT.Identity, t, scale=col(gn, 8 * l + k), bias=col(bn, 8 * l + k))
                xtok[k] = t
                if not final:
                    H.th[k] = act(H.hi[k], X[k][:, :], ACT.Copy, t, NS.hfree)
            yield
            if not final:
                for k in range(8):
                    H.tl[k] = tt(H.lo[k], X[k][:, :], H.hi[k].bitcast(FP), ALU.subtract, H.th[k], NS.hfree)

        def ln_wait():
            tick()
            wait_for(LN.gen)

        def ffn_b(l, which):
            gu, dn = a[f"wgu{which + 1}"], a[f"wd{which + 1}"]
            nm = "ln1" if which == 1 else "ln3"
            first = which == 1 and l == 0

            def acc(n, b, t):
                ln_acc(n, b, t, 2.0 * ALPHA)
                if n == 7:
                    LN.gen = spawn(ln_finish(nm + "_g", nm + "_b", l, 4.0 * EPS_LN, which == 2 and l == 1))

            def before():
                if not first:
                    ln_wait()
                    return

                def g():
                    while not NS.R_ready:
                        yield
                    for k in range(8):
                        xtok[k] = stt(X[k][:, :], X[k][:, :], col("final_norm", k), R[:, :], ALU.mult, ALU.mult,
                                      xtok[k], NS.tR, H.th[k], H.tl[k])
                        yield
                spawn(g())
            ffn(lambda n, u: gu[l, 2 * n + u], lambda n: dn[l, n], acc, first, before)

        MX = Acts([big(2 * i, 512, FR)[:, :] for i in range(8)], [big(16 + 2 * i, 512, FR)[:, :] for i in range(8)])
        q2 = [[big(32 + 4 * i + 2 * j, 512, FR) for j in range(2)] for i in range(4)]
        k2 = [big(48 + 2 * j, 512, FR) for j in range(2)]
        v2 = [big(52 + 2 * j, 512) for j in range(2)]
        e2 = Ring([Buf(big(56 + 1.5 * i, 384)) for i in range(4)])
        w2 = Ring([Buf(big(62 + 1.5 * i, 384)) for i in range(4)])
        p2 = Ring([Buf((big(68 + 3 * i, 384), big(69.5 + 3 * i, 384))) for i in range(2)])
        up = [big(74 + 2.25 * i, 542) for i in range(4)]
        cacc = [big(83 + 2 * i, 512) for i in range(2)]
        cpo = [big(87 + 2 * i, 512) for i in range(2)]
        cpr = Ring([Buf(big(91 + 2 * i, 512)) for i in range(2)])
        TM2 = Ring([Buf(big(95 + 2 * i, 512)) for i in range(4)])
        c_sq, c_D, c_mu = big(103, 512), big(105, 512), RC
        C2, S2 = C_t, S_t
        s_tb = sem()

        def mixer_b(l):
            M = State()

            def before():
                ln_wait()
                f = fence()
                M.f = f
                for r_ in (e2, w2, p2, cpr, TM2):
                    for b_ in r_.q:
                        b_.free = f
                tz = []
                for u in up[0:2]:
                    tz += [PO.do(lambda e, u=u: e.memset(u[:, 0:15], 0.0), f), PO.do(lambda e, u=u: e.memset(u[:, 527:542], 0.0), f)]
                for u in up[2:4]:
                    tz += [PO.do(lambda e, u=u: e.memset(u[:, 0:1], 0.0), f), PO.do(lambda e, u=u: e.memset(u[:, 513:514], 0.0), f)]
                for i in range(2):
                    tz.append(PO.do(lambda e, i=i: e.memset(v2[i][:, :], 0.0), f))
                M.tz = tz[-1]
                if l == 0:
                    SP.dma(C2[:, :], a["tab2"][:, 0:512], s_tb, f)
                    M.ttab = SP.dma(S2[:, :], a["tab2"][:, 512:1024], s_tb, f)
                    NS.ttab = M.ttab

            def rope2(b, tok, dst, out):
                z, w = TM2.get(), TM2.get()
                t = act(z.ap[:, :], b.ap[:, :], ACT.Copy, tok, z.free)
                main.put(b, t)
                yield
                s_ = sideb.get()
                t1 = mm(s_.ap[:, :], perm2[:, :], z.ap[:, :], True, True, t, s_.free, t_c, sig=True)
                t2 = tt(w.ap[:, :], s_.ap[:, :], S2[:, :], ALU.mult, t1, NS.ttab, w.free)
                sideb.put(s_, t2)
                t3 = tt(z.ap[:, :], z.ap[:, :], C2[:, :], ALU.mult, t1)
                t4 = tt(z.ap[:, :], z.ap[:, :], w.ap[:, :], ALU.add, t3, t2)
                TM2.put(w, t4)
                th = act(dst[0][:, :], z.ap[:, :], ACT.Copy, t4, M.f)
                yield
                tl = tt(dst[1][:, :], z.ap[:, :], dst[0][:, :].bitcast(FP), ALU.subtract, th)
                TM2.put(z, tl)
                out[:] = [th, tl]

            def ev_k(b, t):
                M.k = []
                spawn(rope2(b[0], t, k2, M.k))

            def ev_v(b, t):
                def g():
                    z = TM2.get()
                    t1 = act(z.ap[:, :], b[0].ap[:, :], ACT.Copy, t, z.free)
                    main.put(b[0], t1)
                    yield
                    s_ = sideb.get()
                    for j in range(4):
                        t2 = tr(s_.ap[:, 128 * j:128 * j + 128], z.ap[:, 128 * j:128 * j + 128], t1, s_.free, sig=(j == 3))
                    TM2.put(z, t2)
                    hv = lambda x_, i: x_[:, :].rearrange("p (j h c) -> p j h c", j=4, h=2)[:, :, i, :]
                    M.v = [act(hv(v2[0], 0), hv(s_.ap, 0), ACT.Copy, t2, M.tz)]
                    M.v.append(act(hv(v2[1], 1), hv(s_.ap, 1), ACT.Copy, t2, M.tz))
                    sideb.put(s_, M.v[1])
                spawn(g())

            M.q = [[] for _ in range(4)]
            M.units = [[] for _ in range(4)]

            def unit(p, qt):
                k0, k1 = max(qt - 1, 0), min(qt + 2, 4)
                nk = 128 * (k1 - k0)
                sm = st_ring.get()
                mx, ng, su, r_ = (sm.ap[:, 2 * i:2 * i + 2] for i in range(4))
                qs = slice(128 * qt, 128 * qt + 128)
                ks = slice(128 * k0, 128 * k1)
                sk = sink[:, 8 * l:8 * l + 8].rearrange("p (c i) -> p c i", c=2)[:, :, p]
                bs, es = [], []
                for c in range(2):
                    pr_ = slice(64 * c, 64 * c + 64)
                    b = sideb.get()
                    o_ = b.ap[:, 0:nk]
                    mm(o_, q2[p][0][pr_, qs], k2[0][pr_, ks], True, False, M.q[p], M.k, b.free)
                    mm(o_, q2[p][0][pr_, qs], k2[1][pr_, ks], False, False)
                    if qt > 0:
                        mm(b.ap[:, 0:128], identb[:, :], wmask[:, 0:128], False, False, t_wm)
                    if qt < 3:
                        mm(b.ap[:, nk - 128:nk], identb[:, :], wmask[:, 128:256], False, False, t_wm)
                    t = mm(o_, q2[p][1][pr_, qs], k2[0][pr_, ks], False, True, sig=True)
                    bs.append((b, t))
                for c, (b, t) in enumerate(bs):
                    tm = DV.do(lambda e, b=b, c=c: e.tensor_reduce(mx[:, c:c + 1], b.ap[:, 0:nk], AX.X, ALU.max), t, sm.free)
                t = ts(mx, mx, 0.125, None, ALU.mult, None, tm)
                t = tt(mx, mx, sk, ALU.max, t, t_p)
                tn = ts(ng, mx, -1.0, None, ALU.mult, None, t)
                for c, (b, t) in enumerate(bs):
                    e_ = e2.get()
                    te = act(e_.ap[:, 0:nk], b.ap[:, 0:nk], ACT.Exp, tn, e_.free, bias=ng[:, c:c + 1], scale=0.125,
                             accum=su[:, c:c + 1])
                    sideb.put(b, te)
                    es.append(e_)
                t = tt(mx, sk, mx, ALU.subtract, tn)
                te = act(mx, mx, ACT.Exp, t)
                yield
                t = tt(su, su, mx, ALU.add, te)
                t = DV.do(lambda e: e.reciprocal(r_, su), t)
                ws = []
                for c in range(2):
                    w_ = w2.get()
                    tw = ts(w_.ap[:, 0:nk], es[c].ap[:, 0:nk], r_[:, c:c + 1], None, ALU.mult, None, t, w_.free)
                    e2.put(es[c], tw)
                    ws.append((w_, tw))
                st_ring.put(sm, tw)
                yield
                pt = p2.get()
                tp = []
                for c in range(2):
                    b = sideb.get()
                    for j in range(k1 - k0):
                        s_ = slice(128 * j, 128 * j + 128)
                        t = tr(b.ap[:, s_], ws[c][0].ap[:, s_], ws[c][1], b.free, sig=(j == k1 - k0 - 1))
                    w2.put(ws[c][0], t)
                    if c == 0:
                        t = act(pt.ap[c][:, 0:nk], b.ap[:, 0:nk], ACT.Copy, t, pt.free)
                    else:
                        t = DV.do(lambda e, b=b: e.tensor_copy(pt.ap[1][:, 0:nk], b.ap[:, 0:nk]), t, pt.free)
                    sideb.put(b, t)
                    tp.append(t)
                yield
                b = sideb.get()
                n_ = 0
                for c in range(2):
                    for j in range(k1 - k0):
                        t = mm(b.ap[:, 0:128], v2[c][:, 128 * (k0 + j):128 * (k0 + j) + 128],
                               pt.ap[c][:, 128 * j:128 * j + 128], n_ == 0, n_ == 2 * (k1 - k0) - 1, tp, M.v, b.free,
                               sig=(n_ == 2 * (k1 - k0) - 1))
                        n_ += 1
                p2.put(pt, t)
                th = act(MX.hi[2 + p][:, qs], b.ap[:, 0:128], ACT.Copy, t, M.f)
                tl = tt(MX.lo[2 + p][:, qs], b.ap[:, 0:128], MX.hi[2 + p][:, qs].bitcast(FP), ALU.subtract, th, M.f)
                sideb.put(b, tl)
                if MX.th[2 + p] is None:
                    MX.th[2 + p], MX.tl[2 + p] = [], []
                MX.th[2 + p].append(th)
                MX.tl[2 + p].append(tl)

            def units():
                for p in range(4):
                    while not M.q[p] or M.v is None:
                        yield
                    for qt in range(4):
                        spawn(unit(p, qt))
                        yield
                        yield
            M.v = None
            for k in range(8):
                MX.th[k] = MX.tl[k] = None

            def ev_q(b, t, p):
                spawn(rope2(b[0], t, q2[p], M.q[p]))
                if p == 0:
                    spawn(units())

            def ev_sig(b, t, i):
                z = TM2.get()
                M.sg[i] = (z, act(z.ap[:, :], b[0].ap[:, :], ACT.Sigmoid, t, z.free))
                main.put(b[0], M.sg[i][1])

            def ev_a(b, t, i):
                z, tz = M.sg[i]
                t1 = tt(up[i][:, 15:527], b[0].ap[:, :], z.ap[:, :], ALU.mult, t, tz, M.tz)
                main.put(b[0], t1)
                TM2.put(z, t1)
                spawn(conv(i, t1))
            M.sg = [None] * 2
            M.cv = [None] * 2

            NPO = 12

            def conv(i, tu):
                cw = lambda k: col("cc_w", 62 * l + 2 * k + i)
                ta = ts(cacc[i][:, :], up[i][:, NPO:NPO + 512], cw(NPO), col("cc_b", 2 * l + i), ALU.mult, ALU.add, tu, M.f)
                tp = None
                kp = 0
                for k in range(NPO + 1, 31):
                    ta = stt(cacc[i][:, :], up[i][:, k:k + 512], cw(k), cacc[i][:, :], ALU.mult, ALU.add, ta)
                    if kp < NPO:
                        if kp == 0:
                            tp = act(cpo[i][:, :], up[i][:, 0:512], ACT.Copy, tu, M.f, scale=cw(0))
                        else:
                            z = cpr.get()
                            t = act(z.ap[:, :], up[i][:, kp:kp + 512], ACT.Copy, tu, z.free, scale=cw(kp))
                            tp = tt(cpo[i][:, :], cpo[i][:, :], z.ap[:, :], ALU.add, t, tp, q=PO)
                            cpr.put(z, tp)
                        kp += 1
                    if k % 2 == 0:
                        yield
                ta = tt(cacc[i][:, :], cacc[i][:, :], cpo[i][:, :], ALU.add, ta, tp)
                M.cv[i] = ta
                if M.cv[1 - i] is not None:
                    yield
                    yield from cc_norm()

            def cc_norm():
                b = sideb.get()
                for i in range(2):
                    t = mm(b.ap[:, :], ones[:, :], cacc[i][:, :], i == 0, i == 1, M.cv[i], b.free, sig=(i == 1))
                t = act(c_mu[:, :], b.ap[:, :], ACT.Copy, t, M.f, scale=1.0 / 256.0)
                sideb.put(b, t)
                td = [tt(cacc[i][:, :], cacc[i][:, :], c_mu[:, :], ALU.subtract, t) for i in range(2)]
                t0 = act(c_sq[:, :], cacc[0][:, :], ACT.Square, td[0], M.f)
                z = TM2.get()
                t1 = act(z.ap[:, :], cacc[1][:, :], ACT.Square, td[1], z.free)
                tq = tt(c_sq[:, :], c_sq[:, :], z.ap[:, :], ALU.add, t0, t1)
                TM2.put(z, tq)
                yield
                o = {}
                yield from rstd(c_sq, tq, 1.0 / 256.0, EPS_LN, c_D, M.f, o)
                for i in range(2):
                    td[i] = tt(cacc[i][:, :], cacc[i][:, :], o["bank"].ap[:, :], ALU.mult, o["tok"], td[i])
                sideb.put(o["bank"], td[1])
                for i in range(2):
                    td[i] = act(cacc[i][:, :], cacc[i][:, :], ACT.Silu, td[i], scale=col("cc_g", 2 * l + i),
                                bias=col("cc_lb", 2 * l + i))
                    MX.th[6 + i] = act(MX.hi[6 + i], cacc[i][:, :], ACT.Copy, td[i], M.f)
                yield
                for i in range(2):
                    MX.tl[6 + i] = tt(MX.lo[6 + i], cacc[i][:, :], MX.hi[6 + i].bitcast(FP), ALU.subtract, MX.th[6 + i], M.f)

            M.sc = [None] * 2

            def ev_c(b, t, i):
                z = TM2.get()
                M.sc[i] = (z, act(z.ap[:, :], b[0].ap[:, :], ACT.Copy, t, z.free))
                main.put(b[0], M.sc[i][1])

            def ev_h(b, t, i):
                z, tz = M.sc[i]
                t1 = tt(up[2 + i][:, 1:513], b[0].ap[:, :], z.ap[:, :], ALU.mult, t, tz, M.tz)
                main.put(b[0], t1)
                cw = lambda k: col("sc_w", 6 * l + 2 * k + i)
                t2 = ts(z.ap[:, :], up[2 + i][:, 0:512], cw(0), None, ALU.mult, None, t1)
                for k in (1, 2):
                    t2 = stt(z.ap[:, :], up[2 + i][:, k:k + 512], cw(k), z.ap[:, :], ALU.mult, ALU.add, t2)
                M.sc[i] = (z, t2)

            def ev_b(b, t, i):
                def g():
                    z, tz = M.sc[i]
                    t1 = tt(z.ap[:, :], b[0].ap[:, :], z.ap[:, :], ALU.mult, t, tz)
                    main.put(b[0], t1)
                    MX.th[i] = act(MX.hi[i], z.ap[:, :], ACT.Copy, t1, M.f)
                    yield
                    MX.tl[i] = tt(MX.lo[i], z.ap[:, :], MX.hi[i].bitcast(FP), ALU.subtract, MX.th[i], M.f)
                    TM2.put(z, MX.tl[i])
                spawn(g())

            evs = [(10, ev_k), (11, ev_v)]
            evs += [(6, lambda b, t: ev_q(b, t, 0))]
            evs += [(14 + i, lambda b, t, i=i: ev_sig(b, t, i)) if j == 0 else (12 + i, lambda b, t, i=i: ev_a(b, t, i))
                    for i in range(2) for j in range(2)]
            evs += [(6 + i, lambda b, t, i=i: ev_q(b, t, i)) for i in range(1, 4)]
            for i in range(2):
                evs += [(2 + i, lambda b, t, i=i: ev_c(b, t, i)), (4 + i, lambda b, t, i=i: ev_h(b, t, i)),
                        (i, lambda b, t, i=i: ev_b(b, t, i))]
            for n, (tile, ev) in enumerate(evs):
                job([(a["win2"][l, tile], 1024, [(k, H, k, 0, k == 0, k == 7) for k in range(8)])], 1, ev,
                    before if n == 0 else None)
            order = [0, 1, 6, 7, 2, 3, 4, 5]
            for n in range(8):
                def bef(n=n):
                    if n == 0:
                        while side or pend:
                            tick()
                        NS.hfree = PE.last()
                        NS.sfree = fence()

                def ev(b, t, n=n):
                    ln_acc(n, b[0], t, ALPHA)
                    if n == 7:
                        LN.gen = spawn(ln_finish("ln2_g", "ln2_b", l, EPS_LN, False))
                job([(a["wout2"][l, n], 1024, [(k, MX, k, 0, k == order[0], k == order[-1]) for k in order])], 1, ev, bef)

        stages = [("mix0", lambda: first_block(0)), ("ffn0", lambda: ffn_a(0)), ("mix1", lambda: first_block(1)),
                  ("ffn1", lambda: ffn_a(1)),
                  ("b0ln1", lambda: ffn_b(0, 1)), ("b0ln2", lambda: mixer_b(0)), ("b0ln3", lambda: ffn_b(0, 2)),
                  ("b1ln1", lambda: ffn_b(1, 1)), ("b1ln2", lambda: mixer_b(1)), ("b1ln3", lambda: ffn_b(1, 2))]
        for name, f in stages:
            f()
            if name == stop:
                break
        for i in range(NR):
            load(i)
        prep(0)
        prep(1)
        run_jobs()
        settle()
        s_o = sem()
        for k in range(8):
            t_o = SP.dma(a["out"][:, 512 * k:512 * k + 512], X[k][:, :], s_o, xtok[k])

        block = ctx.enter_context(nc.Block())

        @block.sync
        def _(e):
            SP.emit(e)
            e.wait_ge(t_o[0].h, t_o[1])

        @block.scalar
        def _(e):
            AC.emit(e)

        @block.vector
        def _(e):
            DV.emit(e)

        @block.gpsimd
        def _(e):
            PO.emit(e)

        @block.tensor
        def _(e):
            PE.emit(e)
    return P


SCRATCH = 8192
BASE = (SCRATCH + 97 + 31) // 32 * 32
LIMIT = 229344


def host(inputs):
    f = lambda n: np.asarray(inputs[n])
    col = lambda v: np.ascontiguousarray(v.reshape(-1, 128).T)
    parts = [f("attn_norm"), f("ffn_norm"), f("final_norm"), f("da_norm"), f("hg_norm"), f("hg_lb_logits"),
             f("ln1_g_2"), f("ln1_b_2"), f("ln2_g_2"), f("ln2_b_2"), f("ln3_g_2"), f("ln3_b_2"),
             f("sc_conv_w_2"), f("cc_conv_w_2"), f("cc_conv_b_2"), f("cc_ln_g_2"), f("cc_ln_b_2")]
    cols = [col(p) for p in parts]
    invf = (500000.0 ** (-(np.arange(0, 16, 2, dtype=np.float32) / np.float32(16)))).astype(np.float32)
    iv = np.zeros((128, 1), np.float32)
    for c in range(2):
        for j in range(16):
            iv[64 * c + j, 0] = invf[j % 8]
    prm = np.concatenate(cols + [iv], axis=1)
    assert prm.shape[1] == NPRM, (prm.shape, NPRM)
    perm = np.zeros((128, 128), np.float32)
    for c in range(2):
        for j in range(8):
            perm[64 * c + j, 64 * c + j + 8] = -1.0
            perm[64 * c + j + 8, 64 * c + j] = 1.0
    perm2 = np.zeros((128, 128), np.float32)
    for c in range(2):
        for j in range(32):
            perm2[64 * c + j, 64 * c + j + 32] = -1.0
            perm2[64 * c + j + 32, 64 * c + j] = 1.0
    cst = np.concatenate([np.eye(128, dtype=np.float32), np.ones((128, 128), np.float32), perm.T, perm2.T], axis=1)
    j = np.arange(128)[:, None]
    t = np.arange(128)[None, :]

    def lev(n, fwd):
        b0 = (t // n) * n
        mid = b0 + n // 2 - 1
        left = t <= mid
        if fwd:
            m = np.where(left, (j > t) & (j <= mid), (j > mid) & (j <= t))
        else:
            m = np.where(left, (j >= t) & (j <= mid), (j > mid) & (j < t))
        return m.astype(np.float32)
    Mf = [lev(128, 1), lev(64, 1), (j > t), (j <= t)] + [lev(n, 1) for n in (32, 16, 8, 4)]
    Mb = [lev(128, 0), lev(64, 0), (j < t), (j >= t)] + [lev(n, 0) for n in (32, 16, 8, 4)]
    mcst = np.concatenate([np.asarray(m, np.float32) for m in Mf + Mb], axis=1)
    ms = []
    for n in (64, 32, 16, 8, 4, 2):
        ms.append((j // n == t // n) & ((j % n < n // 2) != (t % n < n // 2)))
    ms.append(j == t)
    msk = np.concatenate(ms, axis=1).astype(np.float32)
    c8 = lambda w: np.ascontiguousarray(w.reshape(2, 8, 128, -1, 128).transpose(0, 3, 2, 1, 4)).reshape(2, -1, 128, 1024)
    c4 = lambda w: w.reshape(2, 4, 128, 8, 128).transpose(0, 3, 2, 1, 4)
    gu = lambda g, u: np.ascontiguousarray(np.stack([c8(g), c8(u)], axis=2)).reshape(2, 44, 128, 1024)
    dn = lambda w: np.ascontiguousarray(w.reshape(2, 22, 128, 8, 128).transpose(0, 3, 2, 1, 4)).reshape(2, 8, 128, 2816)
    hq = np.concatenate([np.concatenate([np.arange(64 * i, 64 * i + 64), np.arange(64 * (i + 4), 64 * (i + 4) + 64)])
                         for i in range(4)])
    cols_ = np.arange(2048)
    cols_[768:1280] = 768 + hq
    rows_ = np.arange(1024)
    rows_[256:768] = 256 + hq
    win2 = f("w_in_2")[:, :, cols_]
    wout2 = f("w_out_2")[:, rows_, :]
    inv2 = (10000.0 ** (-np.arange(32, dtype=np.float32) / np.float32(32))).astype(np.float32)
    ang = np.arange(512, dtype=np.float32)[None, :] * inv2[np.arange(128) % 32][:, None]
    tab2 = np.concatenate([np.cos(ang.astype(np.float64)), np.sin(ang.astype(np.float64))], axis=1).astype(np.float32)
    wm = np.concatenate([np.where(t < j, -1e30, 0.0), np.where(t > j, -1e30, 0.0), np.zeros((128, 128))],
                        axis=1).astype(np.float32)
    gu2 = lambda w: gu(w[:, :, :2816], w[:, :, 2816:])
    x = f("x")[0]
    arr = {
        "xT": np.ascontiguousarray(x.T.reshape(8, 128, 512).transpose(1, 0, 2)).reshape(128, 4096),
        "pos": np.ascontiguousarray(f("positions")).astype(np.int32, copy=False),
        "prm": np.ascontiguousarray(prm),
        "lam": np.ascontiguousarray(f("da_lambda").reshape(1, 512)),
        "cst": np.ascontiguousarray(cst), "mcst": np.ascontiguousarray(mcst), "msk": np.ascontiguousarray(msk),
        "win1": c8(f("w_in")),
        "wab": np.ascontiguousarray(np.concatenate([c4(f("w_a")), c4(f("w_b"))], axis=3)).reshape(2, 8, 128, 1024),
        "wo": c8(f("w_o")), "wgu1": gu(f("w_gate"), f("w_up")), "wd1": dn(f("w_down")),
        "sink": np.ascontiguousarray(f("attn_sink_2").reshape(1, 16)), "wmask": wm, "tab2": tab2,
        "wgu2": gu2(f("ffn1_w_gu_2")), "wd2": dn(f("ffn1_w_down_2")),
        "wgu3": gu2(f("ffn2_w_gu_2")), "wd3": dn(f("ffn2_w_down_2")),
        "win2": c8(win2), "wout2": c8(wout2),
    }
    return arr


def kernel(**inputs):
    import concourse.bacc as bacc
    from concourse.bass_utils import run_bass_kernel_spmd as run
    nc = bacc.Bacc("TRN2", target_bir_lowering=False, num_devices=1, dynamic_dma_scratch_size=SCRATCH)
    arr = host(inputs)
    aps = {n: nc.dram_tensor(n, v.shape, mybir.dt.from_np(v.dtype), kind="ExternalInput").ap() for n, v in arr.items()}
    aps["out"] = nc.dram_tensor("out", (128, 4096), FP, kind="ExternalOutput").ap()
    aps["scr"] = nc.dram_tensor("scr", (128, 4096), FP).ap()
    build_program(nc, aps)
    r = run(nc, [arr], core_ids=[0])
    o = r.results[0]["out"]
    return np.ascontiguousarray(o.reshape(128, 8, 512).transpose(1, 0, 2).reshape(1024, 512).T).reshape(1, 512, 1024)
```

```python
import math
from contextlib import ExitStack
import numpy as np
import concourse.bass as bass
from concourse import mybir

FP = mybir.dt.float32
FR = mybir.dt.float32r
BF = mybir.dt.bfloat16
U8 = mybir.dt.uint8
I32 = mybir.dt.int32
ALU = mybir.AluOpType
ACT = mybir.ActivationFunctionType
AX = mybir.AxisListType

T = 512
DEPTH = 2
EPS_RMS = 1e-6
EPS_LN = 1e-5
ALPHA = (2.0 * DEPTH) ** 0.25
BIG = 1e30

PCOL = {}
_n = 0
for _name, _k in (("attn_norm", 16), ("ffn_norm", 16), ("final_norm", 8), ("da_norm", 8), ("hg_norm", 8),
                  ("lb", 16), ("ln1_g", 16), ("ln1_b", 16), ("ln2_g", 16), ("ln2_b", 16), ("ln3_g", 16),
                  ("ln3_b", 16), ("sc_w", 12), ("cc_w", 124), ("cc_b", 4), ("cc_g", 4), ("cc_lb", 4),
                  ("invf", 1)):
    PCOL[_name] = _n
    _n += _k
NPRM = _n

ACT_SET = {ACT.Exp: "natural_log_exp_and_others", ACT.Ln: "natural_log_exp_and_others",
           ACT.Sigmoid: "sigmoid_and_others", ACT.Silu: "silu_and_others", ACT.Sin: "silu_and_others"}


class Sem:
    def __init__(self, h):
        self.h = h
        self.n = 0
        self.t = {0: 0.0}


def flat(after):
    out, stack = [], list(after)
    while stack:
        a = stack.pop()
        if a is None:
            continue
        if isinstance(a, list):
            stack.extend(a)
        else:
            out.append(a)
    return out


def when(after):
    return max([s.t[v] for s, v in flat([after])], default=0.0)


class Queue:

    def __init__(self, sem, lat=60.0):
        self.sem = sem
        self.ops = []
        self.seen = {}
        self.clock = 0.0
        self.lat = lat

    def do(self, fn, *after, sig=True, cost=70.0):
        waits = {}
        for s, v in flat(after):
            self.clock = max(self.clock, s.t[v])
            if self.seen.get(s, 0) < v:
                self.seen[s] = v
                waits[s] = v
        self.clock += cost
        self.ops.append((list(waits.items()), fn, self.sem if sig else None, 1))
        if sig:
            self.sem.n += 1
            self.sem.t[self.sem.n] = self.clock + self.lat
            return (self.sem, self.sem.n)
        return None

    def dma(self, out, in_, sem, *after):
        n = 1
        for d in out.shape:
            n *= d
        self.do(lambda e: e.dma_start(out, in_), *after, sig=False, cost=n * 4 / 350.0)
        w, fn, _, _ = self.ops[-1]
        self.ops[-1] = (w, fn, sem, 16)
        sem.n += 16
        sem.t[sem.n] = self.clock + 2000.0
        return (sem, sem.n)

    def last(self):
        return (self.sem, self.sem.n)

    def emit(self, e):
        for waits, fn, sem, inc in self.ops:
            for s, v in waits:
                e.wait_ge(s.h, v)
            ins = fn(e)
            if sem is not None:
                ins.then_inc(sem.h, inc)


class Buf:
    def __init__(self, ap, free=None):
        self.ap = ap
        self.free = free if free is not None else []


class Ring:

    def __init__(self, bufs):
        self.all = list(bufs)
        self.q = list(bufs)

    def pop(self):
        b = min(self.q, key=lambda b: when(b.free))
        self.q.remove(b)
        return b

    def get(self):
        while not self.q:
            yield None
        return self.pop()

    def put(self, buf, *toks):
        buf.free = list(toks)
        self.q.append(buf)

    def renew(self, toks):
        assert len(self.q) == len(self.all), "a buffer is still out"
        for b in self.q:
            b.free = list(toks)


class Acts:

    def __init__(self, hi, lo):
        self.hi, self.lo = hi, lo
        self.th = [None] * len(hi)
        self.tl = [None] * len(lo)


class Prog:
    pass


def build_program(nc, a, stop=None):
    ctx = ExitStack()
    with ctx:
        P = Prog()
        nsem = [0]

        def sem():
            nsem[0] += 1
            return Sem(ctx.enter_context(nc.semaphore(f"s{nsem[0]}")))

        PE, AC, DV, PO = Queue(sem(), 200.0), Queue(sem()), Queue(sem()), Queue(sem())
        SP = Queue(sem())
        base = BASE
        names = [0]

        def at(off, cols, dt=FP, name=None):
            names[0] += 1
            t = nc.alloc_sbuf_tensor_at(f"{name or 'm'}_{names[0]}", [128, cols], dt, offset=base + off)
            return t

        KB = 1024
        off = [0]

        def take(nbytes):
            o = off[0]
            off[0] += (nbytes + 31) // 32 * 32
            assert off[0] <= LIMIT - base, (off[0], LIMIT - base)
            return o

        def here(cols, dt=FP, size=4, name=None):
            return at(take(cols * size), cols, dt, name)

        prm = here(NPRM, name="prm")
        ident = here(128, name="ident")
        ones = here(128, name="ones")
        permT = here(128, name="permT")
        perm2 = here(128, name="perm2")
        identb = here(128, BF, 2, name="identb")
        wmask = here(256, BF, 2, name="wmask")
        sink = here(16, name="sink")
        M_f = here(1024, FR, name="Mf")
        M_b = here(1024, FR, name="Mb")
        R = here(512, name="R")
        msk = here(7 * 128, U8, 1, name="msk")
        lbt = here(48, name="lbt")
        nlam = here(8, name="nlam")
        small = here(64, name="small")
        tabs = [here(512, name=f"tab{i}") for i in range(4)]
        C_t, S_t, RC, RS = tabs
        NR = 3
        raw = [here(1024, name="raw") for _ in range(NR)]
        whi = [here(1024, FR, name="whi") for _ in range(NR)]
        wlo = [here(1024, FR, name="wlo") for _ in range(NR)]
        X_off = take(16 * KB)
        X = [at(X_off + 2 * KB * k, 512, name="X") for k in range(8)]
        Hh = [here(512, FR, name="Hh") for _ in range(8)]
        Hl = [here(512, FR, name="Hl") for _ in range(8)]
        B0 = off[0]
        BIGSZ = LIMIT - base - B0
        P.bigsz = BIGSZ

        def big(kb, cols, dt=FP, size=4, name=None):
            o = int(kb * KB)
            assert o + cols * size <= BIGSZ, (name, kb, BIGSZ / KB)
            return at(B0 + o, cols, dt, name)

        ps = [ctx.enter_context(nc.psum_tensor(f"ps{i}", [128, 512], FP)) for i in range(8)]
        banks = Ring([Buf(ps[i]) for i in range(8)])

        def bank():
            while len(banks.q) < 3:
                yield None
            b = banks.pop()
            if when(b.free) > PE.clock:
                yield b.free
            return b

        def fence():
            return [PE.last(), AC.last(), DV.last(), PO.last()]

        cur_set = [None]

        def cols_of(ap):
            n = 1
            for d in ap.shape[1:]:
                n *= d
            return n

        def in_psum(*aps):
            return any(x.tensor.name[:2] == "ps" for x in aps)

        def act(out, in_, func, *after, bias=0.0, scale=1.0, accum=None):
            want = ACT_SET.get(func)
            n = cols_of(out)
            cost = 0.834 * n + (52 if in_psum(in_) else 93) + (93 if accum is not None else 0)
            if not isinstance(bias, float) or not isinstance(scale, float):
                cost += 93
            if want is not None and cur_set[0] != want:
                cur_set[0] = want
                AC.do(lambda e: e.preload_act_table_set(want), sig=False, cost=1283)
            if accum is None:
                return AC.do(lambda e: e.activation(out, in_, func, bias=bias, scale=scale), *after, cost=cost)
            return AC.do(lambda e: e.activation(out, in_, func, bias=bias, scale=scale, accum_out=accum), *after,
                         cost=cost)

        def tt(out, x, y, op, *after, q=None):
            n = cols_of(out)
            return (q or DV).do(lambda e: e.tensor_tensor(out, x, y, op), *after,
                                cost=68 + n * (2.26 if q is PO else 1.042))

        def ts(out, x, s1, s2, o1, o2, *after, q=None):
            n = cols_of(out)
            cost = 68 + n * (1.18 if q is PO else 1.042 if in_psum(x) else 0.521)
            if s2 is None:
                return (q or DV).do(lambda e: e.tensor_scalar(out, x, s1, None, o1), *after, cost=cost)
            return (q or DV).do(lambda e: e.tensor_scalar(out, x, s1, s2, o1, o2), *after, cost=cost)

        def stt(out, x, s, y, o1, o2, *after):
            n = cols_of(out)
            return DV.do(lambda e: e.scalar_tensor_tensor(out=out, in0=x, scalar=s, in1=y, op0=o1, op1=o2), *after,
                         cost=68 + 1.16 * n)

        def copy(out, x, *after):
            return DV.do(lambda e: e.tensor_copy(out, x), *after,
                         cost=68 + cols_of(out) * (1.042 if in_psum(x) else 0.521))

        def reduce_max(out, x, *after):
            return DV.do(lambda e: e.tensor_reduce(out, x, AX.X, ALU.max), *after, cost=68 + 1.042 * cols_of(x))

        def mm(out, l, r, start, stop, *after, sig=False):
            n = cols_of(out)
            if l.dtype == FP:
                cost = max(4 * 0.4167 * n + 4, 213)
            elif l.dtype == FR:
                cost = 0.4167 * n + 3 if n >= 256 else 216
            else:
                cost = 0.4167 * n + 3
            return PE.do(lambda e: e.matmul(out, l, r, start=start, stop=stop), *after, sig=sig, cost=cost)

        def tr(out, x, *after, sig=False):
            return PE.do(lambda e: e.transpose(out, x, ident[:, :]), *after, sig=sig, cost=110)

        def mm3(out, Lh, Ll, Rh, Rl, start, stop, *after, sig=False):
            mm(out, Lh, Rh, start, False, *after)
            mm(out, Lh, Rl, False, False)
            return mm(out, Ll, Rh, False, stop, sig=sig)

        V4 = lambda t: t[:, :].rearrange("p (j c) -> p j c", j=4)

        class State:
            pass
        NS = State()
        NS.R_ready = False

        chunks = []
        s_raw = [sem() for _ in range(NR)]
        raw_free = [[] for _ in range(NR)]
        raw_tok = {}
        hi_tok, lo_tok, done = {}, {}, {}

        def load(c):
            if c >= len(chunks):
                return
            w, n = chunks[c]
            s = c % NR
            raw_tok[c] = SP.dma(raw[s][:, 0:n], w, s_raw[s], raw_free[s])

        def prep(c):
            w, n = chunks[c]
            s = c % NR
            yield [raw_tok[c], done.get(c - NR)]
            hi_tok[c] = act(whi[s][:, 0:n], raw[s][:, 0:n], ACT.Copy, raw_tok[c], done.get(c - NR))
            yield [hi_tok[c]]
            lo_tok[c] = tt(wlo[s][:, 0:n], raw[s][:, 0:n], whi[s][:, 0:n].bitcast(FP), ALU.subtract,
                           raw_tok[c], hi_tok[c], done.get(c - NR))
            raw_free[s] = [hi_tok[c], lo_tok[c]]
            load(c + NR)

        first, side = [], []

        def run(lst, ent):
            try:
                ent[1] = next(ent[0])
            except StopIteration:
                lst.remove(ent)

        def pump(limit=0.0, only_first=False):
            n = 0
            for lst in ((first,) if only_first else (first, side)):
                for ent in list(lst):
                    if ent[1] is None:
                        run(lst, ent)
                    elif when(ent[1]) <= max(limit, PE.clock):
                        run(lst, ent)
                        n += 1
            return n

        def spawn(g, lst=None):
            lst = side if lst is None else lst
            lst.append([g, None])
            return lst[-1]

        def advance():
            if pump():
                return
            ents = [(when(e[1]), i, lst, e) for i, (lst, e) in
                    enumerate([(first, e) for e in first] + [(side, e) for e in side]) if e[1] is not None]
            if not ents:
                NS.stuck += 1
                assert NS.stuck < 50, "no work can go on"
                return
            NS.stuck = 0
            _, _, lst, ent = min(ents, key=lambda v: v[:2])
            run(lst, ent)

        def until(cond):
            while not cond():
                advance()

        def settle():
            until(lambda: not side and not first)

        NS.stuck = 0
        NS.evacs = 0
        NS.evaced = 0

        jobs = []

        def job(chs, nb, evac, before=None):
            ids = []
            for w, n, segs in chs:
                ids.append(len(chunks))
                chunks.append((w, n))
            jobs.append((ids, [c[2] for c in chs], nb, evac, before))

        def evac_gen(f, bks, tok, no):
            while NS.evaced != no:
                yield None
            yield [tok]
            while not NS.R_ready:
                yield None
            f(bks, tok)
            NS.evaced += 1

        def run_jobs():
            for ids, segs, nb, evac, before in jobs:
                if before is not None:
                    before()
                bks = None
                for c, sg in zip(ids, segs):
                    if c + 2 < len(chunks):
                        spawn(prep(c + 2), first)
                    s = c % NR
                    for i, (k, A, kt, b, st, sp) in enumerate(sg):
                        until(lambda: c in lo_tok and A.tl[kt] is not None and A.th[kt] is not None)
                        if bks is None:
                            until(lambda: len(banks.q) >= nb)
                            bks = [banks.pop() for _ in range(nb)]
                            bfree = [x.free for x in bks]
                        free = bfree[b] if st else None
                        need = when([hi_tok[c], A.th[kt], free])
                        pump()
                        while PE.clock + 30 < need and pump(need):
                            pass
                        out = bks[b].ap[:, :]
                        wh = whi[s][:, 128 * k:128 * k + 128]
                        wl = wlo[s][:, 128 * k:128 * k + 128]
                        mm(out, wh, A.hi[kt], st, False, hi_tok[c], A.th[kt], free)
                        mm(out, wh, A.lo[kt], False, False, A.tl[kt])
                        done[c] = mm(out, wl, A.hi[kt], False, sp, lo_tok[c], sig=True)
                tok = done[ids[-1]]
                spawn(evac_gen(evac, bks, tok, NS.evacs), first)
                NS.evacs += 1

        s_c, s_x, s_p = sem(), [sem() for _ in range(8)], sem()
        stage = big(0, 2048, name="stage")
        mst = big(20, 896, name="mst")
        posi = big(8, 512, I32, name="posi")
        lamv = big(10, 512, name="lamv")
        for o, i in ((prm, a["prm"]), (ident, a["cst"][:, 0:128]), (ones, a["cst"][:, 128:256]),
                     (permT, a["cst"][:, 256:384]), (perm2, a["cst"][:, 384:512]), (mst, a["msk"]), (stage, a["mcst"])):
            t_c = SP.dma(o[:, :], i, s_c)
        for k in range(8):
            SP.dma(X[k][:, :], a["xT"][:, 512 * k:512 * k + 512], s_x[k])
        xt = [(s_x[k], 16) for k in range(8)]
        t_p = SP.dma(posi[:, :], a["pos"].broadcast_to([128, 512]), s_p)
        t_p = SP.dma(lamv[:, :], a["lam"].broadcast_to([128, 512]), s_p)
        t_p = SP.dma(sink[:, :], a["sink"].broadcast_to([128, 16]), s_p)
        wst = big(18, 384, name="wst")
        t_w = SP.dma(wst[:, :], a["wmask"], s_p)
        t_wm = [act(wmask[:, :], wst[:, 0:256], ACT.Copy, t_w), act(identb[:, :], ident[:, :], ACT.Copy, t_c)]
        t_msk = DV.do(lambda e: e.tensor_copy(msk[:, :], mst[:, :]), t_c)
        t_M = [act(M_f[:, :], stage[:, 0:1024], ACT.Copy, t_c), act(M_b[:, :], stage[:, 1024:2048], ACT.Copy, t_c)]

        def col(name, i):
            return prm[:, PCOL[name] + i:PCOL[name] + i + 1]

        lbraw = prm[:, PCOL["lb"]:PCOL["lb"] + 16].rearrange("p (d l h) -> p d l h", d=2, l=2)
        sc8 = lambda i: lbt[:, 8 * i:8 * i + 8].rearrange("p (d h) -> p d h", d=2)
        la, lc, lca, w0, w1, w2 = [sc8(i) for i in range(6)]
        t = tt(w0, lbraw[:, :, 0, :], lbraw[:, :, 1, :], ALU.max, t_c)
        t0 = tt(w1, lbraw[:, :, 0, :], w0, ALU.subtract, t)
        t1 = tt(w2, lbraw[:, :, 1, :], w0, ALU.subtract, t0)
        t0 = act(w1, w1, ACT.Exp, t1)
        t1 = act(w2, w2, ACT.Exp, t1)
        t = tt(w0, w1, w2, ALU.add, t1)
        t = DV.do(lambda e: e.reciprocal(lbt[:, 24:32], lbt[:, 24:32]), t)
        t0 = tt(w1, w1, w0, ALU.mult, t)
        t1 = tt(w2, w2, w0, ALU.mult, t0)
        t = tt(w0, w1, w2, ALU.add, t1)
        t = tt(w0, w0, w1, ALU.subtract, t)
        t = ts(w1, w0, -1.0, 1.0, ALU.mult, ALU.add, t)
        for src, dst in ((w0, la), (w1, lc)):
            t = ts(w2, src, 1e-18, None, ALU.max, None, t)
            t = act(dst, w2, ACT.Ln, t)
            t = ts(w2, src, 0.0, -BIG, ALU.is_le, ALU.mult, t)
            t = tt(dst, dst, w2, ALU.add, t)
        t_lb = tt(lca, lc, la, ALU.subtract, t)
        lam4 = lamv[:, :].rearrange("p (l r e) -> p l r e", l=2, r=4)
        prod = big(12, 256, name="prod")
        pr4 = prod[:, :].rearrange("p (l r e) -> p l r e", l=2, r=2)
        tt(pr4[:, :, 0, :], lam4[:, :, 0, :], lam4[:, :, 1, :], ALU.mult, t_p)
        t = tt(pr4[:, :, 1, :], lam4[:, :, 2, :], lam4[:, :, 3, :], ALU.mult, t_p)
        t = DV.do(lambda e: e.tensor_reduce(small[:, 0:4], prod[:, :].rearrange("p (a e) -> p a e", a=4), AX.X, ALU.add), t)
        t = act(small[:, 0:4], small[:, 0:4], ACT.Exp, t)
        for l in range(2):
            li = 0.8 - 0.6 * math.exp(-0.3 * l)
            t0 = tt(nlam[:, l:l + 1], small[:, 2 * l + 1:2 * l + 2], small[:, 2 * l:2 * l + 1], ALU.subtract, t)
            t_lam = ts(nlam[:, l:l + 1], nlam[:, l:l + 1], -li, None, ALU.add, None, t0)
            c0 = PCOL["da_norm"] + 4 * l
            t_lam = ts(prm[:, c0:c0 + 4], prm[:, c0:c0 + 4], 1.0 - li, None, ALU.mult, None, t_lam, t_c)

        def tables():
            ang, n1, m1, m2 = [big(k, 512, name="rt") for k in (92, 94, 96, 98)]
            MAGIC = 12582912.0
            t = DV.do(lambda e: e.tensor_copy(ang[:, :], posi[:, :]), t_p, fence())
            t = ts(ang[:, :], ang[:, :], col("invf", 0), None, ALU.mult, None, t, t_c)
            two_pi = 2.0 * math.pi
            c1 = 201.0 / 32.0
            r1 = two_pi - c1

            def top(v, bits):
                m, e = math.frexp(v)
                return math.ldexp(math.floor(m * 2 ** bits), e - bits)
            c2 = top(r1, 8)
            c3 = top(r1 - c2, 8)
            c4 = r1 - c2 - c3
            K = 65536.0
            d2 = top(r1 * K, 11)
            d3 = r1 * K - d2
            yield [t]
            t = ts(n1[:, :], ang[:, :], 1.0 / (two_pi * K), MAGIC, ALU.mult, ALU.add, t)
            t = ts(n1[:, :], n1[:, :], MAGIC, None, ALU.subtract, None, t)
            for cc in (c1 * K, d2):
                t = stt(ang[:, :], n1[:, :], -cc, ang[:, :], ALU.mult, ALU.add, t)
            yield [t]
            for rnd in range(2):
                t = ts(m1[:, :], ang[:, :], 1.0 / two_pi, MAGIC, ALU.mult, ALU.add, t)
                t = ts(m1[:, :], m1[:, :], MAGIC, None, ALU.subtract, None, t)
                for cc in (c1, c2, c3, c4):
                    t = stt(ang[:, :], m1[:, :], -cc, ang[:, :], ALU.mult, ALU.add, t)
                yield [t]
                if rnd == 0:
                    t = stt(ang[:, :], n1[:, :], -d3, ang[:, :], ALU.mult, ALU.add, t)
            t = ts(ang[:, :], ang[:, :], 3.1415925, -3.1415925, ALU.min, ALU.max, t)
            t1 = act(S_t[:, :], ang[:, :], ACT.Sin, t)
            t2 = act(m1[:, :], ang[:, :], ACT.Sin, t, scale=0.5)
            t2 = act(m1[:, :], m1[:, :], ACT.Square, t2)
            yield [t2]
            t = ts(C_t[:, :], m1[:, :], -2.0, 1.0, ALU.mult, ALU.add, t2)
            NS.t_tab = [t1, t]

        st_ring = Ring([Buf(small[:, 8 * i:8 * i + 8]) for i in range(1, 7)])

        def rstd(sq, t_sq, scale, eps, D, Dfree, out):
            yield [t_sq]
            b = yield from bank()
            for j in range(4):
                t = mm(b.ap[:, j:j + 1], sq[:, 128 * j:128 * j + 128], ones[:, 0:1], True, True, t_sq, t_c,
                       b.free, sig=(j == 3))
            s = yield from st_ring.get()
            yield [t]
            t = ts(s.ap[:, 0:4], b.ap[:, 0:4], scale, eps, ALU.mult, ALU.add, t, s.free)
            banks.put(b, t)
            t = PO.do(lambda e: e.tensor_tensor(s.ap[:, 4:8], s.ap[:, 0:4], pm05[:, 0:4], ALU.pow), t, t_pm, cost=960)
            yield [t]
            t = tt(D[:, :].rearrange("p (j c) -> p j c", j=4), ident[:, None, :].broadcast_to([128, 4, 128]),
                   s.ap[:, 4:8][:, :, None].broadcast_to([128, 4, 128]), ALU.mult, t, t_c, Dfree)
            st_ring.put(s, t)
            yield [t]
            b = yield from bank()
            t = mm(b.ap[:, :], ones[:, :], D[:, :], True, True, t, b.free, sig=True)
            out["bank"], out["tok"] = b, t
            yield [t]

        pm05 = nlam[:, 4:8]
        t_pm = PO.do(lambda e: e.memset(pm05, -0.5))


        slot = [[big(22 * s + 2 * i, 512, FR if i in (6, 7, 8, 9) else FP) for i in range(11)] for s in range(2)]
        E_t = [big(44, 2048), big(52, 2048)]
        E_r = [Ring([Buf(E_t[0])]), Ring([Buf(E_t[1])])]
        KQ = Ring([Buf((big(60 + 4 * i, 512), big(62 + 4 * i, 512))) for i in range(4)])
        AT = big(76, 2560)
        AT_r = Ring([Buf(AT)])
        TMP = Ring([Buf(big(84 + 2 * i, 512)) for i in range(4)])
        nb_o, nb_sq, nb_D, nb_r = [big(92 + 2 * i, 512) for i in range(4)]
        NB = Ring([Buf((nb_o, nb_sq, nb_D, nb_r))])
        g_off = [100, 102, 104, 106, 64, 66, 68, 70, 72, 74, 22, 24, 26, 28, 30, 32]
        gate = [big(o, 512) for o in g_off]
        gateR = [big(o, 512, FR) for o in g_off]
        oH = Acts([at(X_off + 2 * KB * h, 512, FR) for h in range(4)],
                  [at(X_off + 8 * KB + 2 * KB * h, 512, FR) for h in range(4)])
        oD = Acts([big(34 + 2 * h, 512, FR) for h in range(4)], [big(76 + 2 * h, 512, FR) for h in range(4)])
        daq = [big(2 * i, 512, FR) for i in range(6)]
        E4 = Ring([Buf(big(12 + 2 * i, 512)) for i in range(4)])
        WT = [big(44, 2048, FR), big(52, 2048, FR)]
        QK_r, V_r, WT_r = (Ring([Buf(None)]) for _ in range(3))
        Wr = Ring([Buf(big(60 + 2 * i, 512)) for i in range(2)])
        hid = Acts([big(2 * i, 512, FR) for i in range(22)], [big(44 + 2 * i, 512, FR) for i in range(22)])
        FT = Ring([Buf(big(o, 512)) for o in (88, 90, 98, 100, 102, 104, 106)])
        H = Acts([t[:, :] for t in Hh], [t[:, :] for t in Hl])
        tv = lambda t: t[:, :]
        for A_ in (oH, oD, hid):
            A_.hi = [tv(t) for t in A_.hi]
            A_.lo = [tv(t) for t in A_.lo]

        def view(t, n, half):
            return t[:, :].rearrange("p (t b h e) -> p t b h e", t=4, h=2, e=n // 2)[:, :, :, half, :]

        def eview(t, j, n, half):
            return t[:, :].rearrange("p (t j b h e) -> p t j b h e", t=4, j=4, h=2, e=n // 2)[:, :, j, :, half, :]

        def prep_x(k, gname, gi, tok, hfree, sfree):
            def g():
                yield [tok]
                th = act(H.hi[k], X[k][:, :], ACT.Copy, tok, hfree, scale=col(gname, gi))
                q = PO
                if k == 0:
                    NS.t = tt(nb_o[:, :], X[k][:, :], X[k][:, :], ALU.mult, tok, sfree, q=q)
                else:
                    t = tt(nb_sq[:, :], X[k][:, :], X[k][:, :], ALU.mult, tok, sfree, NS.t, q=q)
                    NS.t = tt(nb_o[:, :], nb_o[:, :], nb_sq[:, :], ALU.add, t, NS.t, q=q)
                if k == 7:
                    spawn(make_R(1.0 / 1024.0, EPS_RMS))
                yield [th]
                H.tl[k] = stt(H.lo[k], X[k][:, :], col(gname, gi), H.hi[k].bitcast(FP), ALU.mult, ALU.subtract,
                              th, hfree)
                H.th[k] = th
            H.th[k] = H.tl[k] = None
            if k == 7:
                NS.R_ready = False
            spawn(g(), first)

        def make_R(scale, eps):
            o = {}
            yield from rstd(nb_o, NS.t, scale, eps, nb_D, fence(), o)
            NS.tR = act(R[:, :], o["bank"].ap[:, :], ACT.Copy, o["tok"], fence())
            banks.put(o["bank"], NS.tR)
            NS.R_ready = True

        class Head:
            pass

        def hg_gate(st, l, h, d, bk, tok):
            k_, g_, Gh, Gl = slot[st.s][d], slot[st.s][4 + d], slot[st.s][6 + 2 * d], slot[st.s][7 + 2 * d]
            z = yield from TMP.get()
            w = yield from TMP.get()
            t = tt(z.ap[:, :], bk.ap[:, :], R[:, :], ALU.mult, tok, NS.tR, z.free)
            banks.put(bk, t)
            yield [t]
            t1 = act(w.ap[:, :], z.ap[:, :], ACT.Abs, t, w.free)
            t1 = act(w.ap[:, :], w.ap[:, :], ACT.Exp, t1, scale=-1.0)
            t1 = act(w.ap[:, :], w.ap[:, :], ACT.Ln, t1, bias=1.0)
            yield [t1]
            while st.prev2 is not None and st.prev2.last_a is None:
                yield None
            fr = st.prev2.last_a if st.prev2 is not None else st.free
            t2 = stt(g_[:, :], z.ap[:, :], 0.0, w.ap[:, :], ALU.min, ALU.subtract, t1, fr)
            t3 = tt(z.ap[:, :], g_[:, :], z.ap[:, :], ALU.subtract, t2)
            yield [t3]
            if l == 0:
                tk = act(k_[:, :], z.ap[:, :], ACT.Exp, t3, fr)
                tg = t2
            else:
                cc, aa, ca = (lbt[:, 8 * i + 4 * d + h:8 * i + 4 * d + h + 1] for i in (1, 0, 2))
                tk = act(k_[:, :], z.ap[:, :], ACT.Exp, t3, t_lb, fr, bias=cc)
                t1 = act(w.ap[:, :], g_[:, :], ACT.Abs, t2, bias=ca)
                t1 = act(w.ap[:, :], w.ap[:, :], ACT.Exp, t1, scale=-1.0)
                t1 = act(w.ap[:, :], w.ap[:, :], ACT.Ln, t1, bias=1.0)
                yield [t1]
                t2 = ts(g_[:, :], g_[:, :], cc, aa, ALU.add, ALU.max, t1)
                tg = tt(g_[:, :], g_[:, :], w.ap[:, :], ALU.add, t2)
            TMP.put(z, tk)
            TMP.put(w, tg)
            st.k[d] = tk
            yield [tg]
            b = yield from bank()
            for j in range(4):
                t = tr(b.ap[:, 128 * j:128 * j + 128], g_[:, 128 * j:128 * j + 128], tg, b.free, t_c, sig=(j == 3))
            yield [t]
            t1 = act(Gh[:, :], b.ap[:, :], ACT.Copy, t, fr)
            te = act(g_[:, :], g_[:, :], ACT.Exp, t)
            yield [t1]
            t2 = tt(Gl[:, :], b.ap[:, :], Gh[:, :].bitcast(FP), ALU.subtract, t1)
            banks.put(b, t2)
            st.eg[d], st.G[d] = te, [t1, t2]

        def hg_v(st, bk, tok):
            z = yield from TMP.get()
            t = tt(z.ap[:, :], bk.ap[:, :], R[:, :], ALU.mult, tok, NS.tR, z.free)
            banks.put(bk, t)
            yield [t]
            b = yield from bank()
            for j in range(4):
                t1 = tr(b.ap[:, 128 * j:128 * j + 128], z.ap[:, 128 * j:128 * j + 128], t, b.free, t_c, sig=(j == 3))
            TMP.put(z, t1)
            yield [t1]
            while st.prev2 is not None and st.prev2.last_v is None:
                yield None
            st.v = act(slot[st.s][3][:, :], b.ap[:, :], ACT.Copy, t1,
                       st.prev2.last_v if st.prev2 is not None else st.free)
            banks.put(b, st.v)

        def hg_q(st, bk, tok):
            while st.prev2 is not None and st.prev2.last_a is None:
                yield None
            st.q = tt(slot[st.s][2][:, :], bk.ap[:, :], R[:, :], ALU.mult, tok, NS.tR,
                      st.prev2.last_a if st.prev2 is not None else st.free)
            banks.put(bk, st.q)

        def hg_g(st, bk, tok):
            z = yield from TMP.get()
            t1 = tt(z.ap[:, :], bk.ap[:, :], R[:, :], ALU.mult, tok, NS.tR, z.free)
            banks.put(bk, t1)
            yield [t1]
            while st.prev2 is not None and st.prev2.last_g is None:
                yield None
            st.bg = act(slot[st.s][10][:, :], z.ap[:, :], ACT.Sigmoid, t1,
                        st.prev2.last_g if st.prev2 is not None else st.free)
            TMP.put(z, st.bg)

        def hg_main(st, l, h, prev):
            sl = slot[st.s]
            kf, kb, q, V, egf, egb = sl[:6]
            bg = sl[10]

            def exps(d, grp, eb):
                G, M, E = (sl[6 + 2 * d], sl[7 + 2 * d]), (M_f, M_b)[d], E_t[d]
                out = []
                for j in range(4):
                    b = yield from bank()
                    for i in range(2):
                        t = mm(b.ap[:, :], G[i][:, 128 * j:128 * j + 128], M[:, 512 * grp:512 * grp + 512],
                               i == 0, i == 1, st.G[d], t_M, b.free, sig=(i == 1))
                    out.append((b, t))
                for j, (b, t) in enumerate(out):
                    yield [t]
                    st.E[d] = act(E[:, 512 * j:512 * j + 512], b.ap[:, :], ACT.Exp, t, eb.free)
                    banks.put(b, st.E[d])
                yield [st.E[d]]

            def half(K, Q, j, n, d, free):
                E = E_t[d]
                kk = (kf, kb)[d]
                kh, qh = (0, 1) if d == 0 else (1, 0)
                t1 = tt(view(K, n, kh), view(kk, n, kh), eview(E, j, n, kh), ALU.mult, st.k[d], st.E[d], free)
                t2 = tt(view(Q, n, qh), view(q, n, qh), eview(E, j, n, qh), ALU.mult, st.q, st.E[d], free)
                return [t1, t2]

            ATd = AT[:, :].rearrange("p (i c) -> p i c", c=640)[:, :, 0:128]

            def scores(kq, K, Q, lev):
                yield [kq.t]
                if lev == 0:
                    st.atb = yield from AT_r.get()
                else:
                    while st.at is None:
                        yield None
                b = yield from bank()
                for j in range(4):
                    s_ = slice(128 * j, 128 * j + 128)
                    t = mm(b.ap[:, s_], K[:, s_], Q[:, s_], True, True, kq.t, b.free, sig=(j == 3))
                KQ.put(kq, t)
                yield [t]
                if lev == 0:
                    st.at = act(ATd, V4(b.ap), ACT.Copy, t, st.atb.free)
                else:
                    m_ = msk[:, 128 * (lev - 1):128 * lev]
                    st.at = DV.do(lambda e: e.copy_predicated(ATd, m_[:, None, :].broadcast_to([128, 4, 128]),
                                                              V4(b.ap)), t, st.at, t_msk, cost=602)
                banks.put(b, st.at)
                st.levels += 1

            def offs(b, d):
                K, Q = b.ap
                E = E_t[d]
                kk = (kf, kb)[d]
                E5 = E[:, :].rearrange("p (t j c) -> p t j c", t=4, j=4)
                k4, q4, K4, Q4 = V4(kk), V4(q), V4(K), V4(Q)
                k_e = E5[:, :, 2, :]
                q_e = E5[:, :, 3, :]
                tot = lambda j: q_e[:, j, 127:128] if d == 0 else q_e[:, j, 0:1]
                w = [st.k[d], st.q, st.E[d], b.free]
                pr = lambda ap, o: ap.rearrange("p (a b) c -> p a b c", b=2)[:, :, o, :]
                if d == 0:
                    t = tt(K4[:, 0:3, :], k4[:, 0:3, :], k_e[:, 0:3, :], ALU.mult, w)
                    t1 = ts(K4[:, 3, :], K4[:, 0, :], tot(1), None, ALU.mult, None, t)
                    tt(Q4[:, 0:2, :], pr(q4, 1), pr(q_e, 1), ALU.mult, w)
                    t = tt(Q4[:, 2, :], q4[:, 2, :], q_e[:, 2, :], ALU.mult, w)
                    t2 = ts(Q4[:, 3, :], Q4[:, 1, :], tot(2), None, ALU.mult, None, t)
                else:
                    t = tt(K4[:, 0:3, :], k4[:, 1:4, :], k_e[:, 1:4, :], ALU.mult, w)
                    t1 = ts(K4[:, 3, :], K4[:, 2, :], tot(2), None, ALU.mult, None, t)
                    tt(Q4[:, 2:4, :], pr(q4, 0), pr(q_e, 0), ALU.mult, w)
                    t = tt(Q4[:, 1, :], q4[:, 1, :], q_e[:, 1, :], ALU.mult, w)
                    t2 = ts(Q4[:, 0, :], Q4[:, 2, :], tot(1), None, ALU.mult, None, t)
                b.t = [t1, t2]

            def off_scores(kq, d):
                yield [kq.t]
                while st.atb is None:
                    yield None
                K, Q = kq.ap
                c = lambda t_, i, n=1: t_[:, 128 * i:128 * (i + n)]
                ba = yield from bank()
                if d == 0:
                    mm(c(ba.ap, 0), c(K, 0), c(Q, 0), True, True, kq.t, ba.free)
                    t = mm(c(ba.ap, 1, 2), c(K, 3), c(Q, 2, 2), True, True, sig=True)
                else:
                    mm(c(ba.ap, 0, 2), c(K, 3), c(Q, 0, 2), True, True, kq.t, ba.free)
                    t = mm(c(ba.ap, 2), c(K, 2), c(Q, 3), True, True, sig=True)
                bb = yield from bank()
                if d == 0:
                    mm(c(bb.ap, 0, 2), c(K, 1), c(Q, 2, 2), True, True, bb.free)
                    t2 = mm(c(bb.ap, 2), c(K, 2), c(Q, 1), True, True, sig=True)
                else:
                    mm(c(bb.ap, 0, 2), c(K, 1), c(Q, 0, 2), True, True, bb.free)
                    t2 = mm(c(bb.ap, 2), c(K, 0), c(Q, 2), True, True, sig=True)
                KQ.put(kq, t2)
                yield [t]
                fr = st.atb.free
                o1, o2, o3 = ((1, 6, 11), (12, 8, 4))[d]
                t = act(c(AT, o1, 3), c(ba.ap, 0, 3), ACT.Copy, t, fr)
                banks.put(ba, t)
                yield [t2]
                act(c(AT, o2, 2), c(bb.ap, 0, 2), ACT.Copy, t2, fr)
                st.off[d] = act(c(AT, o3), c(bb.ap, 2), ACT.Copy, t2)
                banks.put(bb, st.off[d])

            ready = lambda: st.q is not None and st.G[0] is not None and st.G[1] is not None
            while not ready() or (prev is not None and not prev.passed_E):
                yield None
            yield [st.G[0]]
            st.levels, st.at, st.atb = 0, None, None
            l128 = yield from KQ.get()
            for d in range(2):
                eb = yield from E_r[d].get()
                yield from exps(d, 0, eb)
                if d == 0:
                    l128.t = [half(l128.ap[0], l128.ap[1], 0, 128, 0, l128.free)]
                    l64 = yield from KQ.get()
                    l64.t = [half(l64.ap[0], l64.ap[1], 1, 64, 0, l64.free)]
                else:
                    l128.t.append(half(l128.ap[0], l128.ap[1], 0, 128, 1, l128.free))
                    spawn(scores(l128, l128.ap[0], l128.ap[1], 0))
                    l64.t.append(half(l64.ap[0], l64.ap[1], 1, 64, 1, l64.free))
                    spawn(scores(l64, l64.ap[0], l64.ap[1], 1))
                of = yield from KQ.get()
                offs(of, d)
                spawn(off_scores(of, d))
                E_r[d].put(eb, of.t)
                if d == 0:
                    yield [st.G[1]]
            dg = yield from KQ.get()
            dg.t = [tt(dg.ap[0][:, :], kf[:, :], kb[:, :], ALU.add, st.k, dg.free), st.q]
            spawn(scores(dg, dg.ap[0], q, 7))
            l2 = yield from KQ.get()
            K, Q = l2.ap
            l2.t = [copy(view(K, 2, 0), view(kf, 2, 0), st.k, l2.free),
                    copy(view(K, 2, 1), view(kb, 2, 1), st.k, l2.free),
                    tt(view(Q, 2, 1), view(q, 2, 1), view(egf, 2, 1), ALU.mult, st.q, st.eg, l2.free),
                    tt(view(Q, 2, 0), view(q, 2, 0), view(egb, 2, 0), ALU.mult, st.q, st.eg, l2.free)]
            spawn(scores(l2, K, Q, 6))
            ebs = []
            for d in range(2):
                eb = yield from E_r[d].get()
                ebs.append(eb)
                yield from exps(d, 1, eb)
            for j, n in enumerate((32, 16, 8, 4)):
                kq = yield from KQ.get()
                kq.t = [half(kq.ap[0], kq.ap[1], j, n, d, kq.free) for d in range(2)]
                spawn(scores(kq, kq.ap[0], kq.ap[1], 2 + j))
            for d in range(2):
                E_r[d].put(ebs[d], kq.t)
            st.passed_E = True
            while st.levels < 8 or st.off[0] is None or st.off[1] is None or st.v is None:
                yield None
            st.last_a = fence()
            yield [st.at, st.off, st.v]
            b = yield from bank()
            for i in range(4):
                t = mm(b.ap[:, :], V[:, 128 * i:128 * i + 128], AT[:, 512 * i:512 * i + 512], i == 0, i == 3,
                       st.at, st.off, st.v, b.free, sig=(i == 3))
            AT_r.put(st.atb, t)
            st.last_v = [t]
            yield from norm_out(b, t, col("hg_norm", 4 * l + h), bg, st, oH, h, oH_free)
            st.last_g = fence()

        def norm_out(b, t, gcol, extra, st, O, h, ofree):
            nb = yield from NB.get()
            yield [t]
            to = act(nb_o[:, :], b.ap[:, :], ACT.Copy, t, nb.free)
            banks.put(b, to)
            tq = act(nb_sq[:, :], nb_o[:, :], ACT.Square, to)
            o = {}
            yield from rstd(nb_sq, tq, 1.0 / 128.0, EPS_RMS, nb_D, nb.free, o)
            t = stt(nb_r[:, :], nb_o[:, :], gcol, o["bank"].ap[:, :], ALU.mult, ALU.mult, o["tok"], t_lam)
            banks.put(o["bank"], t)
            if extra is not None:
                while st.bg is None:
                    yield None
                t = tt(nb_r[:, :], nb_r[:, :], extra[:, :], ALU.mult, t, st.bg)
            yield [t]
            th = act(O.hi[h], nb_r[:, :], ACT.Copy, t, ofree())
            yield [th]
            O.tl[h] = tt(O.lo[h], nb_r[:, :], O.hi[h].bitcast(FP), ALU.subtract, th)
            O.th[h] = th
            NB.put(nb, O.tl[h])

        def da_rope(st, which, bk, tok):
            z = yield from TMP.get()
            w = yield from TMP.get()
            t = act(z.ap[:, :], bk.ap[:, :], ACT.Copy, tok, z.free)
            banks.put(bk, t)
            yield [t]
            b = yield from bank()
            t1 = mm(b.ap[:, :], permT[:, :], z.ap[:, :], True, True, t, b.free, t_c, sig=True)
            yield [t1]
            t2 = tt(w.ap[:, :], b.ap[:, :], RS[:, :], ALU.mult, t1, NS.tRC, w.free)
            banks.put(b, t2)
            t3 = tt(z.ap[:, :], z.ap[:, :], RC[:, :], ALU.mult, t1)
            t4 = tt(z.ap[:, :], z.ap[:, :], w.ap[:, :], ALU.add, t3, t2)
            TMP.put(w, t4)
            yield [t4]
            if which == 0:
                st.qk_b = yield from QK_r.get()
            while st.qk_b is None:
                yield None
            th = act(daq[2 * which][:, :], z.ap[:, :], ACT.Copy, t4, st.qk_b.free)
            yield [th]
            tl = tt(daq[2 * which + 1][:, :], z.ap[:, :], daq[2 * which][:, :].bitcast(FP), ALU.subtract, th,
                    st.qk_b.free)
            TMP.put(z, tl)
            st.qk[which] = [th, tl]

        def da_v(st, bk, tok):
            z = yield from TMP.get()
            t = tt(z.ap[:, :], bk.ap[:, :], R[:, :], ALU.mult, tok, NS.tR, z.free)
            banks.put(bk, t)
            yield [t]
            b = yield from bank()
            for j in range(4):
                t1 = tr(b.ap[:, 128 * j:128 * j + 128], z.ap[:, 128 * j:128 * j + 128], t, b.free, sig=(j == 3))
            TMP.put(z, t1)
            st.v_b = yield from V_r.get()
            yield [t1]
            th = act(daq[4][:, :], b.ap[:, :], ACT.Copy, t1, st.v_b.free)
            yield [th]
            tl = tt(daq[5][:, :], b.ap[:, :], daq[4][:, :].bitcast(FP), ALU.subtract, th, st.v_b.free)
            banks.put(b, tl)
            st.v = [th, tl]

        def da_block(st, l, qt):
            sm = yield from st_ring.get()
            mx, ng, su, r_ = (sm.ap[:, 2 * i:2 * i + 2] for i in range(4))
            qs = slice(128 * qt, 128 * qt + 128)
            bs, es = [], []
            for c in range(2):
                p = slice(64 * c, 64 * c + 64)
                b = yield from bank()
                t = mm3(b.ap[:, :], daq[0][p, qs], daq[1][p, qs], daq[2][p, :], daq[3][p, :], True, True,
                        [st.qk[0], st.qk[1]], b.free, sig=True)
                bs.append((b, t))
            st.scored = t
            st.nsc += 1
            for c, (b, t) in enumerate(bs):
                yield [t]
                tm = reduce_max(mx[:, c:c + 1], b.ap[:, :], t, sm.free)
                tn = ts(ng[:, c:c + 1], mx[:, c:c + 1], -0.125, None, ALU.mult, None, tm, sm.free)
                bs[c] = (b, [t, tn])
            for c, (b, t) in enumerate(bs):
                e_ = yield from E4.get()
                yield [t]
                te = act(e_.ap[:, :], b.ap[:, :], ACT.Exp, t, e_.free, bias=ng[:, c:c + 1], scale=0.125,
                         accum=su[:, c:c + 1])
                banks.put(b, te)
                es.append((e_, te))
            w = yield from Wr.get()
            yield [te]
            t = DV.do(lambda e: e.reciprocal(r_, su), te, es[0][1], cost=81)
            t = tt(r_[:, 1:2], r_[:, 1:2], nlam[:, l:l + 1], ALU.mult, t, t_lam)
            t1 = ts(w.ap[:, :], es[0][0].ap[:, :], r_[:, 0:1], None, ALU.mult, None, t, w.free)
            t2 = stt(w.ap[:, :], es[1][0].ap[:, :], r_[:, 1:2], w.ap[:, :], ALU.mult, ALU.add, t1)
            st_ring.put(sm, t2)
            E4.put(es[0][0], t2)
            E4.put(es[1][0], t2)
            yield [t2]
            if qt == 0:
                st.wt_b = yield from WT_r.get()
            while st.wt_b is None:
                yield None
            b = yield from bank()
            for j in range(4):
                t = tr(b.ap[:, 128 * j:128 * j + 128], w.ap[:, 128 * j:128 * j + 128], t2, b.free, sig=(j == 3))
            Wr.put(w, t)
            dst = [V4(W_)[:, :, qs] for W_ in WT]
            yield [t]
            th = act(dst[0], V4(b.ap), ACT.Copy, t, st.wt_b.free)
            yield [th]
            tl = tt(dst[1], V4(b.ap), dst[0].bitcast(FP), ALU.subtract, th, st.wt_b.free)
            banks.put(b, tl)
            st.WT += [th, tl]
            st.nwt += 1

        def da_main(st, l, h):
            st.nsc, st.nwt, st.WT, st.wt_b = 0, 0, [], None
            while st.qk[0] is None or st.qk[1] is None:
                yield None
            yield st.qk[0] + st.qk[1]
            for qt in range(4):
                spawn(da_block(st, l, qt))
                while st.nsc <= qt:
                    yield None
            QK_r.put(st.qk_b, st.scored)
            while st.nwt < 4 or st.v is None:
                yield None
            yield st.WT + st.v
            b = yield from bank()
            for j in range(4):
                s_ = slice(128 * j, 128 * j + 128)
                t = mm3(b.ap[:, :], daq[4][:, s_], daq[5][:, s_], WT[0][:, 512 * j:512 * j + 512],
                        WT[1][:, 512 * j:512 * j + 512], j == 0, j == 3, [st.WT, st.v], b.free, sig=(j == 3))
            WT_r.put(st.wt_b, t)
            V_r.put(st.v_b, t)
            yield from norm_out(b, t, col("da_norm", 4 * l + h), None, st, oD, h, oD_free)

        oH_free = lambda: NS.oH_free()
        oD_free = lambda: NS.oD_free

        s_re = [sem() for _ in range(8)]
        s_sp = sem()
        scr = a["scr"]
        xtok = list(xt)

        def w1(name, l, n):
            return a[name][l, n]

        def in_job(l, n, evac, before=None):
            job([(a["win1"][l, n], 1024, [(k, H, k, 0, k == 0, k == 7) for k in range(8)])], 1, evac, before)

        def first_block(l):
            hs = [Head() for _ in range(4)]
            ds = [Head() for _ in range(4)]

            def start_layer():
                if l == 0:
                    for k in range(8):
                        H.th[k] = act(H.hi[k], X[k][:, :], ACT.Copy, xtok[k], t_c, scale=col("attn_norm", k))
                        H.tl[k] = stt(H.lo[k], X[k][:, :], col("attn_norm", k), H.hi[k].bitcast(FP),
                                      ALU.mult, ALU.subtract, H.th[k])
                    ta = tb = None
                    for k in range(4):
                        if k == 0:
                            ta = tt(nb_o[:, :], X[0][:, :], X[0][:, :], ALU.mult, xtok[0], q=PO)
                            tb = tt(nb_r[:, :], X[4][:, :], X[4][:, :], ALU.mult, xtok[4])
                        else:
                            t1 = tt(nb_sq[:, :], X[k][:, :], X[k][:, :], ALU.mult, xtok[k], ta, q=PO)
                            ta = tt(nb_o[:, :], nb_o[:, :], nb_sq[:, :], ALU.add, t1, q=PO)
                            t1 = tt(nb_D[:, :], X[4 + k][:, :], X[4 + k][:, :], ALU.mult, xtok[4 + k], tb)
                            tb = tt(nb_r[:, :], nb_r[:, :], nb_D[:, :], ALU.add, t1)
                    NS.t = tt(nb_o[:, :], nb_o[:, :], nb_r[:, :], ALU.add, ta, tb)
                    f = fence()
                    NS.oH_free = lambda: f
                else:
                    NS.oH_free = lambda: NS.spill + [fence()]
                for r_ in (KQ, TMP, E_r[0], E_r[1], AT_r):
                    r_.renew(fence())
                for A_ in (oH, oD):
                    for k in range(4):
                        A_.th[k] = A_.tl[k] = None
                nb = NB.pop()

                def g():
                    if l == 0:
                        NS.R_ready = False
                        yield [NS.t]
                        yield from make_R(1.0 / 1024.0, EPS_RMS)
                        yield from tables()
                    while not NS.R_ready or (l and len(NS.spill) < 8):
                        yield None
                    NB.put(nb, fence())
                    yield [NS.tR]
                    t1 = tt(RC[:, :], C_t[:, :], R[:, :], ALU.mult, NS.tR, NS.t_tab, fence(), q=PO)
                    t2 = tt(RS[:, :], S_t[:, :], R[:, :], ALU.mult, NS.tR, NS.t_tab, q=PO)
                    NS.tRC = [t1, t2]
                spawn(g())

            for h in range(4):
                st = hs[h]
                st.s = h % 2
                st.k, st.eg, st.G, st.E, st.off = [None] * 2, [None] * 2, [None] * 2, [None] * 2, [None] * 2
                st.passed_E, st.last_a, st.last_v, st.last_g = False, None, None, None
                st.q = st.v = st.bg = None
                st.prev2 = hs[h - 2] if h >= 2 else None

                def bef(h=h, st=st):
                    if h == 0:
                        start_layer()
                    st.free = fence()

                def ev_q(b, t, h=h, st=st):
                    spawn(hg_q(st, b[0], t), first)
                    spawn(hg_main(st, l, h, hs[h - 1] if h else None))

                in_job(l, 16 + h, lambda b, t, h=h, st=st: spawn(hg_gate(st, l, h, 0, b[0], t)), bef)
                in_job(l, 20 + h, lambda b, t, h=h, st=st: spawn(hg_gate(st, l, h, 1, b[0], t)))
                in_job(l, 24 + h, lambda b, t, st=st: spawn(hg_v(st, b[0], t)))
                in_job(l, 12 + h, ev_q)
                in_job(l, 28 + h, lambda b, t, st=st: spawn(hg_g(st, b[0], t)))

            def gates(i0, n):
                for i in range(i0, i0 + n):
                    def ev(b, t, i=i, i0=i0, n=n):
                        def g():
                            fr = hs[3].free
                            if i >= 4:
                                while hs[3].last_a is None:
                                    yield None
                                fr = hs[3].last_a
                            if i >= 10:
                                while hs[3].last_v is None:
                                    yield None
                                fr = hs[3].last_v
                            t1 = tt(gate[i][:, :], b[0].ap[:, :], R[:, :], ALU.mult, t, NS.tR, fr)
                            banks.put(b[0], t1)
                            gr[i] = t1
                            if i == i0 + n - 1:
                                yield [t1]
                                for m in range(i0, i0 + n):
                                    gt[m] = act(gate[m][:, :], gate[m][:, :], ACT.Sigmoid, gr[m])
                        spawn(g())
                    in_job(l, (32 if i % 2 == 0 else 40) + i // 2, ev)

            gt = [None] * 16
            gr = [None] * 16

            def da(h):
                st = ds[h]
                st.qk, st.v, st.qk_b, st.v_b = [None, None], None, None, None

                def ev(b, t, w=0):
                    def g():
                        if h == 0 and w == 0:
                            while hs[2].last_v is None:
                                yield None
                            for r_ in (QK_r, V_r, E4):
                                r_.renew([hs[2].last_v, hs[2].last_a])
                        if w == 2:
                            yield from da_v(st, b[0], t)
                        else:
                            yield from da_rope(st, w, b[0], t)

                    def start():
                        if h == 0:
                            while hs[3].last_v is None:
                                yield None
                            f = [hs[3].last_v, hs[3].last_a]
                            NS.oD_free = f
                            WT_r.renew(f)
                            Wr.renew(f)
                        yield from da_main(st, l, h)
                    spawn(g())
                    if w == 2:
                        spawn(start())
                for w in range(3):
                    in_job(l, 4 * w + h, lambda b, t, w=w, ev=ev: ev(b, t, w))

            gates(0, 4)
            da(0)
            gates(4, 2)
            da(1)
            gates(6, 2)
            da(2)
            gates(8, 2)
            da(3)
            gates(10, 3)
            gates(13, 3)

            mg = Acts([g[:, :] for g in gateR[0::2]], [g[:, :] for g in gateR[1::2]])
            for n in range(8):
                def ev(b, t, n=n):
                    def g():
                        x_ = yield from TMP.get()
                        y_ = yield from TMP.get()
                        while gt[2 * n] is None or gt[2 * n + 1] is None:
                            yield None
                        t1 = tt(x_.ap[:, :], b[0].ap[:, :], gate[2 * n][:, :], ALU.mult, t, gt[2 * n], x_.free)
                        banks.put(b[0], t1)
                        t2 = tt(y_.ap[:, :], b[1].ap[:, :], gate[2 * n + 1][:, :], ALU.mult, t, gt[2 * n + 1], y_.free)
                        banks.put(b[1], t2)
                        t1 = tt(x_.ap[:, :], x_.ap[:, :], y_.ap[:, :], ALU.add, t1, t2)
                        TMP.put(y_, t1)
                        yield [t1]
                        th = act(mg.hi[n], x_.ap[:, :], ACT.Copy, t1)
                        yield [th]
                        mg.tl[n] = tt(mg.lo[n], x_.ap[:, :], mg.hi[n].bitcast(FP), ALU.subtract, th)
                        mg.th[n] = th
                        TMP.put(x_, mg.tl[n])
                    spawn(g())

                job([(a["wab"][l, n], 1024,
                      [(4 + k, oH, k, 1, k == 0, k == 3) for k in range(4)]
                      + [(k, oD, k, 0, k == 0, k == 3) for k in range(4)])], 2, ev)

            src = a["xT"] if l == 0 else scr
            for n in range(8):
                def bef(n=n):
                    if n == 0:
                        until(lambda: len(NB.q) == 1)
                        for k in range(8):
                            xtok[k] = SP.dma(X[k][:, :], src[:, 512 * k:512 * k + 512], s_re[k], PE.last(),
                                             NS.oH_free())
                            H.th[k] = H.tl[k] = None
                        NS.hfree = PE.last()
                        NS.sfree = fence()

                def ev(b, t, n=n):
                    xtok[n] = tt(X[n][:, :], X[n][:, :], b[0].ap[:, :], ALU.add, t, xtok[n])
                    banks.put(b[0], xtok[n])
                    prep_x(n, "ffn_norm", 8 * l + n, xtok[n], NS.hfree, NS.sfree)
                job([(a["wo"][l, n], 1024, [(k, mg, k, 0, k == 0, k == 7) for k in range(8)])], 1, ev, bef)

        def ffn(gu, dn, acc, useR, before=None):
            for n in range(22):
                s_ = {}

                def ev_G(b, t, s=s_, n=n):
                    def g():
                        x_ = yield from FT.get()
                        if useR:
                            t1 = tt(x_.ap[:, :], b[0].ap[:, :], R[:, :], ALU.mult, t, NS.tR, x_.free)
                            banks.put(b[0], t1)
                            yield [t1]
                            s["t"] = act(x_.ap[:, :], x_.ap[:, :], ACT.Silu, t1)
                        else:
                            s["t"] = act(x_.ap[:, :], b[0].ap[:, :], ACT.Silu, t, x_.free)
                            banks.put(b[0], s["t"])
                        s["g"] = x_
                    spawn(g())

                def ev_U(b, t, s=s_, n=n):
                    def g():
                        y_ = yield from FT.get()
                        while "g" not in s:
                            yield None
                        x_ = s["g"]
                        if useR:
                            t1 = tt(y_.ap[:, :], b[0].ap[:, :], R[:, :], ALU.mult, t, NS.tR, y_.free)
                            banks.put(b[0], t1)
                            t1 = tt(y_.ap[:, :], y_.ap[:, :], x_.ap[:, :], ALU.mult, t1, s["t"])
                        else:
                            t1 = tt(y_.ap[:, :], b[0].ap[:, :], x_.ap[:, :], ALU.mult, t, s["t"], y_.free)
                            banks.put(b[0], t1)
                        FT.put(x_, t1)
                        yield [t1]
                        th = act(hid.hi[n], y_.ap[:, :], ACT.Copy, t1, NS.hidfree)
                        yield [th]
                        hid.tl[n] = tt(hid.lo[n], y_.ap[:, :], hid.hi[n].bitcast(FP), ALU.subtract, th, NS.hidfree)
                        hid.th[n] = th
                        FT.put(y_, hid.tl[n])
                    spawn(g())

                def bef(n=n):
                    if n == 0:
                        if before is not None:
                            before()
                        NS.hidfree = fence()
                        FT.renew(NS.hidfree)
                        for k in range(22):
                            hid.th[k] = hid.tl[k] = None
                job([(gu(n, 0), 1024, [(k, H, k, 0, k == 0, k == 7) for k in range(8)])], 1, ev_G, bef)
                job([(gu(n, 1), 1024, [(k, H, k, 0, k == 0, k == 7) for k in range(8)])], 1, ev_U)
            for n in range(8):
                w = dn(n)
                chs = []
                for c0, kn in ((0, 8), (8, 8), (16, 6)):
                    chs.append((w[:, 128 * c0:128 * (c0 + kn)], 128 * kn,
                                [(k, hid, c0 + k, 0, c0 + k == 0, c0 + k == 21) for k in range(kn)]))

                def bef(n=n):
                    if n == 0:
                        NS.hfree = PE.last()
                        for k in range(8):
                            H.th[k] = H.tl[k] = None
                        until(lambda: len(FT.q) == len(FT.all))
                        NS.sfree = fence()
                        NS.spill = []
                job(chs, 1, lambda b, t, n=n: acc(n, b[0], t), bef)

        def ffn_a(l):
            def acc(n, b, t):
                xtok[n] = tt(X[n][:, :], X[n][:, :], b.ap[:, :], ALU.add, t, xtok[n])
                banks.put(b, xtok[n])
                if l == 0:
                    prep_x(n, "attn_norm", 8 * (l + 1) + n, xtok[n], NS.hfree, NS.sfree)
                    NS.spill.append(SP.dma(scr[:, 512 * n:512 * n + 512], X[n][:, :], s_sp, xtok[n]))
                else:
                    prep_x(n, "final_norm", n, xtok[n], NS.hfree, NS.sfree)
            ffn(lambda n, u: a["wgu1"][l, 2 * n + u], lambda n: a["wd1"][l, n], acc, True)

        L_m0, L_s1, L_s2, L_sq, L_DR, L_DC, L_C = [big(92 + 2 * i, 512) for i in range(7)]
        LN = State()

        def ln_acc(n, b, t, scale):
            t = stt(X[n][:, :], X[n][:, :], scale, b.ap[:, :], ALU.mult, ALU.add, t, xtok[n])
            banks.put(b, t)
            xtok[n] = t

            def g(t=t):
                if n == 0:
                    LN.m0 = LN.s1 = LN.s2 = None
                    LN.n = 0
                    yield [t]
                    s_ = yield from bank()
                    t1 = mm(s_.ap[:, :], ones[:, :], X[0][:, :], True, True, t, s_.free, sig=True)
                    yield [t1]
                    LN.m0 = act(L_m0[:, :], s_.ap[:, :], ACT.Copy, t1, NS.sfree, scale=1.0 / 128.0)
                    banks.put(s_, LN.m0)
                while LN.n != n:
                    yield None
                yield [LN.m0]
                t = tt(X[n][:, :], X[n][:, :], L_m0[:, :], ALU.subtract, t, LN.m0)
                xtok[n] = t
                yield [t]
                if n == 0:
                    LN.s1 = PO.do(lambda e: e.tensor_copy(L_s1[:, :], X[0][:, :]), t, NS.sfree, cost=1830)
                    LN.s2 = act(L_s2[:, :], X[0][:, :], ACT.Square, t, NS.sfree)
                else:
                    LN.s1 = tt(L_s1[:, :], L_s1[:, :], X[n][:, :], ALU.add, t, LN.s1, q=PO)
                    t1 = act(L_sq[:, :], X[n][:, :], ACT.Square, t, LN.s2, NS.sfree)
                    yield [t1]
                    LN.s2 = tt(L_s2[:, :], L_s2[:, :], L_sq[:, :], ALU.add, t1, LN.s2, q=PO)
                LN.n += 1
            spawn(g(), first)

        def ln_finish(gn, bn, l, eps, final):
            while LN.n != 8:
                yield None
            yield [LN.s1, LN.s2]
            b = yield from bank()
            for i, (S_, ts_) in enumerate(((L_s1, LN.s1), (L_s2, LN.s2))):
                for j in range(4):
                    t = mm(b.ap[:, 4 * i + j:4 * i + j + 1], S_[:, 128 * j:128 * j + 128], ones[:, 0:1], True, True,
                           ts_, b.free, sig=(i == 1 and j == 3))
            sa = yield from st_ring.get()
            sb_ = yield from st_ring.get()
            md, v, r_, c_ = sa.ap[:, 0:4], sa.ap[:, 4:8], sb_.ap[:, 0:4], sb_.ap[:, 4:8]
            t1 = ts(md, b.ap[:, 0:4], 1.0 / 1024.0, None, ALU.mult, None, t, sa.free)
            t2 = ts(v, b.ap[:, 4:8], 1.0 / 1024.0, eps, ALU.mult, ALU.add, t)
            banks.put(b, t2)
            t1 = tt(c_, md, md, ALU.mult, t1, sb_.free)
            t2 = tt(v, v, c_, ALU.subtract, t1, t2)
            t = PO.do(lambda e: e.tensor_tensor(r_, v, pm05[:, 0:4], ALU.pow), t2, t_pm, cost=960)
            t = stt(c_, md, -1.0, r_, ALU.mult, ALU.mult, t)
            br = yield from bank()
            bc = yield from bank()
            tb = []
            for D_, s_, bb in ((L_DR, r_, br), (L_DC, c_, bc)):
                t1 = tt(D_[:, :].rearrange("p (j c) -> p j c", j=4), ident[:, None, :].broadcast_to([128, 4, 128]),
                        s_[:, :, None].broadcast_to([128, 4, 128]), ALU.mult, t, NS.sfree)
                tb.append(mm(bb.ap[:, :], ones[:, :], D_[:, :], True, True, t1, bb.free, sig=True))
            st_ring.put(sa, t1)
            st_ring.put(sb_, t1)
            tc = act(L_C[:, :], bc.ap[:, :], ACT.Copy, tb[1])
            banks.put(bc, tc)
            for k in range(9):
                if k < 8:
                    t = tt(X[k][:, :], X[k][:, :], br.ap[:, :], ALU.mult, tb[0], xtok[k], LN.s1, LN.s2)
                    if k == 7:
                        banks.put(br, t)
                    t = tt(X[k][:, :], X[k][:, :], L_C[:, :], ALU.add, t, tc, q=PO if k % 2 else DV)
                if k > 0 and not final:
                    H.tl[k - 1] = tt(H.lo[k - 1], X[k - 1][:, :], H.hi[k - 1].bitcast(FP), ALU.subtract, th, NS.hfree)
                    H.th[k - 1] = th
                if k < 8:
                    t = act(X[k][:, :], X[k][:, :], ACT.Identity, t, scale=col(gn, 8 * l + k), bias=col(bn, 8 * l + k))
                    xtok[k] = t
                    if not final:
                        th = act(H.hi[k], X[k][:, :], ACT.Copy, t, NS.hfree)

        def ffn_b(l, which):
            gu, dn = a[f"wgu{which + 1}"], a[f"wd{which + 1}"]
            nm = "ln1" if which == 1 else "ln3"
            begins = which == 1 and l == 0

            def acc(n, b, t):
                ln_acc(n, b, t, 2.0 * ALPHA)
                if n == 7:
                    spawn(ln_finish(nm + "_g", nm + "_b", l, 4.0 * EPS_LN, which == 2 and l == 1), first)

            def before():
                if not begins:
                    until(lambda: H.tl[0] is not None)
                    return

                def g():
                    while not NS.R_ready or H.tl[7] is None:
                        yield None
                    for k in range(8):
                        xtok[k] = stt(X[k][:, :], X[k][:, :], col("final_norm", k), R[:, :], ALU.mult, ALU.mult,
                                      xtok[k], NS.tR, H.th[k], H.tl[k])
                        yield [xtok[k]]
                spawn(g())
            ffn(lambda n, u: gu[l, 2 * n + u], lambda n: dn[l, n], acc, begins, before)

        MX = Acts([big(2 * i, 512, FR)[:, :] for i in range(8)], [big(16 + 2 * i, 512, FR)[:, :] for i in range(8)])
        q2 = [[big(32 + 4 * i + 2 * j, 512, FR) for j in range(2)] for i in range(4)]
        k2 = [big(48 + 2 * j, 512, FR) for j in range(2)]
        v2 = [big(52 + 2 * j, 512) for j in range(2)]
        e2 = Ring([Buf(big(56 + 1.5 * i, 384)) for i in range(4)])
        w2 = Ring([Buf(big(62 + 1.5 * i, 384)) for i in range(4)])
        p2 = Ring([Buf((big(68 + 3 * i, 384), big(69.5 + 3 * i, 384))) for i in range(2)])
        up = [big(74 + 2.25 * i, 542) for i in range(4)]
        cacc = [big(83 + 2 * i, 512) for i in range(2)]
        cpo = [big(87 + 2 * i, 512) for i in range(2)]
        cpr = Ring([Buf(big(91 + 2 * i, 512)) for i in range(2)])
        TM2 = Ring([Buf(big(95 + 2 * i, 512)) for i in range(4)])
        c_sq, c_D, c_mu = big(103, 512), big(105, 512), RC
        CN = Ring([Buf(RS)])
        C2, S2 = C_t, S_t
        s_tb = sem()

        def mixer_b(l):
            M = State()

            def before():
                until(lambda: H.tl[0] is not None)
                f = fence()
                M.f = f
                for r_ in (e2, w2, p2, cpr, TM2, CN):
                    r_.renew(f)
                tz = []
                for u, n in ((up[0], 15), (up[1], 15), (up[2], 1), (up[3], 1)):
                    for c0 in (0, 512 + n):
                        PO.do(lambda e, u=u, c0=c0, n=n: e.memset(u[:, c0:c0 + n], 0.0), f)
                for i in range(2):
                    M.tz = PO.do(lambda e, i=i: e.memset(v2[i][:, :], 0.0), f, cost=300)
                if l == 0:
                    SP.dma(C2[:, :], a["tab2"][:, 0:512], s_tb, f)
                    NS.ttab = SP.dma(S2[:, :], a["tab2"][:, 512:1024], s_tb, f)

            def rope2(b, tok, dst, out):
                z = yield from TM2.get()
                w = yield from TM2.get()
                t = act(z.ap[:, :], b.ap[:, :], ACT.Copy, tok, z.free)
                banks.put(b, t)
                yield [t]
                s_ = yield from bank()
                t1 = mm(s_.ap[:, :], perm2[:, :], z.ap[:, :], True, True, t, s_.free, t_c, sig=True)
                yield [t1]
                t2 = tt(w.ap[:, :], s_.ap[:, :], S2[:, :], ALU.mult, t1, NS.ttab, w.free)
                banks.put(s_, t2)
                t3 = tt(z.ap[:, :], z.ap[:, :], C2[:, :], ALU.mult, t1)
                t4 = tt(z.ap[:, :], z.ap[:, :], w.ap[:, :], ALU.add, t3, t2)
                TM2.put(w, t4)
                yield [t4]
                th = act(dst[0][:, :], z.ap[:, :], ACT.Copy, t4, M.f)
                yield [th]
                tl = tt(dst[1][:, :], z.ap[:, :], dst[0][:, :].bitcast(FP), ALU.subtract, th, M.f)
                TM2.put(z, tl)
                out[:] = [th, tl]

            def ev_k(b, t):
                M.k = []
                spawn(rope2(b[0], t, k2, M.k))

            def ev_v(b, t):
                def g():
                    z = yield from TM2.get()
                    t1 = act(z.ap[:, :], b[0].ap[:, :], ACT.Copy, t, z.free)
                    banks.put(b[0], t1)
                    yield [t1]
                    s_ = yield from bank()
                    for j in range(4):
                        t2 = tr(s_.ap[:, 128 * j:128 * j + 128], z.ap[:, 128 * j:128 * j + 128], t1, s_.free, sig=(j == 3))
                    TM2.put(z, t2)
                    yield [t2]
                    hv = lambda x_, i: x_[:, :].rearrange("p (j h c) -> p j h c", j=4, h=2)[:, :, i, :]
                    t0 = act(hv(v2[0], 0), hv(s_.ap, 0), ACT.Copy, t2, M.tz)
                    t1 = act(hv(v2[1], 1), hv(s_.ap, 1), ACT.Copy, t2, M.tz)
                    M.v = [t0, t1]
                    banks.put(s_, t1)
                spawn(g())

            M.q = [[] for _ in range(4)]

            def unit(p, qt):
                k0, k1 = max(qt - 1, 0), min(qt + 2, 4)
                nk = 128 * (k1 - k0)
                sm = yield from st_ring.get()
                mx, ng, su, r_ = (sm.ap[:, 2 * i:2 * i + 2] for i in range(4))
                qs = slice(128 * qt, 128 * qt + 128)
                ks = slice(128 * k0, 128 * k1)
                sk = sink[:, 8 * l:8 * l + 8].rearrange("p (c i) -> p c i", c=2)[:, :, p]
                bs, es = [], []
                for c in range(2):
                    pr_ = slice(64 * c, 64 * c + 64)
                    b = yield from bank()
                    o_ = b.ap[:, 0:nk]
                    mm(o_, q2[p][0][pr_, qs], k2[0][pr_, ks], True, False, M.q[p], M.k, b.free)
                    mm(o_, q2[p][0][pr_, qs], k2[1][pr_, ks], False, False)
                    if qt > 0:
                        mm(b.ap[:, 0:128], identb[:, :], wmask[:, 0:128], False, False, t_wm)
                    if qt < 3:
                        mm(b.ap[:, nk - 128:nk], identb[:, :], wmask[:, 128:256], False, False, t_wm)
                    t = mm(o_, q2[p][1][pr_, qs], k2[0][pr_, ks], False, True, sig=True)
                    bs.append((b, t))
                M.nsc += 1
                for c, (b, t) in enumerate(bs):
                    yield [t]
                    tm = reduce_max(mx[:, c:c + 1], b.ap[:, 0:nk], t, sm.free)
                t = ts(mx, mx, 0.125, None, ALU.mult, None, tm)
                t = tt(mx, mx, sk, ALU.max, t, t_p)
                tn = ts(ng, mx, -1.0, None, ALU.mult, None, t)
                tx = tt(mx, sk, mx, ALU.subtract, tn)
                yield [tn]
                for c, (b, t) in enumerate(bs):
                    e_ = yield from e2.get()
                    te = act(e_.ap[:, 0:nk], b.ap[:, 0:nk], ACT.Exp, tn, e_.free, bias=ng[:, c:c + 1], scale=0.125,
                             accum=su[:, c:c + 1])
                    banks.put(b, te)
                    es.append(e_)
                te = act(mx, mx, ACT.Exp, tx)
                yield [te]
                t = tt(su, su, mx, ALU.add, te)
                t = DV.do(lambda e: e.reciprocal(r_, su), t, cost=81)
                ws = []
                for c in range(2):
                    w_ = yield from w2.get()
                    tw = ts(w_.ap[:, 0:nk], es[c].ap[:, 0:nk], r_[:, c:c + 1], None, ALU.mult, None, t, w_.free)
                    e2.put(es[c], tw)
                    ws.append((w_, tw))
                st_ring.put(sm, tw)
                pt = yield from p2.get()
                tp = []
                for c in range(2):
                    yield [ws[c][1]]
                    b = yield from bank()
                    for j in range(k1 - k0):
                        s_ = slice(128 * j, 128 * j + 128)
                        t = tr(b.ap[:, s_], ws[c][0].ap[:, s_], ws[c][1], b.free, sig=(j == k1 - k0 - 1))
                    w2.put(ws[c][0], t)
                    yield [t]
                    if c == 0:
                        t = act(pt.ap[c][:, 0:nk], b.ap[:, 0:nk], ACT.Copy, t, pt.free)
                    else:
                        t = copy(pt.ap[1][:, 0:nk], b.ap[:, 0:nk], t, pt.free)
                    banks.put(b, t)
                    tp.append(t)
                yield tp + M.v
                b = yield from bank()
                n_ = 0
                for c in range(2):
                    for j in range(k1 - k0):
                        t = mm(b.ap[:, 0:128], v2[c][:, 128 * (k0 + j):128 * (k0 + j) + 128],
                               pt.ap[c][:, 128 * j:128 * j + 128], n_ == 0, n_ == 2 * (k1 - k0) - 1, tp, M.v, b.free,
                               sig=(n_ == 2 * (k1 - k0) - 1))
                        n_ += 1
                p2.put(pt, t)
                yield [t]
                th = act(MX.hi[2 + p][:, qs], b.ap[:, 0:128], ACT.Copy, t, M.f)
                yield [th]
                tl = tt(MX.lo[2 + p][:, qs], b.ap[:, 0:128], MX.hi[2 + p][:, qs].bitcast(FP), ALU.subtract, th, M.f)
                banks.put(b, tl)
                M.att[p] += [th, tl]
                if len(M.att[p]) == 8:
                    MX.th[2 + p] = MX.tl[2 + p] = M.att[p]

            def units():
                M.nsc = 0
                n = 0
                for p in range(4):
                    while not M.q[p] or M.v is None or not M.k:
                        yield None
                    yield M.q[p] + M.k
                    for qt in range(4):
                        spawn(unit(p, qt))
                        n += 1
                        while M.nsc < n:
                            yield None
            M.v = None
            M.att = [[] for _ in range(4)]

            def ev_q(b, t, p):
                spawn(rope2(b[0], t, q2[p], M.q[p]))
                if p == 0:
                    for k in range(8):
                        MX.th[k] = MX.tl[k] = None
                    spawn(units())

            def ev_sig(b, t, i):
                def g():
                    z = yield from TM2.get()
                    t1 = act(z.ap[:, :], b[0].ap[:, :], ACT.Sigmoid, t, z.free)
                    M.sg[i] = (z, t1)
                    banks.put(b[0], t1)
                spawn(g())

            def ev_a(b, t, i):
                def g():
                    while M.sg[i] is None:
                        yield None
                    z, tz = M.sg[i]
                    t1 = tt(up[i][:, 15:527], b[0].ap[:, :], z.ap[:, :], ALU.mult, t, tz, M.tz)
                    banks.put(b[0], t1)
                    TM2.put(z, t1)
                    yield from conv(i, t1)
                spawn(g())
            M.sg = [None] * 2
            M.cv = [None] * 2

            NPO = 12

            def conv(i, tu):
                cw = lambda k: col("cc_w", 62 * l + 2 * k + i)
                ta = ts(cacc[i][:, :], up[i][:, NPO:NPO + 512], cw(NPO), col("cc_b", 2 * l + i), ALU.mult, ALU.add, tu, M.f)
                tp = act(cpo[i][:, :], up[i][:, 0:512], ACT.Copy, tu, M.f, scale=cw(0))
                kp = 1
                for k in range(NPO + 1, 31):
                    yield [ta]
                    ta = stt(cacc[i][:, :], up[i][:, k:k + 512], cw(k), cacc[i][:, :], ALU.mult, ALU.add, ta)
                    if kp < NPO and cpr.q:
                        z = cpr.pop()
                        t = act(z.ap[:, :], up[i][:, kp:kp + 512], ACT.Copy, tu, z.free, scale=cw(kp))
                        tp = tt(cpo[i][:, :], cpo[i][:, :], z.ap[:, :], ALU.add, t, tp, q=PO)
                        cpr.put(z, tp)
                        kp += 1
                assert kp == NPO
                yield [ta, tp]
                ta = tt(cacc[i][:, :], cacc[i][:, :], cpo[i][:, :], ALU.add, ta, tp)
                M.cv[i] = ta
                if M.cv[1 - i] is not None:
                    yield from cc_norm()

            def cc_norm():
                yield M.cv
                b = yield from bank()
                for i in range(2):
                    t = mm(b.ap[:, :], ones[:, :], cacc[i][:, :], i == 0, i == 1, M.cv[i], b.free, sig=(i == 1))
                yield [t]
                t = act(c_mu[:, :], b.ap[:, :], ACT.Copy, t, M.f, scale=1.0 / 256.0)
                banks.put(b, t)
                yield [t]
                td = [tt(cacc[i][:, :], cacc[i][:, :], c_mu[:, :], ALU.subtract, t) for i in range(2)]
                yield td
                z = yield from TM2.get()
                t0 = act(c_sq[:, :], cacc[0][:, :], ACT.Square, td[0], M.f)
                t1 = act(z.ap[:, :], cacc[1][:, :], ACT.Square, td[1], z.free)
                yield [t1]
                tq = tt(c_sq[:, :], c_sq[:, :], z.ap[:, :], ALU.add, t0, t1)
                TM2.put(z, tq)
                o = {}
                yield from rstd(c_sq, tq, 1.0 / 256.0, EPS_LN, c_D, M.f, o)
                for i in range(2):
                    td[i] = tt(cacc[i][:, :], cacc[i][:, :], o["bank"].ap[:, :], ALU.mult, o["tok"], td[i])
                banks.put(o["bank"], td[1])
                yield td
                for i in range(2):
                    td[i] = act(cacc[i][:, :], cacc[i][:, :], ACT.Silu, td[i], scale=col("cc_g", 2 * l + i),
                                bias=col("cc_lb", 2 * l + i))
                for i in range(2):
                    th = act(MX.hi[6 + i], cacc[i][:, :], ACT.Copy, td[i], M.f)
                    yield [th]
                    MX.tl[6 + i] = tt(MX.lo[6 + i], cacc[i][:, :], MX.hi[6 + i].bitcast(FP), ALU.subtract, th, M.f)
                    MX.th[6 + i] = th

            M.sc = [None] * 2

            def ev_c(b, t, i):
                def g():
                    z = yield from CN.get()
                    t1 = act(z.ap[:, :], b[0].ap[:, :], ACT.Copy, t, z.free)
                    M.sc[i] = (z, t1)
                    banks.put(b[0], t1)
                spawn(g())

            def ev_h(b, t, i):
                def g():
                    while M.sc[i] is None:
                        yield None
                    z, tz = M.sc[i]
                    t1 = tt(up[2 + i][:, 1:513], b[0].ap[:, :], z.ap[:, :], ALU.mult, t, tz, M.tz)
                    banks.put(b[0], t1)
                    cw = lambda k: col("sc_w", 6 * l + 2 * k + i)
                    t2 = ts(z.ap[:, :], up[2 + i][:, 0:512], cw(0), None, ALU.mult, None, t1)
                    for k in (1, 2):
                        yield [t2]
                        t2 = stt(z.ap[:, :], up[2 + i][:, k:k + 512], cw(k), z.ap[:, :], ALU.mult, ALU.add, t2)
                    M.sd[i] = (z, t2)
                spawn(g())
            M.sd = [None] * 2

            def ev_b(b, t, i):
                def g():
                    while M.sd[i] is None:
                        yield None
                    z, tz = M.sd[i]
                    t1 = tt(z.ap[:, :], b[0].ap[:, :], z.ap[:, :], ALU.mult, t, tz)
                    banks.put(b[0], t1)
                    yield [t1]
                    th = act(MX.hi[i], z.ap[:, :], ACT.Copy, t1, M.f)
                    yield [th]
                    MX.tl[i] = tt(MX.lo[i], z.ap[:, :], MX.hi[i].bitcast(FP), ALU.subtract, th, M.f)
                    MX.th[i] = th
                    CN.put(z, MX.tl[i])
                spawn(g())

            evs = [(10, ev_k), (11, ev_v)]
            evs += [(6, lambda b, t: ev_q(b, t, 0))]
            evs += [(14 + i, lambda b, t, i=i: ev_sig(b, t, i)) if j == 0 else (12 + i, lambda b, t, i=i: ev_a(b, t, i))
                    for i in range(2) for j in range(2)]
            evs += [(6 + i, lambda b, t, i=i: ev_q(b, t, i)) for i in range(1, 4)]
            for i in range(2):
                evs += [(2 + i, lambda b, t, i=i: ev_c(b, t, i)), (4 + i, lambda b, t, i=i: ev_h(b, t, i)),
                        (i, lambda b, t, i=i: ev_b(b, t, i))]
            for n, (tile, ev) in enumerate(evs):
                job([(a["win2"][l, tile], 1024, [(k, H, k, 0, k == 0, k == 7) for k in range(8)])], 1, ev,
                    before if n == 0 else None)
            order = [0, 1, 6, 7, 2, 3, 4, 5]
            for n in range(8):
                def bef(n=n):
                    if n == 0:
                        NS.hfree = PE.last()
                        for k in range(8):
                            H.th[k] = H.tl[k] = None
                        until(lambda: len(TM2.q) == len(TM2.all) and MX.tl[6] is not None and MX.tl[7] is not None)
                        NS.sfree = fence()

                def ev(b, t, n=n):
                    ln_acc(n, b[0], t, ALPHA)
                    if n == 7:
                        spawn(ln_finish("ln2_g", "ln2_b", l, EPS_LN, False), first)
                job([(a["wout2"][l, n], 1024, [(k, MX, k, 0, k == order[0], k == order[-1]) for k in order])], 1, ev, bef)

        stages = [("mix0", lambda: first_block(0)), ("ffn0", lambda: ffn_a(0)), ("mix1", lambda: first_block(1)),
                  ("ffn1", lambda: ffn_a(1)),
                  ("b0ln1", lambda: ffn_b(0, 1)), ("b0ln2", lambda: mixer_b(0)), ("b0ln3", lambda: ffn_b(0, 2)),
                  ("b1ln1", lambda: ffn_b(1, 1)), ("b1ln2", lambda: mixer_b(1)), ("b1ln3", lambda: ffn_b(1, 2))]
        for name, f in stages:
            f()
            if name == stop:
                break
        for i in range(NR):
            load(i)
        spawn(prep(0), first)
        spawn(prep(1), first)
        run_jobs()
        settle()
        s_o = sem()
        for k in range(8):
            t_o = SP.dma(a["out"][:, 512 * k:512 * k + 512], X[k][:, :], s_o, xtok[k])

        block = ctx.enter_context(nc.Block())

        @block.sync
        def _(e):
            SP.emit(e)
            e.wait_ge(t_o[0].h, t_o[1])

        @block.scalar
        def _(e):
            AC.emit(e)

        @block.vector
        def _(e):
            DV.emit(e)

        @block.gpsimd
        def _(e):
            PO.emit(e)

        @block.tensor
        def _(e):
            PE.emit(e)
    return P


SCRATCH = 8192
BASE = (SCRATCH + 97 + 31) // 32 * 32
LIMIT = 229344


def host(inputs):
    f = lambda n: np.asarray(inputs[n])
    col = lambda v: np.ascontiguousarray(v.reshape(-1, 128).T)
    parts = [f("attn_norm"), f("ffn_norm"), f("final_norm"), f("da_norm"), f("hg_norm"), f("hg_lb_logits"),
             f("ln1_g_2"), f("ln1_b_2"), f("ln2_g_2"), f("ln2_b_2"), f("ln3_g_2"), f("ln3_b_2"),
             f("sc_conv_w_2"), f("cc_conv_w_2"), f("cc_conv_b_2"), f("cc_ln_g_2"), f("cc_ln_b_2")]
    cols = [col(p) for p in parts]
    invf = (500000.0 ** (-(np.arange(0, 16, 2, dtype=np.float32) / np.float32(16)))).astype(np.float32)
    iv = np.zeros((128, 1), np.float32)
    for c in range(2):
        for j in range(16):
            iv[64 * c + j, 0] = invf[j % 8]
    prm = np.concatenate(cols + [iv], axis=1)
    assert prm.shape[1] == NPRM, (prm.shape, NPRM)
    perm = np.zeros((128, 128), np.float32)
    for c in range(2):
        for j in range(8):
            perm[64 * c + j, 64 * c + j + 8] = -1.0
            perm[64 * c + j + 8, 64 * c + j] = 1.0
    perm2 = np.zeros((128, 128), np.float32)
    for c in range(2):
        for j in range(32):
            perm2[64 * c + j, 64 * c + j + 32] = -1.0
            perm2[64 * c + j + 32, 64 * c + j] = 1.0
    cst = np.concatenate([np.eye(128, dtype=np.float32), np.ones((128, 128), np.float32), perm.T, perm2.T], axis=1)
    j = np.arange(128)[:, None]
    t = np.arange(128)[None, :]

    def lev(n, fwd):
        b0 = (t // n) * n
        mid = b0 + n // 2 - 1
        left = t <= mid
        if fwd:
            m = np.where(left, (j > t) & (j <= mid), (j > mid) & (j <= t))
        else:
            m = np.where(left, (j >= t) & (j <= mid), (j > mid) & (j < t))
        return m.astype(np.float32)
    Mf = [lev(128, 1), lev(64, 1), (j > t), (j <= t)] + [lev(n, 1) for n in (32, 16, 8, 4)]
    Mb = [lev(128, 0), lev(64, 0), (j < t), (j >= t)] + [lev(n, 0) for n in (32, 16, 8, 4)]
    mcst = np.concatenate([np.asarray(m, np.float32) for m in Mf + Mb], axis=1)
    ms = []
    for n in (64, 32, 16, 8, 4, 2):
        ms.append((j // n == t // n) & ((j % n < n // 2) != (t % n < n // 2)))
    ms.append(j == t)
    msk = np.concatenate(ms, axis=1).astype(np.float32)
    c8 = lambda w: np.ascontiguousarray(w.reshape(2, 8, 128, -1, 128).transpose(0, 3, 2, 1, 4)).reshape(2, -1, 128, 1024)
    c4 = lambda w: w.reshape(2, 4, 128, 8, 128).transpose(0, 3, 2, 1, 4)
    gu = lambda g, u: np.ascontiguousarray(np.stack([c8(g), c8(u)], axis=2)).reshape(2, 44, 128, 1024)
    dn = lambda w: np.ascontiguousarray(w.reshape(2, 22, 128, 8, 128).transpose(0, 3, 2, 1, 4)).reshape(2, 8, 128, 2816)
    hq = np.concatenate([np.concatenate([np.arange(64 * i, 64 * i + 64), np.arange(64 * (i + 4), 64 * (i + 4) + 64)])
                         for i in range(4)])
    cols_ = np.arange(2048)
    cols_[768:1280] = 768 + hq
    rows_ = np.arange(1024)
    rows_[256:768] = 256 + hq
    win2 = f("w_in_2")[:, :, cols_]
    wout2 = f("w_out_2")[:, rows_, :]
    inv2 = (10000.0 ** (-np.arange(32, dtype=np.float32) / np.float32(32))).astype(np.float32)
    ang = np.arange(512, dtype=np.float32)[None, :] * inv2[np.arange(128) % 32][:, None]
    tab2 = np.concatenate([np.cos(ang.astype(np.float64)), np.sin(ang.astype(np.float64))], axis=1).astype(np.float32)
    wm = np.concatenate([np.where(t < j, -1e30, 0.0), np.where(t > j, -1e30, 0.0), np.zeros((128, 128))],
                        axis=1).astype(np.float32)
    gu2 = lambda w: gu(w[:, :, :2816], w[:, :, 2816:])
    x = f("x")[0]
    arr = {
        "xT": np.ascontiguousarray(x.T.reshape(8, 128, 512).transpose(1, 0, 2)).reshape(128, 4096),
        "pos": np.ascontiguousarray(f("positions")).astype(np.int32, copy=False),
        "prm": np.ascontiguousarray(prm),
        "lam": np.ascontiguousarray(f("da_lambda").reshape(1, 512)),
        "cst": np.ascontiguousarray(cst), "mcst": np.ascontiguousarray(mcst), "msk": np.ascontiguousarray(msk),
        "win1": c8(f("w_in")),
        "wab": np.ascontiguousarray(np.concatenate([c4(f("w_a")), c4(f("w_b"))], axis=3)).reshape(2, 8, 128, 1024),
        "wo": c8(f("w_o")), "wgu1": gu(f("w_gate"), f("w_up")), "wd1": dn(f("w_down")),
        "sink": np.ascontiguousarray(f("attn_sink_2").reshape(1, 16)), "wmask": wm, "tab2": tab2,
        "wgu2": gu2(f("ffn1_w_gu_2")), "wd2": dn(f("ffn1_w_down_2")),
        "wgu3": gu2(f("ffn2_w_gu_2")), "wd3": dn(f("ffn2_w_down_2")),
        "win2": c8(win2), "wout2": c8(wout2),
    }
    return arr


def kernel(**inputs):
    import concourse.bacc as bacc
    from concourse.bass_utils import run_bass_kernel_spmd as run
    nc = bacc.Bacc("TRN2", target_bir_lowering=False, num_devices=1, dynamic_dma_scratch_size=SCRATCH)
    arr = host(inputs)
    aps = {n: nc.dram_tensor(n, v.shape, mybir.dt.from_np(v.dtype), kind="ExternalInput").ap() for n, v in arr.items()}
    aps["out"] = nc.dram_tensor("out", (128, 4096), FP, kind="ExternalOutput").ap()
    aps["scr"] = nc.dram_tensor("scr", (128, 4096), FP).ap()
    build_program(nc, aps)
    r = run(nc, [arr], core_ids=[0])
    o = r.results[0]["out"]
    return np.ascontiguousarray(o.reshape(128, 8, 512).transpose(1, 0, 2).reshape(1024, 512).T).reshape(1, 512, 1024)
```

```python
import math
from contextlib import ExitStack
import numpy as np
import concourse.bass as bass
from concourse import mybir

FP = mybir.dt.float32
FR = mybir.dt.float32r
BF = mybir.dt.bfloat16
U8 = mybir.dt.uint8
I32 = mybir.dt.int32
ALU = mybir.AluOpType
ACT = mybir.ActivationFunctionType
AX = mybir.AxisListType

T = 512
NFIX = 4
DEPTH = 2
HOLD = 3
LN_PRE = ()
LN_ADD = (6, 7)
NPO = 20
FIN_ADD = (1, 3, 5)
FIN_MUL = (2, 5)
FIN_TS = (1, 4, 6)
LN_DV = ((6, 7), (7,))
LN_DV2 = ((1, 2, 3, 4, 5, 7), (7,))
POOL_LO = (0, 1, 2, 3, 4)
POOL_MX = range(2, 12, 2)
EPS_RMS = 1e-6
EPS_LN = 1e-5
ALPHA = (2.0 * DEPTH) ** 0.25
BIG = 1e30

PCOL = {}
_n = 0
for _name, _k in (("attn_norm", 16), ("ffn_norm", 16), ("final_norm", 8), ("da_norm", 8), ("hg_norm", 8),
                  ("lb", 16), ("ln1", 32), ("ln2", 32), ("ln3", 32), ("sc_w", 12), ("cc_w", 124), ("cc_b", 4), ("cc_g", 4), ("cc_lb", 4),
                  ("invf", 1), ("rsgn", 1)):
    PCOL[_name] = _n
    _n += _k
NPRM = _n

ACT_SET = {ACT.Exp: "natural_log_exp_and_others", ACT.Ln: "natural_log_exp_and_others",
           ACT.Sigmoid: "sigmoid_and_others", ACT.Silu: "silu_and_others", ACT.Sin: "silu_and_others"}


class Sem:
    def __init__(self, h):
        self.h = h
        self.n = 0
        self.t = {0: 0.0}


def flat(after):
    out, stack = [], list(after)
    while stack:
        a = stack.pop()
        if a is None:
            continue
        if isinstance(a, list):
            stack.extend(a)
        else:
            out.append(a)
    return out


def when(after):
    return max([s.t[v] for s, v in flat([after])], default=0.0)


class Queue:

    def __init__(self, sem, lat=60.0):
        self.sem = sem
        self.ops = []
        self.seen = {}
        self.clock = 0.0
        self.lat = lat

    def do(self, fn, *after, sig=True, cost=70.0):
        waits = {}
        for s, v in flat(after):
            self.clock = max(self.clock, s.t[v])
            if self.seen.get(s, 0) < v:
                self.seen[s] = v
                waits[s] = v
        self.clock += cost
        self.ops.append((list(waits.items()), fn, self.sem if sig else None, 1))
        if sig:
            self.sem.n += 1
            self.sem.t[self.sem.n] = self.clock + self.lat
            return (self.sem, self.sem.n)
        return None

    def dma(self, out, in_, sem, *after):
        n = 1
        for d in out.shape:
            n *= d
        self.do(lambda e: e.dma_start(out, in_), *after, sig=False, cost=n * 4 / 350.0)
        w, fn, _, _ = self.ops[-1]
        self.ops[-1] = (w, fn, sem, 16)
        sem.n += 16
        sem.t[sem.n] = self.clock + 2000.0
        return (sem, sem.n)

    def last(self):
        return (self.sem, self.sem.n)

    def emit(self, e):
        for waits, fn, sem, inc in self.ops:
            for s, v in waits:
                e.wait_ge(s.h, v)
            ins = fn(e)
            if sem is not None:
                ins.then_inc(sem.h, inc)


class Buf:
    def __init__(self, ap, free=None):
        self.ap = ap
        self.free = free if free is not None else []


class Ring:

    def __init__(self, bufs):
        self.all = list(bufs)
        self.q = list(bufs)

    def pop(self):
        b = min(self.q, key=lambda b: when(b.free))
        self.q.remove(b)
        return b

    def get(self):
        while not self.q:
            yield None
        return self.pop()

    def get2(self):
        while len(self.q) < 2:
            yield None
        return self.pop(), self.pop()

    def put(self, buf, *toks):
        buf.free = list(toks)
        self.q.append(buf)

    def renew(self, toks):
        assert len(self.q) == len(self.all), "a buffer is still out"
        for b in self.q:
            b.free = list(toks)


class Acts:

    def __init__(self, hi, lo):
        self.hi, self.lo = hi, lo
        self.th = [None] * len(hi)
        self.tl = [None] * len(lo)
        self.reset()

    def reset(self):
        for k in range(len(self.hi)):
            self.th[k] = self.tl[k] = None
        self.rd = [None] * len(self.hi)
        self.nrd = [0] * len(self.hi)


class Prog:
    pass


def build_program(nc, a, stop=None):
    ctx = ExitStack()
    with ctx:
        P = Prog()
        nsem = [0]

        def sem():
            nsem[0] += 1
            return Sem(ctx.enter_context(nc.semaphore(f"s{nsem[0]}")))

        PE, AC, DV, PO = Queue(sem(), 200.0), Queue(sem()), Queue(sem()), Queue(sem())
        SP = Queue(sem())
        base = BASE
        names = [0]

        def at(off, cols, dt=FP, name=None):
            names[0] += 1
            t = nc.alloc_sbuf_tensor_at(f"{name or 'm'}_{names[0]}", [128, cols], dt, offset=base + off)
            return t

        KB = 1024
        off = [0]

        def take(nbytes):
            o = off[0]
            off[0] += (nbytes + 31) // 32 * 32
            assert off[0] <= LIMIT - base, (off[0], LIMIT - base)
            return o

        def here(cols, dt=FP, size=4, name=None):
            return at(take(cols * size), cols, dt, name)

        prm = here(NPRM, name="prm")
        cst = here(256, name="cst")
        ident, ones = cst[:, 0:128], cst[:, 128:256]
        identb = here(128, BF, 2, name="identb")
        wmask = here(256, BF, 2, name="wmask")
        sink = here(16, name="sink")
        nsink = here(16, name="nsink")
        M_off = take(8 * 1024)
        R = here(512, name="R")
        msk = here(7 * 128, U8, 1, name="msk")
        lbt = here(40, name="lbt")
        nlam = here(8, name="nlam")
        small = here(64, name="small")
        fxt = here(12 * NFIX, name="fxt")
        here8 = [here(8, FR) for _ in range(2)]
        rows = here(128, FR, name="rows")
        tabs = [here(512, name=f"tab{i}") for i in range(4)]
        C_t, S_t, RC, RS = tabs
        selr = here(512, FR, name="selr")
        NR = 3
        raw = [here(1024, name="raw") for _ in range(NR)]
        whi = [here(1024, FR, name="whi") for _ in range(NR)]
        wlo = [here(1024, FR, name="wlo") for _ in range(NR)]
        X_off = take(16 * KB)
        X = [at(X_off + 2 * KB * k, 512, name="X") for k in range(8)]
        Hh = [here(512, FR, name="Hh") for _ in range(8)]
        Hl = [here(512, FR, name="Hl") for _ in range(8)]
        B0 = off[0]
        BIGSZ = LIMIT - base - B0
        P.bigsz = BIGSZ

        def big(kb, cols, dt=FP, size=4, name=None):
            o = int(kb * KB)
            assert o + cols * size <= BIGSZ, (name, kb, BIGSZ / KB)
            return at(B0 + o, cols, dt, name)

        ps = [ctx.enter_context(nc.psum_tensor(f"ps{i}", [128, 512], FP)) for i in range(8)]
        banks = Ring([Buf(ps[i]) for i in range(8)])

        def bank():
            while len(banks.q) < NS.reserve:
                yield None
            b = banks.pop()
            if when(b.free) > PE.clock:
                yield b.free
            return b

        def fence():
            return [PE.last(), AC.last(), DV.last(), PO.last()]

        cur_set = [None]

        def cols_of(ap):
            n = 1
            for d in ap.shape[1:]:
                n *= d
            return n

        def in_psum(*aps):
            return any(x.tensor.name[:2] == "ps" for x in aps)

        def act(out, in_, func, *after, bias=0.0, scale=1.0, accum=None):
            want = ACT_SET.get(func)
            n = cols_of(out)
            cost = 0.834 * n + (52 if in_psum(in_) else 93) + (93 if accum is not None else 0)
            if not isinstance(bias, float) or not isinstance(scale, float):
                cost += 93
            if want is not None and cur_set[0] != want:
                cur_set[0] = want
                AC.do(lambda e: e.preload_act_table_set(want), sig=False, cost=1283)
            if accum is None:
                return AC.do(lambda e: e.activation(out, in_, func, bias=bias, scale=scale), *after, cost=cost)
            return AC.do(lambda e: e.activation(out, in_, func, bias=bias, scale=scale, accum_out=accum), *after,
                         cost=cost)

        def tt(out, x, y, op, *after, q=None):
            n = cols_of(out)
            return (q or DV).do(lambda e: e.tensor_tensor(out, x, y, op), *after,
                                cost=68 + n * (2.26 if q is PO else 1.042))

        def ts(out, x, s1, s2, o1, o2, *after, q=None):
            n = cols_of(out)
            cost = 68 + n * (1.18 if q is PO else 1.042 if in_psum(x) else 0.521)
            if s2 is None:
                return (q or DV).do(lambda e: e.tensor_scalar(out, x, s1, None, o1), *after, cost=cost)
            return (q or DV).do(lambda e: e.tensor_scalar(out, x, s1, s2, o1, o2), *after, cost=cost)

        def stt(out, x, s, y, o1, o2, *after):
            n = cols_of(out)
            return DV.do(lambda e: e.scalar_tensor_tensor(out=out, in0=x, scalar=s, in1=y, op0=o1, op1=o2), *after,
                         cost=68 + 1.16 * n)

        def copy(out, x, *after):
            return DV.do(lambda e: e.tensor_copy(out, x), *after,
                         cost=68 + cols_of(out) * (1.042 if in_psum(x) else 0.521))

        def swap(out, x, n, *after):
            mask = [(i + n) % (2 * n) if i < 2 * n else i for i in range(32)]
            return DV.do(lambda e: e.stream_shuffle(out, x, mask), *after, cost=68 + 1.042 * cols_of(out))

        def reduce_max(out, x, *after):
            return DV.do(lambda e: e.tensor_reduce(out, x, AX.X, ALU.max), *after, cost=68 + 1.042 * cols_of(x))

        def mm(out, l, r, start, stop, *after, sig=False):
            n = cols_of(out)
            if l.dtype == FP:
                cost = max(4 * 0.4167 * n + 4, 213)
            elif l.dtype == FR:
                cost = 0.4167 * n + 3 if n >= 256 else 216
            else:
                cost = 0.4167 * n + 3
            return PE.do(lambda e: e.matmul(out, l, r, start=start, stop=stop), *after, sig=sig, cost=cost)

        def tr(out, x, *after, sig=False):
            return PE.do(lambda e: e.transpose(out, x, ident), *after, sig=sig, cost=110)

        def mm3(out, Lh, Ll, Rh, Rl, start, stop, *after, sig=False):
            mm(out, Lh, Rh, start, False, *after)
            mm(out, Lh, Rl, False, False)
            return mm(out, Ll, Rh, False, stop, sig=sig)

        V4 = lambda t: t[:, :].rearrange("p (j c) -> p j c", j=4)

        class State:
            pass
        NS = State()
        NS.R_ready = False
        NS.ready = False
        NS.reserve = 3

        chunks = []
        s_raw = [sem() for _ in range(NR)]
        raw_free = [[] for _ in range(NR)]
        raw_tok = {}
        hi_tok, lo_tok, done = {}, {}, {}
        on_pool = set()

        def load(c):
            if c >= len(chunks):
                return
            w, n = chunks[c]
            s = c % NR
            raw_tok[c] = SP.dma(raw[s][:, 0:n], w, s_raw[s], raw_free[s])

        def prep(c):
            w, n = chunks[c]
            s = c % NR
            while c not in raw_tok:
                yield None
            yield [raw_tok[c], done.get(c - NR)]
            hi_tok[c] = act(whi[s][:, 0:n], raw[s][:, 0:n], ACT.Copy, raw_tok[c], done.get(c - NR))
            yield [hi_tok[c]]
            lo_tok[c] = tt(wlo[s][:, 0:n], raw[s][:, 0:n], whi[s][:, 0:n].bitcast(FP), ALU.subtract,
                           raw_tok[c], hi_tok[c], done.get(c - NR), q=PO if c in on_pool else DV)
            raw_free[s] = [hi_tok[c], lo_tok[c]]
            load(c + NR)

        first, side = [], []

        def run(lst, ent):
            try:
                ent[1] = next(ent[0])
            except StopIteration:
                lst.remove(ent)

        def pump(limit=0.0):
            n = 0
            for lst in (first, side):
                todo = sorted(((when(e[1]) if e[1] is not None else 0.0, i) for i, e in enumerate(lst)))
                ents = [(w, lst[i]) for w, i in todo]
                for w, ent in ents:
                    if w > max(limit, PE.clock):
                        break
                    timed = ent[1] is not None
                    run(lst, ent)
                    n += timed
            return n

        def spawn(g, lst=None):
            lst = side if lst is None else lst
            lst.append([g, None])
            return lst[-1]

        def advance():
            if pump():
                return
            ents = [(when(e[1]), i, lst, e) for i, (lst, e) in
                    enumerate([(first, e) for e in first] + [(side, e) for e in side]) if e[1] is not None]
            if not ents:
                NS.stuck += 1
                assert NS.stuck < 50, "no work can go on"
                return
            NS.stuck = 0
            _, _, lst, ent = min(ents, key=lambda v: v[:2])
            run(lst, ent)

        def until(cond):
            while not cond():
                advance()

        def settle():
            until(lambda: not side and not first)

        NS.stuck = 0
        NS.evacs = 0
        NS.evaced = 0

        jobs = []

        def job(chs, nb, evac, before=None):
            ids = []
            for w, n, segs in chs:
                ids.append(len(chunks))
                chunks.append((w, n))
            jobs.append((ids, [c[2] for c in chs], nb, evac, before))

        def evac_gen(f, bks, tok, no):
            while NS.evaced != no:
                yield None
            yield [tok]
            while not NS.R_ready:
                yield None
            f(bks, tok)
            NS.evaced += 1

        def run_jobs():
            for ids, segs, nb, evac, before in jobs:
                if before is not None:
                    before()
                bks = None
                for c, sg in zip(ids, segs):
                    if c + 2 < len(chunks):
                        spawn(prep(c + 2), first)
                    s = c % NR
                    for i, (k, A, kt, b, st, sp) in enumerate(sg):
                        until(lambda: c in lo_tok and A.tl[kt] is not None and A.th[kt] is not None)
                        if bks is None:
                            until(lambda: len(banks.q) >= nb)
                            bks = [banks.pop() for _ in range(nb)]
                            bfree = [x.free for x in bks]
                        free = bfree[b] if st else None
                        need = when([hi_tok[c], A.th[kt], free])
                        pump()
                        while PE.clock + 30 < need and pump(need):
                            pass
                        out = bks[b].ap[:, :]
                        wh = whi[s][:, 128 * k:128 * k + 128]
                        wl = wlo[s][:, 128 * k:128 * k + 128]
                        mm(out, wh, A.hi[kt], st, False, hi_tok[c], A.th[kt], free)
                        mm(out, wh, A.lo[kt], False, False, A.tl[kt])
                        done[c] = mm(out, wl, A.hi[kt], False, sp, lo_tok[c], sig=True)
                        A.rd[kt] = done[c]
                        A.nrd[kt] += 1
                tok = done[ids[-1]]
                spawn(evac_gen(evac, bks, tok, NS.evacs), first)
                NS.evacs += 1

        s_sl = sem()
        s_c, s_x, s_p, s_q = sem(), [sem() for _ in range(8)], sem(), sem()
        mst = big(20, 896, name="mst")
        selst = big(106, 512, name="selst")
        posi = big(8, 512, I32, name="posi")
        lamv = big(10, 512, name="lamv")
        wst = big(18, 384, name="wst")
        t_c = SP.dma(prm[:, :], a["prm"], s_c)
        t_c = SP.dma(cst[:, :], a["cst"], s_c)

        def early_loads():
            load(0)
            for k in range(8):
                SP.dma(X[k][:, :], a["xT"][:, 512 * k:512 * k + 512], s_x[k])
                if k == 3:
                    load(1)
            load(2)
            NS.t_sl = SP.dma(selst[0:8, :], a["sel"], s_sl)
            NS.t_q = SP.dma(posi[:, :], a["pos"].broadcast_to([128, 512]), s_p)
            NS.t_q = SP.dma(lamv[:, :], a["lam"].broadcast_to([128, 512]), s_p)
            NS.t_q = SP.dma(sink[:, :], a["sink"].broadcast_to([128, 16]), s_p)
            NS.t_q = SP.dma(wst[:, :], a["wmask"], s_p)
            NS.t_q = SP.dma(mst[:, :], a["msk"], s_p)

        def col(name, i, n=1):
            return prm[:, PCOL[name] + i:PCOL[name] + i + n]

        def setup():
            yield [t_c]
            NS.t_wm = [act(identb[:, :], ident, ACT.Copy, t_c)]
            yield [NS.t_sl]
            NS.t_sel = act(selr[0:8, :], selst[0:8, :], ACT.Copy, NS.t_sl)
            lbraw = prm[:, PCOL["lb"]:PCOL["lb"] + 16].rearrange("p (d l h) -> p d l h", d=2, l=2)
            sc8 = lambda i: lbt[:, 8 * i:8 * i + 8].rearrange("p (d h) -> p d h", d=2)
            w0, w1, w2 = [sc8(i) for i in range(3)]
            t = tt(w0, lbraw[:, :, 0, :], lbraw[:, :, 1, :], ALU.max, t_c)
            t0 = tt(w1, lbraw[:, :, 0, :], w0, ALU.subtract, t)
            t1 = tt(w2, lbraw[:, :, 1, :], w0, ALU.subtract, t0)
            yield [t1]
            t0 = act(w1, w1, ACT.Exp, t1)
            t1 = act(w2, w2, ACT.Exp, t1)
            yield [t1]
            t = tt(w0, w1, w2, ALU.add, t1)
            t = DV.do(lambda e: e.reciprocal(lbt[:, 0:8], lbt[:, 0:8]), t)
            t0 = tt(w1, w1, w0, ALU.mult, t)
            t1 = tt(w2, w2, w0, ALU.mult, t0)
            t = tt(w0, w1, w2, ALU.add, t1)
            t = tt(w0, w0, w1, ALU.subtract, t)
            NS.t_lb = ts(w1, w0, -1.0, 1.0, ALU.mult, ALU.add, t)
            yield [NS.t_q]
            lam4 = lamv[:, :].rearrange("p (l r e) -> p l r e", l=2, r=4)
            prod = big(12, 256, name="prod")
            pr4 = prod[:, :].rearrange("p (l r e) -> p l r e", l=2, r=2)
            t0 = tt(pr4[:, :, 0, :], lam4[:, :, 0, :], lam4[:, :, 1, :], ALU.mult, NS.t_q)
            t = tt(pr4[:, :, 1, :], lam4[:, :, 2, :], lam4[:, :, 3, :], ALU.mult, NS.t_q)
            t = DV.do(lambda e: e.tensor_reduce(small[:, 0:4], prod[:, :].rearrange("p (a e) -> p a e", a=4),
                                                AX.X, ALU.add), t0, t, cost=335)
            yield [t]
            t = act(small[:, 0:4], small[:, 0:4], ACT.Exp, t)
            yield [t]
            for l in range(2):
                li = 0.8 - 0.6 * math.exp(-0.3 * l)
                t0 = tt(nlam[:, l:l + 1], small[:, 2 * l + 1:2 * l + 2], small[:, 2 * l:2 * l + 1], ALU.subtract, t)
                t_l = ts(nlam[:, l:l + 1], nlam[:, l:l + 1], -li, None, ALU.add, None, t0)
                c0 = PCOL["da_norm"] + 4 * l
                t_l = ts(prm[:, c0:c0 + 4], prm[:, c0:c0 + 4], 1.0 - li, None, ALU.mult, None, t_l, t_c)
            NS.t_lam = t_l
            NS.t_wm.append(act(wmask[:, :], wst[:, 0:256], ACT.Copy, NS.t_q))
            NS.t_ns = ts(nsink[:, :], sink[:, :], -1.0, None, ALU.mult, None, NS.t_q)
            NS.t_msk = copy(msk[:, :], mst[:, :], NS.t_q)
            NS.ready = True

        def tables():
            ang, n1, m1, m2 = [big(k, 512, name="rt") for k in (92, 94, 96, 98)]
            MAGIC = 12582912.0
            t = DV.do(lambda e: e.tensor_copy(ang[:, :], posi[:, :]), NS.t_q, fence())
            t = ts(ang[:, :], ang[:, :], col("invf", 0), None, ALU.mult, None, t, t_c)
            two_pi = 2.0 * math.pi
            c1 = 201.0 / 32.0
            r1 = two_pi - c1

            def top(v, bits):
                m, e = math.frexp(v)
                return math.ldexp(math.floor(m * 2 ** bits), e - bits)
            c2 = top(r1, 8)
            c3 = top(r1 - c2, 8)
            c4 = r1 - c2 - c3
            K = 65536.0
            d2 = top(r1 * K, 11)
            d3 = r1 * K - d2
            yield [t]
            t = ts(n1[:, :], ang[:, :], 1.0 / (two_pi * K), MAGIC, ALU.mult, ALU.add, t)
            t = ts(n1[:, :], n1[:, :], MAGIC, None, ALU.subtract, None, t)
            for cc in (c1 * K, d2):
                t = stt(ang[:, :], n1[:, :], -cc, ang[:, :], ALU.mult, ALU.add, t)
            yield [t]
            for rnd in range(2):
                t = ts(m1[:, :], ang[:, :], 1.0 / two_pi, MAGIC, ALU.mult, ALU.add, t)
                t = ts(m1[:, :], m1[:, :], MAGIC, None, ALU.subtract, None, t)
                for cc in (c1, c2, c3, c4):
                    t = stt(ang[:, :], m1[:, :], -cc, ang[:, :], ALU.mult, ALU.add, t)
                yield [t]
                if rnd == 0:
                    t = stt(ang[:, :], n1[:, :], -d3, ang[:, :], ALU.mult, ALU.add, t)
            t = ts(ang[:, :], ang[:, :], 3.1415925, -3.1415925, ALU.min, ALU.max, t)
            t1 = act(S_t[:, :], ang[:, :], ACT.Sin, t, scale=col("rsgn", 0))
            t2 = act(m1[:, :], ang[:, :], ACT.Sin, t, scale=0.5)
            t2 = act(m1[:, :], m1[:, :], ACT.Square, t2)
            yield [t2]
            t = ts(C_t[:, :], m1[:, :], -2.0, 1.0, ALU.mult, ALU.add, t2)
            NS.t_tab = [t1, t]

        st_ring = Ring([Buf(small[:, 8 * i:8 * i + 8]) for i in range(1, 7)])

        rr_ring = Ring([Buf(here8[i]) for i in range(2)])

        def spread(r, rr, b, t):
            th = act(rr.ap[:, 0:4], r, ACT.Copy, t, rr.free)
            tl = tt(rr.ap[:, 4:8], r, rr.ap[:, 0:4].bitcast(FP), ALU.subtract, t, th, rr.free)
            yield [tl]
            rw = yield from row_ring.get()
            t = tr(b.ap[0:8, 0:128], rr.ap[:, :].bitcast(FP), th, tl, b.free, t_c, sig=True)
            rr_ring.put(rr, t)
            yield [t]
            t = act(rw.ap, b.ap[0:8, 0:128], ACT.Copy, t, rw.free)
            yield [t]
            for j in range(4):
                c_ = slice(128 * j, 128 * j + 128)
                t1 = mm(b.ap[:, c_], selr[0:8, c_], rw.ap, True, True, t, NS.t_sel, sig=(j == 3))
            row_ring.put(rw, t1)
            return t1

        row_ring = Ring([Buf(rows[0:8, :])])

        def rstd(sq, t_sq, scale, eps, out):
            yield [t_sq]
            b = yield from bank()
            for j in range(4):
                t = mm(b.ap[:, j:j + 1], sq[:, 128 * j:128 * j + 128], ones[:, 0:1], True, True, t_sq, t_c,
                       b.free, sig=(j == 3))
            s = yield from st_ring.get()
            yield [t]
            t = ts(s.ap[:, 0:4], b.ap[:, 0:4], scale, eps, ALU.mult, ALU.add, t, s.free)
            banks.put(b, t)
            t = PO.do(lambda e: e.tensor_tensor(s.ap[:, 4:8], s.ap[:, 0:4], pm05[:, 0:4], ALU.pow), t, t_pm, cost=960)
            yield [t]
            rr = yield from rr_ring.get()
            b = yield from bank()
            t = yield from spread(s.ap[:, 4:8], rr, b, t)
            st_ring.put(s, t)
            out["bank"], out["tok"] = b, t
            yield [t]

        pm05 = nlam[:, 4:8]
        t_pm = PO.do(lambda e: e.memset(pm05, -0.5))


        slot = []
        for s in range(2):
            sl = Prog()
            sl.K = big(20 * s, 1280)
            sl.Q = big(20 * s + 5, 1280)
            sl.E = big(20 * s + 10, 1024)
            sl.q, sl.V, sl.bg = [big(20 * s + 14 + 2 * i, 512) for i in range(3)]
            slot.append(sl)
        AT_r = Ring([Buf(big(76, 2048)), Buf(at(M_off, 2048))])
        KQ = Ring([Buf((big(60 + 4 * i, 512), big(62 + 4 * i, 512))) for i in range(4)])
        TMP = Ring([Buf(big(84 + 2 * i, 512)) for i in range(4)])
        nb_o, nb_sq, nb_r = [big(92 + 2 * i, 512) for i in (0, 1, 3)]
        NB = Ring([Buf(None)])
        g_off = [100, 102, 104, 106, 64, 66, 68, 70, 72, 74, 22, 24, 26, 28, 30, 32]
        gate = [big(o, 512) for o in g_off]
        gateR = [big(o, 512, FR) for o in g_off]
        oH = Acts([at(X_off + 2 * KB * h, 512, FR) for h in range(4)],
                  [at(X_off + 8 * KB + 2 * KB * h, 512, FR) for h in range(4)])
        oD = Acts([big(o, 512, FR) for o in (42, 20, 34, 36)], [big(76 + 2 * h, 512, FR) for h in range(4)])
        daQ = [big(2 * i, 512, FR) for i in range(2)]
        daK = [big(o, 512, FR) for o in (4, 6, 108)]
        daV = [big(8 + 2 * i, 512, FR) for i in range(2)]
        E4 = Ring([Buf(big(o, 512)) for o in (12, 14, 16, 40)])
        WT = [big(44, 2048, FR), big(52, 2048, FR)]
        QK_r, V_r, WT_r = (Ring([Buf(None)]) for _ in range(3))
        Wr = Ring([Buf(big(60 + 2 * i, 512)) for i in range(2)])
        hid = Acts([big(2 * i, 512, FR) for i in range(22)], [big(44 + 2 * i, 512, FR) for i in range(22)])
        FT = Ring([Buf(big(o, 512)) for o in (88, 90, 98, 100, 102, 104, 106)])
        H = Acts([t[:, :] for t in Hh], [t[:, :] for t in Hl])
        HP = Acts(H.hi, H.lo)
        tv = lambda t: t[:, :]
        for A_ in (oH, oD, hid):
            A_.hi = [tv(t) for t in A_.hi]
            A_.lo = [tv(t) for t in A_.lo]

        def pat(t, off, *dims):
            return bass.AP(t[:, :].tensor, off, [[t.shape[1], 128]] + [[s, n] for s, n in dims if n > 1])

        def prep_x(k, gname, gi, tok, hfree, sfree):
            def g():
                yield [tok]
                th = act(H.hi[k], X[k][:, :], ACT.Copy, tok, hfree, scale=col(gname, gi))
                q = PO
                if k == 0:
                    NS.t = tt(nb_o[:, :], X[k][:, :], X[k][:, :], ALU.mult, tok, sfree, q=q)
                else:
                    t = tt(nb_sq[:, :], X[k][:, :], X[k][:, :], ALU.mult, tok, sfree, NS.t, q=q)
                    NS.t = tt(nb_o[:, :], nb_o[:, :], nb_sq[:, :], ALU.add, t, NS.t, q=q)
                if k == 7:
                    spawn(make_R(1.0 / 1024.0, EPS_RMS))
                yield [th]
                H.tl[k] = stt(H.lo[k], X[k][:, :], col(gname, gi), H.hi[k].bitcast(FP), ALU.mult, ALU.subtract,
                              th, hfree)
                H.th[k] = th
            H.th[k] = H.tl[k] = None
            if k == 7:
                NS.R_ready = False
            spawn(g(), first)

        def make_R(scale, eps):
            o = {}
            yield from rstd(nb_o, NS.t, scale, eps, o)
            NS.tR = act(R[:, :], o["bank"].ap[:, :], ACT.Copy, o["tok"], fence())
            banks.put(o["bank"], NS.tR)
            NS.R_ready = True

        class Head:
            pass

        def hg_gate(st, l, h, d, bk, tok):
            sl = slot[st.s]
            k_, e_ = sl.K[:, 512 * d:512 * d + 512], sl.E[:, 512 * d:512 * d + 512]
            z = yield from TMP.get()
            t = tt(z.ap[:, :], bk.ap[:, :], R[:, :], ALU.mult, tok, NS.tR, z.free)
            banks.put(bk, t)
            yield [t]
            while st.prev2 is not None and st.prev2.last_a is None:
                yield None
            fr = st.prev2.last_a if st.prev2 is not None else st.free
            tk = act(k_, z.ap[:, :], ACT.Sigmoid, t, fr, scale=-1.0)
            te = act(e_, z.ap[:, :], ACT.Sigmoid, t, fr)
            TMP.put(z, te)
            if l:
                yield [te]
                bb, cc = (lbt[:, 8 * i + 4 * d + h:8 * i + 4 * d + h + 1] for i in (0, 1))
                tk = ts(k_, k_, cc, None, ALU.mult, None, tk, NS.t_lb)
                te = ts(e_, e_, cc, bb, ALU.mult, ALU.add, te, NS.t_lb)
            st.k[d], st.eg[d] = tk, te

        def hg_v(st, bk, tok):
            z = yield from TMP.get()
            t = tt(z.ap[:, :], bk.ap[:, :], R[:, :], ALU.mult, tok, NS.tR, z.free)
            banks.put(bk, t)
            yield [t]
            b = yield from bank()
            for j in range(4):
                t1 = tr(b.ap[:, 128 * j:128 * j + 128], z.ap[:, 128 * j:128 * j + 128], t, b.free, t_c, sig=(j == 3))
            TMP.put(z, t1)
            yield [t1]
            while st.prev2 is not None and st.prev2.last_v is None:
                yield None
            st.v = act(slot[st.s].V[:, :], b.ap[:, :], ACT.Copy, t1,
                       st.prev2.last_v if st.prev2 is not None else st.free)
            banks.put(b, st.v)

        def hg_q(st, bk, tok):
            while st.prev2 is not None and st.prev2.last_a is None:
                yield None
            st.q = tt(slot[st.s].q[:, :], bk.ap[:, :], R[:, :], ALU.mult, tok, NS.tR,
                      st.prev2.last_a if st.prev2 is not None else st.free)
            banks.put(bk, st.q)

        def hg_g(st, bk, tok):
            z = yield from TMP.get()
            t1 = tt(z.ap[:, :], bk.ap[:, :], R[:, :], ALU.mult, tok, NS.tR, z.free)
            banks.put(bk, t1)
            yield [t1]
            while st.prev2 is not None and st.prev2.last_g is None:
                yield None
            st.bg = act(slot[st.s].bg[:, :], z.ap[:, :], ACT.Sigmoid, t1,
                        st.prev2.last_g if st.prev2 is not None else st.free)
            TMP.put(z, st.bg)

        def hg_main(st, l, h, prev):
            sl = slot[st.s]
            K, Q, E, q = sl.K, sl.Q, sl.E, sl.q

            def keep(b, t, lev):
                yield [t]
                ATd = pat(at_.ap, 0, (640, 4), (1, 128))
                if lev is None:
                    st.at = act(ATd, V4(b.ap), ACT.Copy, t, at_.free)
                else:
                    while st.at is None:
                        yield None
                    m_ = msk[:, 128 * lev:128 * lev + 128]
                    st.at = DV.do(lambda e: e.copy_predicated(ATd, m_[:, None, :].broadcast_to([128, 4, 128]),
                                                              V4(b.ap)), t, st.at, NS.t_msk, cost=602)
                banks.put(b, st.at)
                st.levels += 1

            def scores(kv, qv, after, lev, done_):
                yield [after]
                b = yield from bank()
                for j in range(4):
                    s_ = slice(128 * j, 128 * j + 128)
                    t = mm(b.ap[:, s_], kv[:, s_], qv[:, s_], True, True, after, b.free, sig=(j == 3))
                done_(t)
                yield from keep(b, t, lev)

            def level(n, lev, after):
                m = n // 2
                kq = yield from KQ.get()
                yield [kq.free, after]
                dims = [(n, 512 // n), (m + 512, 2), (1, m)]
                out = [x_[:, :].rearrange("p (b h e) -> p b h e", h=2, e=m) for x_ in kq.ap]
                if m == 1:
                    out = [x_[:, :, :, 0] for x_ in out]
                if n == 512:
                    out = [x_[:, 0] for x_ in out]
                t = [act(out[0], pat(K, 0, *dims), ACT.Copy, after, kq.free),
                     act(out[1], pat(Q, 128, *dims), ACT.Copy, after)]
                spawn(scores(kq.ap[0], kq.ap[1], t, lev, lambda t: KQ.put(kq, t)))
                return t

            def double(m, after):
                nb = 512 // (2 * m)
                dims = [(2 * m, nb), (1, m)]
                tot = lambda d, h: pat(E, 512 * d + h * m + m - 1, (2 * m, nb))

                def by(x, y, *aft):
                    y = y[:, :, None].broadcast_to([128, nb, m]) if m > 1 else y
                    return tt(x, x, y, ALU.mult, *aft)
                ks = [pat(K, 0, *dims), pat(K, 512 + m, *dims)]
                qs = [pat(Q, 640 + m, *dims), pat(Q, 128, *dims)]
                r = []
                for d in range(2):
                    r.append(by(ks[d], tot(d, 1 - d), after))
                    r.append(by(qs[d], tot(d, d), after))
                out = pat(E, 2 * m - 1, (512, 2), (2 * m, nb))
                r.append(tt(out, out, pat(E, m - 1, (512, 2), (2 * m, nb)), ALU.mult, r))
                return r

            while st.q is None or None in st.k or None in st.eg:
                yield None
            yield [st.k, st.eg, st.q]
            st.levels, st.at = 0, None
            x = yield from TMP.get()
            tx = tt(x.ap[:, :], K[:, 0:512], K[:, 512:1024], ALU.add, st.k, x.free)
            tq = [tt(Q[:, 640 - 512 * d:1152 - 512 * d], q[:, :], E[:, 512 * d:512 * d + 512], ALU.mult, st.eg, st.q)
                  for d in range(2)]
            at_ = yield from AT_r.get()
            yield [tx]
            spawn(scores(x.ap, q, [tx, st.q], None, lambda t: TMP.put(x, t)))
            yield tq
            t = yield from level(2, 6, [tq, st.k])
            tn = [tq, st.k, st.eg]
            for i in range(6):
                yield [t]
                tn = double(2 ** i, [t, tn])
                yield [tn[3]]
                t = yield from level(4 * 2 ** i, 5 - i, tn[0:4])
            yield [t]
            tn = double(64, [t, tn])
            tot = lambda d, j: E[:, 512 * d + 128 * j + 127:512 * d + 128 * j + 128]
            kf, kb = (lambda j: K[:, 128 * j:128 * j + 128]), (lambda j: K[:, 512 + 128 * j:640 + 128 * j])
            qb, qf = (lambda j: Q[:, 128 + 128 * j:256 + 128 * j]), (lambda j: Q[:, 640 + 128 * j:768 + 128 * j])
            ts(K[:, 1024:1152], kf(0), tot(0, 1), None, ALU.mult, None, tn)
            ts(Q[:, 1152:1280], qf(3), tot(0, 2), None, ALU.mult, None)
            ts(K[:, 1152:1280], kb(3), tot(1, 2), None, ALU.mult, None)
            tn = ts(Q[:, 0:128], qb(0), tot(1, 1), None, ALU.mult, None)
            yield [tn]
            st.off = []
            far = [(K[:, 1024:1152], K[:, 1152:1280]), ([pat(Q, 896, (256, 2), (1, 128))], [pat(Q, 0, (256, 2), (1, 128))])]
            for d in range(2):
                kx, (qp,) = far[0][d], far[1][d]
                c = lambda t_, i, n=1: t_[:, 128 * i:128 * (i + n)]
                ba = yield from bank()
                if d == 0:
                    mm(c(ba.ap, 0), kf(0), qf(1), True, True, tn, ba.free)
                    t = mm(c(ba.ap, 1, 2), kx, qp, True, True, sig=True)
                else:
                    mm(c(ba.ap, 0, 2), kx, qp, True, True, tn, ba.free)
                    t = mm(c(ba.ap, 2), kb(3), qb(2), True, True, sig=True)
                bb = yield from bank()
                if d == 0:
                    mm(c(bb.ap, 0, 2), kf(1), qp, True, True, bb.free)
                    t2 = mm(c(bb.ap, 2), kf(2), qf(3), True, True, sig=True)
                else:
                    mm(c(bb.ap, 0, 2), kb(2), qp, True, True, bb.free)
                    t2 = mm(c(bb.ap, 2), kb(1), qb(0), True, True, sig=True)

                def store(d=d, ba=ba, bb=bb, t=t, t2=t2):
                    o1, o2, o3 = ((1, 6, 11), (12, 8, 4))[d]
                    yield [t]
                    t = act(c(at_.ap, o1, 3), c(ba.ap, 0, 3), ACT.Copy, t, at_.free)
                    banks.put(ba, t)
                    yield [t2]
                    act(c(at_.ap, o2, 2), c(bb.ap, 0, 2), ACT.Copy, t2)
                    t = act(c(at_.ap, o3), c(bb.ap, 2), ACT.Copy, t2)
                    banks.put(bb, t)
                    st.off.append(t)
                spawn(store())
            st.last_a = [t2, tn]
            while st.levels < 8 or len(st.off) < 2 or st.v is None:
                yield None
            yield [st.at, st.off, st.v]
            b = yield from bank()
            for i in range(4):
                t = mm(b.ap[:, :], sl.V[:, 128 * i:128 * i + 128], at_.ap[:, 512 * i:512 * i + 512], i == 0, i == 3,
                       st.at, st.off, st.v, b.free, sig=(i == 3))
            AT_r.put(at_, t)
            st.last_v = [t]
            yield from norm_out(b, t, col("hg_norm", 4 * l + h), sl.bg, st, oH, h, oH_free)
            st.last_g = fence()

        def norm_out(b, t, gcol, extra, st, O, h, ofree):
            nb = yield from NB.get()
            yield [t]
            to = act(nb_o[:, :], b.ap[:, :], ACT.Copy, t, nb.free)
            banks.put(b, to)
            tq = act(nb_sq[:, :], nb_o[:, :], ACT.Square, to)
            o = {}
            yield from rstd(nb_sq, tq, 1.0 / 128.0, EPS_RMS, o)
            t = stt(nb_r[:, :], nb_o[:, :], gcol, o["bank"].ap[:, :], ALU.mult, ALU.mult, o["tok"], NS.t_lam)
            banks.put(o["bank"], t)
            if extra is not None:
                while st.bg is None:
                    yield None
                t = tt(nb_r[:, :], nb_r[:, :], extra[:, :], ALU.mult, t, st.bg)
            yield [t]
            th = act(O.hi[h], nb_r[:, :], ACT.Copy, t, ofree())
            yield [th]
            O.tl[h] = tt(O.lo[h], nb_r[:, :], O.hi[h].bitcast(FP), ALU.subtract, th)
            O.th[h] = th
            NB.put(nb, O.tl[h])

        lo64, hi64 = slice(0, 64), slice(64, 128)

        def split_q(Q, z, t, free):
            th = [act(Q[c][p, :], z[p, :], ACT.Copy, t, free) for c, p in enumerate((lo64, hi64))]
            yield th
            tl = [tt(Q[c][o, :], z[p, :], Q[c][p, :].bitcast(FP), ALU.subtract, th[c], free)
                  for c, p, o in ((0, lo64, hi64), (1, hi64, lo64))]
            return th + tl

        def split_k(K, z, t, free):
            th = [act(K[c][p, :], z[p, :], ACT.Copy, t, free) for c, p in enumerate((lo64, hi64))]
            yield th
            tl = []
            for c, p, o in ((0, lo64, hi64), (1, hi64, lo64)):
                tl.append(copy(K[c][o, :], K[c][p, :].bitcast(FP), th[c], free))
                tl.append(tt(K[2][p, :], z[p, :], K[c][p, :].bitcast(FP), ALU.subtract, th[c], free))
            return th + tl

        def score(out, Q, K, c, qs, ks, more, *after):
            p = (lo64, hi64)[c]
            mm(out, Q[c][:, qs], K[c][:, ks], True, False, *after)
            more()
            return mm(out, Q[c][p, qs], K[2][p, ks], False, True, sig=True)

        def da_rope(st, which, bk, tok):
            z = yield from TMP.get()
            w = yield from TMP.get()
            t1 = swap(w.ap[:, :], bk.ap[:, :], 8, tok, w.free)
            t2 = tt(w.ap[:, :], w.ap[:, :], RS[:, :], ALU.mult, t1, NS.tRC)
            t3 = tt(z.ap[:, :], bk.ap[:, :], RC[:, :], ALU.mult, tok, z.free, NS.tRC)
            banks.put(bk, t3)
            yield [t3]
            t4 = tt(z.ap[:, :], z.ap[:, :], w.ap[:, :], ALU.add, t3, t2)
            TMP.put(w, t4)
            yield [t4]
            if which == 0:
                st.qk_b = yield from QK_r.get()
            while st.qk_b is None:
                yield None
            f = (split_q, split_k)[which]
            tl = yield from f((daQ, daK)[which], z.ap, t4, st.qk_b.free)
            TMP.put(z, tl)
            st.qk[which] = tl

        def da_v(st, bk, tok):
            z = yield from TMP.get()
            t = tt(z.ap[:, :], bk.ap[:, :], R[:, :], ALU.mult, tok, NS.tR, z.free)
            banks.put(bk, t)
            yield [t]
            b = yield from bank()
            for j in range(4):
                t1 = tr(b.ap[:, 128 * j:128 * j + 128], z.ap[:, 128 * j:128 * j + 128], t, b.free, sig=(j == 3))
            TMP.put(z, t1)
            st.v_b = yield from V_r.get()
            yield [t1]
            th = act(daV[0][:, :], b.ap[:, :], ACT.Copy, t1, st.v_b.free)
            yield [th]
            tl = tt(daV[1][:, :], b.ap[:, :], daV[0][:, :].bitcast(FP), ALU.subtract, th, st.v_b.free)
            banks.put(b, tl)
            st.v = [th, tl]

        def da_block(st, l, qt):
            sm = yield from st_ring.get()
            mx, ng, su, r_ = (sm.ap[:, 2 * i:2 * i + 2] for i in range(4))
            qs = slice(128 * qt, 128 * qt + 128)
            bs, es = [], []
            for c in range(2):
                b = yield from bank()
                t = score(b.ap[:, :], daQ, daK, c, qs, slice(0, 512), lambda: None,
                          [st.qk[0], st.qk[1]], b.free)
                bs.append((b, t))
            st.scored = t
            st.nsc += 1
            for c, (b, t) in enumerate(bs):
                yield [t]
                tm = reduce_max(mx[:, c:c + 1], b.ap[:, :], t, sm.free)
                tn = ts(ng[:, c:c + 1], mx[:, c:c + 1], -0.125, None, ALU.mult, None, tm, sm.free)
                bs[c] = (b, [t, tn])
            for c, (b, t) in enumerate(bs):
                e_ = yield from E4.get()
                yield [t]
                te = act(e_.ap[:, :], b.ap[:, :], ACT.Exp, t, e_.free, bias=ng[:, c:c + 1], scale=0.125,
                         accum=su[:, c:c + 1])
                banks.put(b, te)
                es.append((e_, te))
            w = yield from Wr.get()
            yield [te]
            t = DV.do(lambda e: e.reciprocal(r_, su), te, es[0][1], cost=81)
            t = tt(r_[:, 1:2], r_[:, 1:2], nlam[:, l:l + 1], ALU.mult, t, NS.t_lam)
            t1 = ts(w.ap[:, :], es[0][0].ap[:, :], r_[:, 0:1], None, ALU.mult, None, t, w.free)
            t2 = stt(w.ap[:, :], es[1][0].ap[:, :], r_[:, 1:2], w.ap[:, :], ALU.mult, ALU.add, t1)
            st_ring.put(sm, t2)
            E4.put(es[0][0], t2)
            E4.put(es[1][0], t2)
            yield [t2]
            if qt == 0:
                st.wt_b = yield from WT_r.get()
            while st.wt_b is None:
                yield None
            b = yield from bank()
            for j in range(4):
                t = tr(b.ap[:, 128 * j:128 * j + 128], w.ap[:, 128 * j:128 * j + 128], t2, b.free, sig=(j == 3))
            Wr.put(w, t)
            dst = [V4(W_)[:, :, qs] for W_ in WT]
            yield [t]
            th = act(dst[0], V4(b.ap), ACT.Copy, t, st.wt_b.free)
            yield [th]
            tl = tt(dst[1], V4(b.ap), dst[0].bitcast(FP), ALU.subtract, th, st.wt_b.free)
            banks.put(b, tl)
            st.WT += [th, tl]
            st.nwt += 1

        def da_main(st, l, h):
            st.nsc, st.nwt, st.WT, st.wt_b = 0, 0, [], None
            while st.qk[0] is None or st.qk[1] is None:
                yield None
            yield st.qk[0] + st.qk[1]
            for qt in range(4):
                spawn(da_block(st, l, qt))
                while st.nsc <= qt:
                    yield None
            QK_r.put(st.qk_b, st.scored)
            while st.nwt < 4 or st.v is None:
                yield None
            yield st.WT + st.v
            b = yield from bank()
            for j in range(4):
                s_ = slice(128 * j, 128 * j + 128)
                t = mm3(b.ap[:, :], daV[0][:, s_], daV[1][:, s_], WT[0][:, 512 * j:512 * j + 512],
                        WT[1][:, 512 * j:512 * j + 512], j == 0, j == 3, [st.WT, st.v], b.free, sig=(j == 3))
            WT_r.put(st.wt_b, t)
            V_r.put(st.v_b, t)
            yield from norm_out(b, t, col("da_norm", 4 * l + h), None, st, oD, h, oD_free)

        oH_free = lambda: NS.oH_free()
        oD_free = lambda: NS.oD_free

        s_re = [sem() for _ in range(8)]
        s_sp = sem()
        scr = a["scr"]
        xtok = [(s_x[k], 16) for k in range(8)]

        def w1(name, l, n):
            return a[name][l, n]

        def in_job(l, n, evac, before=None):
            job([(a["win1"][l, n], 1024, [(k, H, k, 0, k == 0, k == 7) for k in range(8)])], 1, evac, before)

        def first_block(l):
            hs = [Head() for _ in range(4)]
            ds = [Head() for _ in range(4)]

            def start_layer():
                if l == 0:
                    for k in range(8):
                        H.th[k] = H.tl[k] = None

                    def xg():
                        sq = [nb_sq, nb_r]
                        free = [None, None]
                        for k in range(8):
                            yield [xtok[k], t_c]
                            th = act(H.hi[k], X[k][:, :], ACT.Copy, xtok[k], t_c, scale=col("attn_norm", k))
                            if k == 0:
                                NS.t = act(nb_o[:, :], X[k][:, :], ACT.Square, xtok[k])
                            else:
                                t = act(sq[k % 2][:, :], X[k][:, :], ACT.Square, xtok[k], free[k % 2])
                            yield [th]
                            H.tl[k] = stt(H.lo[k], X[k][:, :], col("attn_norm", k), H.hi[k].bitcast(FP),
                                          ALU.mult, ALU.subtract, th)
                            H.th[k] = th
                            if k:
                                NS.t = tt(nb_o[:, :], nb_o[:, :], sq[k % 2][:, :], ALU.add, t, NS.t, q=PO)
                                free[k % 2] = NS.t
                        NS.xread = fence()
                        spawn(g())
                    spawn(xg(), first)
                    spawn(setup())
                    NS.R_ready = False
                    NS.oH_free = lambda: NS.xread
                else:
                    NS.oH_free = lambda: NS.spill + [fence()]
                    for r_ in (KQ, TMP, AT_r):
                        r_.renew(fence())
                for A_ in (oH, oD):
                    for k in range(4):
                        A_.th[k] = A_.tl[k] = None
                nb = NB.pop()

                def g():
                    if l == 0:
                        while not NS.ready:
                            yield None
                        for r_ in (KQ, TMP, AT_r):
                            r_.renew(fence())
                        hs[0].free = hs[1].free = fence()
                        yield [NS.t]
                        yield from make_R(1.0 / 1024.0, EPS_RMS)
                        yield from tables()
                    while not NS.R_ready or (l and len(NS.spill) < 8):
                        yield None
                    NB.put(nb, fence())
                    yield [NS.tR]
                    t1 = tt(RC[:, :], C_t[:, :], R[:, :], ALU.mult, NS.tR, NS.t_tab, fence(), q=PO)
                    t2 = tt(RS[:, :], S_t[:, :], R[:, :], ALU.mult, NS.tR, NS.t_tab, q=PO)
                    NS.tRC = [t1, t2]
                if l:
                    spawn(g())

            for h in range(4):
                st = hs[h]
                st.s = h % 2
                st.k, st.eg = [None] * 2, [None] * 2
                st.last_a = st.last_v = st.last_g = None
                st.q = st.v = st.bg = None
                st.prev2 = hs[h - 2] if h >= 2 else None

                def bef(h=h, st=st):
                    if h == 0:
                        start_layer()
                    st.free = fence()

                def ev_q(b, t, h=h, st=st):
                    spawn(hg_q(st, b[0], t), first)
                    spawn(hg_main(st, l, h, hs[h - 1] if h else None))

                in_job(l, 16 + h, lambda b, t, h=h, st=st: spawn(hg_gate(st, l, h, 0, b[0], t)), bef)
                in_job(l, 20 + h, lambda b, t, h=h, st=st: spawn(hg_gate(st, l, h, 1, b[0], t)))
                in_job(l, 24 + h, lambda b, t, st=st: spawn(hg_v(st, b[0], t)))
                in_job(l, 12 + h, ev_q)
                in_job(l, 28 + h, lambda b, t, st=st: spawn(hg_g(st, b[0], t)))

            def gates(i0, n):
                for i in range(i0, i0 + n):
                    def ev(b, t, i=i, i0=i0, n=n):
                        def g():
                            fr = hs[3].free
                            if i >= 4:
                                while hs[3].last_a is None:
                                    yield None
                                fr = hs[3].last_a
                            if i >= 10:
                                while hs[3].last_v is None:
                                    yield None
                                fr = hs[3].last_v
                            t1 = tt(gate[i][:, :], b[0].ap[:, :], R[:, :], ALU.mult, t, NS.tR, fr)
                            banks.put(b[0], t1)
                            gr[i] = t1
                            if i == i0 + n - 1:
                                yield [t1]
                                for m in range(i0, i0 + n):
                                    gt[m] = act(gate[m][:, :], gate[m][:, :], ACT.Sigmoid, gr[m])
                        spawn(g())
                    in_job(l, (32 if i % 2 == 0 else 40) + i // 2, ev)

            gt = [None] * 16
            gr = [None] * 16

            def da(h):
                st = ds[h]
                st.qk, st.v, st.qk_b, st.v_b = [None, None], None, None, None

                def ev(b, t, w=0):
                    def g():
                        if h == 0 and w == 0:
                            while hs[2].last_v is None:
                                yield None
                            for r_ in (QK_r, V_r, E4):
                                r_.renew([hs[2].last_v, hs[2].last_a])
                        if w == 2:
                            yield from da_v(st, b[0], t)
                        else:
                            yield from da_rope(st, w, b[0], t)

                    def start():
                        if h == 0:
                            while hs[3].last_v is None:
                                yield None
                            f = [hs[3].last_v, hs[3].last_a, hs[2].last_v]
                            NS.oD_free = f
                            WT_r.renew(f)
                            Wr.renew(f)
                        yield from da_main(st, l, h)
                    spawn(g())
                    if w == 2:
                        spawn(start())
                for w in range(3):
                    in_job(l, 4 * w + h, lambda b, t, w=w, ev=ev: ev(b, t, w))

            gates(0, 4)
            da(0)
            gates(4, 2)
            da(1)
            gates(6, 2)
            da(2)
            gates(8, 2)
            da(3)
            gates(10, 3)
            gates(13, 3)

            mg = Acts([g[:, :] for g in gateR[0::2]], [g[:, :] for g in gateR[1::2]])
            for n in range(8):
                def ev(b, t, n=n):
                    def g():
                        x_ = yield from TMP.get()
                        y_ = yield from TMP.get()
                        while gt[2 * n] is None or gt[2 * n + 1] is None:
                            yield None
                        t1 = tt(x_.ap[:, :], b[0].ap[:, :], gate[2 * n][:, :], ALU.mult, t, gt[2 * n], x_.free)
                        banks.put(b[0], t1)
                        t2 = tt(y_.ap[:, :], b[1].ap[:, :], gate[2 * n + 1][:, :], ALU.mult, t, gt[2 * n + 1], y_.free)
                        banks.put(b[1], t2)
                        t1 = tt(x_.ap[:, :], x_.ap[:, :], y_.ap[:, :], ALU.add, t1, t2)
                        TMP.put(y_, t1)
                        yield [t1]
                        th = act(mg.hi[n], x_.ap[:, :], ACT.Copy, t1)
                        yield [th]
                        mg.tl[n] = tt(mg.lo[n], x_.ap[:, :], mg.hi[n].bitcast(FP), ALU.subtract, th)
                        mg.th[n] = th
                        TMP.put(x_, mg.tl[n])
                    spawn(g())

                job([(a["wab"][l, n], 1024,
                      [(4 + k, oH, k, 1, k == 0, k == 3) for k in range(4)]
                      + [(k, oD, k, 0, k == 0, k == 3) for k in range(4)])], 2, ev)

            src = a["xT"] if l == 0 else scr
            for n in range(8):
                def bef(n=n):
                    if n == 0:
                        until(lambda: len(NB.q) == 1)
                        for k in range(8):
                            xtok[k] = SP.dma(X[k][:, :], src[:, 512 * k:512 * k + 512], s_re[k], PE.last(),
                                             NS.oH_free())
                        ln_start()

                def ev(b, t, n=n):
                    xtok[n] = tt(X[n][:, :], X[n][:, :], b[0].ap[:, :], ALU.add, t, xtok[n])
                    banks.put(b[0], xtok[n])
                    prep_x(n, "ffn_norm", 8 * l + n, xtok[n], NS.hfree, NS.sfree)
                job([(a["wo"][l, n], 1024, [(k, mg, k, 0, k == 0, k == 7) for k in range(8)])], 1, ev, bef)

        def up_job(w, j, fix, ev, bef=None):
            A = HP if fix and j < NFIX else H
            if fix and j in (POOL_MX if fix[0] == 'ln1' else POOL_LO):
                on_pool.add(len(chunks))
            job([(w, 1024, [(k, A, k, 0, k == 0, k == 7) for k in range(8)])], 1, ev, bef)

        def ffn(gu, dn, acc, useR, before=None, fix=None):
            for n in range(22):
                s_ = {}

                def ev_G(b, t, s=s_, n=n):
                    def g():
                        if fix and 2 * n < NFIX:
                            x_, t1, wb = yield from fixed(fix, 2 * n, b[0], t, FT)
                            yield [t1]
                            s["t"] = act(x_.ap[:, :], x_.ap[:, :], ACT.Silu, t1, bias=wb)
                            s["g"] = x_
                            return
                        x_ = yield from FT.get()
                        if useR:
                            t1 = tt(x_.ap[:, :], b[0].ap[:, :], R[:, :], ALU.mult, t, NS.tR, x_.free)
                            banks.put(b[0], t1)
                            yield [t1]
                            s["t"] = act(x_.ap[:, :], x_.ap[:, :], ACT.Silu, t1)
                        else:
                            s["t"] = act(x_.ap[:, :], b[0].ap[:, :], ACT.Silu, t, x_.free)
                            banks.put(b[0], s["t"])
                        s["g"] = x_
                    spawn(g())

                def ev_U(b, t, s=s_, n=n):
                    def g():
                        isfix = fix and 2 * n + 1 < NFIX
                        if isfix:
                            y_, t1, wb = yield from fixed(fix, 2 * n + 1, b[0], t, FT)
                        else:
                            y_ = yield from FT.get()
                        while "g" not in s:
                            yield None
                        x_ = s["g"]
                        if isfix:
                            t1 = stt(y_.ap[:, :], y_.ap[:, :], wb, x_.ap[:, :], ALU.add, ALU.mult, t1, s["t"])
                        elif useR:
                            t1 = tt(y_.ap[:, :], b[0].ap[:, :], R[:, :], ALU.mult, t, NS.tR, y_.free)
                            banks.put(b[0], t1)
                            t1 = tt(y_.ap[:, :], y_.ap[:, :], x_.ap[:, :], ALU.mult, t1, s["t"])
                        else:
                            t1 = tt(y_.ap[:, :], b[0].ap[:, :], x_.ap[:, :], ALU.mult, t, s["t"], y_.free)
                            banks.put(b[0], t1)
                        FT.put(x_, t1)
                        yield [t1]
                        th = act(hid.hi[n], y_.ap[:, :], ACT.Copy, t1, NS.hidfree)
                        yield [th]
                        hid.tl[n] = tt(hid.lo[n], y_.ap[:, :], hid.hi[n].bitcast(FP), ALU.subtract, th, NS.hidfree)
                        hid.th[n] = th
                        FT.put(y_, hid.tl[n])
                    spawn(g())

                def bef(n=n):
                    if n == 0:
                        if before is not None:
                            before()
                        NS.hidfree = fence()
                        FT.renew(NS.hidfree)
                        hid.reset()
                up_job(gu(n, 0), 2 * n, fix, ev_G, bef)
                up_job(gu(n, 1), 2 * n + 1, fix, ev_U)
            for n in range(8):
                w = dn(n)
                chs = []
                for c0, kn in ((0, 8), (8, 8), (16, 6)):
                    chs.append((w[:, 128 * c0:128 * (c0 + kn)], 128 * kn,
                                [(k, hid, c0 + k, 0, c0 + k == 0, c0 + k == 21) for k in range(kn)]))

                def bef(n=n):
                    if n == 0:
                        until(lambda: len(FT.q) == len(FT.all))
                        ln_start()
                        NS.spill = []
                job(chs, 1, lambda b, t, n=n: acc(n, b[0], t), bef)

        def ffn_a(l):
            def acc(n, b, t):
                xtok[n] = tt(X[n][:, :], X[n][:, :], b.ap[:, :], ALU.add, t, xtok[n])
                banks.put(b, xtok[n])
                if l == 0:
                    prep_x(n, "attn_norm", 8 * (l + 1) + n, xtok[n], NS.hfree, NS.sfree)
                    NS.spill.append(SP.dma(scr[:, 512 * n:512 * n + 512], X[n][:, :], s_sp, xtok[n]))
                else:
                    prep_x(n, "final_norm", n, xtok[n], NS.hfree, NS.sfree)
            ffn(lambda n, u: a["wgu1"][l, 2 * n + u], lambda n: a["wd1"][l, n], acc, True)

        L_m0, L_s1, L_s2, L_sq = [at(M_off + 2048 * i, 512) for i in range(4)]
        L_M = RC
        LN = State()

        def ln_start():
            NS.hfree = PE.last()
            H.reset()
            HP.reset()
            NS.sfree = fence()
            LN.m0 = LN.s1 = LN.s2 = None
            LN.n = 0

        def ln_acc(n, b, t, scale, name, l, final):
            if n == 7:
                NS.R_ready = False
            if n == 0:
                t = stt(X[0][:, :], X[0][:, :], scale, b.ap[:, :], ALU.mult, ALU.add, t, xtok[0])
                banks.put(b, t)
                LN.pre = [None] * 8

            def early():
                for k in range(1, 8):
                    xtok[k] = tt(X[k][:, :], X[k][:, :], L_m0[:, :], ALU.subtract, xtok[k], LN.m0,
                                 q=PO if k in LN_PRE else DV)
                    LN.pre[k] = xtok[k]
                    yield [xtok[k]]

            def g(t=t):
                if n == 0:
                    yield [t]
                    s_ = yield from bank()
                    t1 = mm(s_.ap[:, :], ones, X[0][:, :], True, True, t, s_.free, sig=True)
                    yield [t1]
                    LN.m0 = act(L_m0[:, :], s_.ap[:, :], ACT.Copy, t1, NS.sfree, scale=1.0 / (128.0 * scale))
                    banks.put(s_, LN.m0)
                    yield [LN.m0]
                    spawn(early(), first)
                    t = stt(X[0][:, :], L_m0[:, :], -scale, X[0][:, :], ALU.mult, ALU.add, t, LN.m0)
                else:
                    while LN.pre[n] is None:
                        yield None
                    yield [LN.pre[n]]
                    t = stt(X[n][:, :], X[n][:, :], scale, b.ap[:, :], ALU.mult, ALU.add, t, LN.pre[n])
                    banks.put(b, t)
                xtok[n] = t
                while LN.n != n:
                    yield None
                yield [t]
                on_dv = LN_DV2 if name == "ln2" else LN_DV
                q1, q2 = (DV if n in on_dv[i] else PO for i in range(2))
                if n and n == 7:
                    t1 = act(L_sq[:, :], X[n][:, :], ACT.Square, t, LN.s2, NS.sfree)
                if not final:
                    th = act(H.hi[n], X[n][:, :], ACT.Copy, t, NS.hfree, scale=col(name, 16 * l + 2 * n))
                if n == 0:
                    LN.s1 = PO.do(lambda e: e.tensor_copy(L_s1[:, :], X[0][:, :]), t, NS.sfree, cost=1830)
                    LN.s2 = act(L_s2[:, :], X[0][:, :], ACT.Square, t, NS.sfree)
                else:
                    LN.s1 = tt(L_s1[:, :], L_s1[:, :], X[n][:, :], ALU.add, t, LN.s1, q=q1)
                    if n < 7:
                        t1 = act(L_sq[:, :], X[n][:, :], ACT.Square, t, LN.s2, NS.sfree)
                if n == 7:
                    yield [t1]
                    LN.s2 = tt(L_s2[:, :], L_s2[:, :], L_sq[:, :], ALU.add, t1, LN.s2, q=q2)
                if not final:
                    HP.tl[n] = stt(H.lo[n], X[n][:, :], col(name, 16 * l + 2 * n), H.hi[n].bitcast(FP),
                                   ALU.mult, ALU.subtract, th, NS.hfree)
                    HP.th[n] = th
                if 0 < n < 7:
                    yield [t1]
                    LN.s2 = tt(L_s2[:, :], L_s2[:, :], L_sq[:, :], ALU.add, t1, LN.s2, q=q2)
                LN.n += 1
            spawn(g(), first)
            if n == 7:
                spawn(ln_finish(name, l, 4.0 * EPS_LN if name != "ln2" else EPS_LN, final), first)

        def ln_finish(name, l, eps, final):
            while LN.n != 8:
                yield None
            yield [LN.s1, LN.s2]
            bm = yield from bank()
            br = yield from bank()
            tst = []
            for i, (S_, ts_) in enumerate(((L_s1, LN.s1), (L_s2, LN.s2))):
                b = (bm, br)[i]
                for j in range(4):
                    t = mm(b.ap[:, j:j + 1], S_[:, 128 * j:128 * j + 128], ones[:, 0:1], True, True,
                           ts_, b.free, sig=(j == 3))
                tst.append(t)
            sa = yield from st_ring.get()
            sb_ = yield from st_ring.get()
            yield [tst[0]]
            md, v, r_, q_ = sa.ap[:, 0:4], sa.ap[:, 4:8], sb_.ap[:, 0:4], sb_.ap[:, 4:8]
            tm = ts(md, bm.ap[:, 0:4], -1.0 / 1024.0, None, ALU.mult, None, tst[0], sa.free)
            t1 = tt(q_, md, md, ALU.mult, tm, sb_.free)
            t2 = ts(v, br.ap[:, 0:4], 1.0 / 1024.0, eps, ALU.mult, ALU.add, tst[1], sa.free)
            bm.free, br.free = [tm], [t2]
            t2 = tt(v, v, q_, ALU.subtract, t1, t2)
            t = PO.do(lambda e: e.tensor_tensor(r_, v, pm05[:, 0:4], ALU.pow), t2, t_pm, sb_.free, cost=960)
            rr = yield from rr_ring.get()
            tM = yield from spread(md, rr, bm, tm)
            yield [tM]
            LN.tM = (copy(L_M[:, :], bm.ap[:, :], tM, NS.sfree) if final else
                     act(L_M[:, :], bm.ap[:, :], ACT.Copy, tM, NS.sfree))
            banks.put(bm, LN.tM)
            xr = [LN.s1, LN.s2]

            def add_mean():
                for k in range(8):
                    yield [LN.tM]
                    xtok[k] = tt(X[k][:, :], X[k][:, :], L_M[:, :], ALU.add, LN.tM, xtok[k], xr, HP.tl[k], HP.th[k],
                                 q=PO if k in (FIN_ADD if final else LN_ADD) else DV)
                    LN.am[k] = xtok[k]
            LN.am = [None] * 8
            spawn(add_mean(), first)
            yield [t]
            rr = yield from rr_ring.get()
            tR = yield from spread(r_, rr, br, t)
            st_ring.put(sa, tR)
            st_ring.put(sb_, tR)
            yield [tR]
            NS.tR = act(R[:, :], br.ap[:, :], ACT.Copy, tR, NS.sfree)
            banks.put(br, NS.tR)
            NS.R_ready = True
            yield [NS.tR]
            for k in range(8):
                while LN.am[k] is None:
                    yield None
                gcol, bcol = col(name, 16 * l + 2 * k), col(name, 16 * l + 2 * k + 1)
                if not final:
                    t = tt(X[k][:, :], X[k][:, :], R[:, :], ALU.mult, NS.tR, xtok[k])
                    yield [t]
                    xtok[k] = act(X[k][:, :], X[k][:, :], ACT.Identity, t, scale=gcol, bias=bcol)
                    spawn(true_h(k), first)
                    continue
                t = tt(X[k][:, :], X[k][:, :], R[:, :], ALU.mult, NS.tR, xtok[k], q=PO if k in FIN_MUL else DV)
                if k in FIN_TS:
                    xtok[k] = ts(X[k][:, :], X[k][:, :], gcol, bcol, ALU.mult, ALU.add, t)
                else:
                    yield [t]
                    xtok[k] = act(X[k][:, :], X[k][:, :], ACT.Identity, t, scale=gcol, bias=bcol)

        def true_h(k):
            while HP.nrd[k] < NFIX:
                yield None
            yield [HP.rd[k], xtok[k]]
            th = act(H.hi[k], X[k][:, :], ACT.Copy, xtok[k], HP.rd[k])
            yield [th]
            H.tl[k] = tt(H.lo[k], X[k][:, :], H.hi[k].bitcast(FP), ALU.subtract, th, HP.rd[k])
            H.th[k] = th

        FX = Ring([Buf(big(96, 512)), Buf(big(108, 512))])
        FXG = [big(92, 512), big(94, 512)]
        NORMS = [("ln1", 0), ("ln2", 0), ("ln3", 0), ("ln1", 1), ("ln2", 1)]
        s_fx = [sem() for _ in range(3)]
        fx_tok = {}
        fx_read = [[] for _ in range(3)]

        def weight_sums(norm):
            i = NORMS.index(norm)
            base = 4 * NFIX * (i % 3)
            f = [FX.f]
            for hf in range(2):
                for p in range(2):
                    tg = SP.dma(FXG[p][:, :], a["gb"][i, 1024 * p + 512 * hf:1024 * p + 512 * hf + 512]
                                .unsqueeze(0).broadcast_to([128, 512]), s_fx[2], f)
                for j in range(NFIX):
                    z = yield from FX.get()
                    k = FX.all.index(z)
                    t = SP.dma(z.ap[:, :], a["wfix"][i, j, :, 512 * hf:512 * hf + 512], s_fx[k], z.free)
                    yield [t, tg]
                    b = yield from bank()
                    t1 = None
                    for p in range(2):
                        o = fxt[:, base + 4 * j + 2 * hf + p:base + 4 * j + 2 * hf + p + 1]
                        t1 = DV.do(lambda e, z=z, b=b, p=p, o=o: e.scalar_tensor_tensor(
                            out=b.ap[:, :], in0=z.ap[:, :], scalar=1.0, in1=FXG[p][:, :], op0=ALU.mult, op1=ALU.mult,
                            accum_out=o), t, tg, t1, b.free, fx_read[i % 3], cost=662)
                    banks.put(b, t1)
                    FX.put(z, t1)
                f = [t1]
            FX.f = f
            yield [t1]
            v = fxt[:, base:base + 4 * NFIX].rearrange("p (j h c) -> p j h c", h=2, c=2)
            fx_tok[norm] = tt(v[:, :, 0, :], v[:, :, 0, :], v[:, :, 1, :], ALU.add, t1)

        def fixed(norm, j, b, t, ring, two=None):
            i = NORMS.index(norm)
            c = 4 * NFIX * (i % 3) + 4 * j
            while H.tl[7] is None:
                yield None
            z = two if two else (yield from ring.get())
            t1 = stt(z.ap[:, :], L_M[:, :], fxt[:, c:c + 1], b.ap[:, :], ALU.mult, ALU.add, t, LN.tM, fx_tok[norm], z.free)
            banks.put(b, t1)
            fx_read[i % 3] = fx_read[i % 3][-NFIX + 1:] + [t1]
            t1 = tt(z.ap[:, :], z.ap[:, :], R[:, :], ALU.mult, t1, NS.tR)
            return z, t1, fxt[:, c + 1:c + 2]

        def ffn_b(l, which):
            gu, dn = a[f"wgu{which + 1}"], a[f"wd{which + 1}"]
            nm = "ln1" if which == 1 else "ln3"
            begins = which == 1 and l == 0

            def acc(n, b, t):
                ln_acc(n, b, t, 2.0 * ALPHA, nm, l, stop == f"b{l}{nm}" or (which == 2 and l == 1))

            def before():
                def sums():
                    while not NS.R_ready or H.tl[7] is None:
                        yield None
                    FX.f = fence()
                    FX.renew(FX.f)
                    for norm in ((("ln1", l), ("ln2", l)) if which == 1 else (("ln3", l),)):
                        if norm in NORMS:
                            yield from weight_sums(norm)
                spawn(sums())
                if not begins:
                    return

                def g():
                    while not NS.R_ready or H.tl[7] is None:
                        yield None
                    for k in range(8):
                        xtok[k] = stt(X[k][:, :], X[k][:, :], col("final_norm", k), R[:, :], ALU.mult, ALU.mult,
                                      xtok[k], NS.tR, H.th[k], H.tl[k])
                        yield [xtok[k]]
                spawn(g())
            ffn(lambda n, u: gu[l, 2 * n + u], lambda n: dn[l, n], acc, begins, before,
                None if begins else ("ln3", l - 1) if which == 1 else ("ln2", l))

        MX = Acts([big(2 * i, 512, FR)[:, :] for i in range(8)], [big(16 + 2 * i, 512, FR)[:, :] for i in range(8)])
        q2 = [[big(32 + 4 * i + 2 * j, 512, FR) for j in range(2)] for i in range(4)]
        k2 = [big(o, 512, FR) for o in (48, 50, 103)]
        v2 = [big(52 + 2 * j, 512) for j in range(2)]
        e2 = Ring([Buf(big(56 + 1.5 * i, 384)) for i in range(4)])
        w2 = Ring([Buf(big(62 + 1.5 * i, 384)) for i in range(4)])
        p2 = Ring([Buf((big(68 + 3 * i, 384), big(69.5 + 3 * i, 384))) for i in range(2)])
        up = [big(74 + 2.25 * i, 542) for i in range(4)]
        cacc = [big(83 + 2 * i, 512) for i in range(2)]
        cpo = [big(87 + 2 * i, 512) for i in range(2)]
        cpr = Ring([Buf(big(91 + 2 * i, 512)) for i in range(2)])
        TM2 = Ring([Buf(big(o, 512)) for o in (95, 97, 99, 101, 105, 107)])
        c_sq, c_mu = L_s1, L_s2
        CN = Ring([Buf(RS)])
        C2, S2 = C_t, S_t
        s_tb = sem()

        def mixer_b(l):
            M = State()

            def before():
                f = fence()
                M.f = f
                for r_ in (e2, w2, p2, cpr, TM2):
                    r_.renew(f)
                tz = []
                for u, n in ((up[0], 15), (up[1], 15), (up[2], 1), (up[3], 1)):
                    for c0 in (0, 512 + n):
                        PO.do(lambda e, u=u, c0=c0, n=n: e.memset(u[:, c0:c0 + n], 0.0), f)
                for i in range(2):
                    M.tz = PO.do(lambda e, i=i: e.memset(v2[i][:, :], 0.0), f, cost=300)
                if l == 0:
                    SP.dma(C2[:, :], a["tab2"][:, 0:512], s_tb, f)
                    NS.ttab = SP.dma(S2[:, :], a["tab2"][:, 512:1024], s_tb, f)

            def rope2(b, tok, f, dst, out, j=NFIX):
                if j < NFIX:
                    while H.tl[7] is None:
                        yield None
                z, w = yield from TM2.get2()
                if j < NFIX:
                    _, t, wb = yield from fixed(("ln1", l), j, b, tok, TM2, z)
                    t = ts(z.ap[:, :], z.ap[:, :], wb, None, ALU.add, None, t)
                    x_ = z.ap
                else:
                    x_, t = b.ap, tok
                t2 = swap(w.ap[:, :], x_[:, :], 16, t, w.free)
                t3 = tt(z.ap[:, :], x_[:, :], C2[:, :], ALU.mult, t, t2, NS.ttab, z.free)
                if j >= NFIX:
                    banks.put(b, t3)
                yield [t3]
                t2 = tt(w.ap[:, :], w.ap[:, :], S2[:, :], ALU.mult, t2, NS.ttab)
                t4 = tt(z.ap[:, :], z.ap[:, :], w.ap[:, :], ALU.add, t3, t2)
                TM2.put(w, t4)
                yield [t4]
                tl = yield from f(dst, z.ap, t4, M.f)
                TM2.put(z, tl)
                out[:] = tl

            def ev_k(b, t):
                M.k = []
                spawn(rope2(b[0], t, split_k, k2, M.k, 0))

            def ev_v(b, t):
                def g():
                    z, t1, wb = yield from fixed(("ln1", l), 1, b[0], t, TM2)
                    yield [t1]
                    t1 = act(z.ap[:, :], z.ap[:, :], ACT.Identity, t1, bias=wb)
                    yield [t1]
                    s_ = yield from bank()
                    for j in range(4):
                        t2 = tr(s_.ap[:, 128 * j:128 * j + 128], z.ap[:, 128 * j:128 * j + 128], t1, s_.free, sig=(j == 3))
                    TM2.put(z, t2)
                    yield [t2]
                    hv = lambda x_, i: x_[:, :].rearrange("p (j h c) -> p j h c", j=4, h=2)[:, :, i, :]
                    t0 = act(hv(v2[0], 0), hv(s_.ap, 0), ACT.Copy, t2, M.tz)
                    t1 = act(hv(v2[1], 1), hv(s_.ap, 1), ACT.Copy, t2, M.tz)
                    M.v = [t0, t1]
                    banks.put(s_, t1)
                spawn(g())

            M.q = [[] for _ in range(4)]

            def unit(p, qt):
                k0, k1 = max(qt - 1, 0), min(qt + 2, 4)
                nk = 128 * (k1 - k0)
                sm = yield from st_ring.get()
                mx, ng, su, r_ = (sm.ap[:, 2 * i:2 * i + 2] for i in range(4))
                qs = slice(128 * qt, 128 * qt + 128)
                ks = slice(128 * k0, 128 * k1)
                sk, nsk = (x_[:, 8 * l:8 * l + 8].rearrange("p (c i) -> p c i", c=2)[:, :, p] for x_ in (sink, nsink))
                bs, es = [], []
                for c in range(2):
                    b = yield from bank()

                    def window():
                        if qt > 0:
                            mm(b.ap[:, 0:128], identb[:, :], wmask[:, 0:128], False, False, NS.t_wm)
                        if qt < 3:
                            mm(b.ap[:, nk - 128:nk], identb[:, :], wmask[:, 128:256], False, False, NS.t_wm)
                    t = score(b.ap[:, 0:nk], q2[p], k2, c, qs, ks, window, M.q[p], M.k, b.free)
                    bs.append((b, t))
                M.nsc += 1
                for c, (b, t) in enumerate(bs):
                    yield [t]
                    tm = reduce_max(mx[:, c:c + 1], b.ap[:, 0:nk], t, sm.free)
                tn = DV.do(lambda e: e.scalar_tensor_tensor(out=ng, in0=mx, scalar=-0.125, in1=nsk, op0=ALU.mult,
                                                            op1=ALU.min), tm, NS.t_ns)
                tx = tt(mx, sk, ng, ALU.add, tn, NS.t_q)
                yield [tn]
                for c, (b, t) in enumerate(bs):
                    e_ = yield from e2.get()
                    te = act(e_.ap[:, 0:nk], b.ap[:, 0:nk], ACT.Exp, tn, e_.free, bias=ng[:, c:c + 1], scale=0.125,
                             accum=su[:, c:c + 1])
                    banks.put(b, te)
                    es.append(e_)
                M.holds -= 1
                te = act(mx, mx, ACT.Exp, tx)
                yield [te]
                t = tt(su, su, mx, ALU.add, te)
                t = DV.do(lambda e: e.reciprocal(r_, su), t, cost=81)
                ws = []
                for c in range(2):
                    w_ = yield from w2.get()
                    tw = ts(w_.ap[:, 0:nk], es[c].ap[:, 0:nk], r_[:, c:c + 1], None, ALU.mult, None, t, w_.free)
                    e2.put(es[c], tw)
                    ws.append((w_, tw))
                st_ring.put(sm, tw)
                pt = yield from p2.get()
                tp = []
                for c in range(2):
                    yield [ws[c][1]]
                    b = yield from bank()
                    for j in range(k1 - k0):
                        s_ = slice(128 * j, 128 * j + 128)
                        t = tr(b.ap[:, s_], ws[c][0].ap[:, s_], ws[c][1], b.free, sig=(j == k1 - k0 - 1))
                    w2.put(ws[c][0], t)
                    yield [t]
                    t = act(pt.ap[c][:, 0:nk], b.ap[:, 0:nk], ACT.Copy, t, pt.free)
                    banks.put(b, t)
                    tp.append(t)
                yield tp + M.v
                b = yield from bank()
                n_ = 0
                for c in range(2):
                    for j in range(k1 - k0):
                        t = mm(b.ap[:, 0:128], v2[c][:, 128 * (k0 + j):128 * (k0 + j) + 128],
                               pt.ap[c][:, 128 * j:128 * j + 128], n_ == 0, n_ == 2 * (k1 - k0) - 1, tp, M.v, b.free,
                               sig=(n_ == 2 * (k1 - k0) - 1))
                        n_ += 1
                p2.put(pt, t)
                yield [t]
                th = act(MX.hi[2 + p][:, qs], b.ap[:, 0:128], ACT.Copy, t, M.f)
                yield [th]
                tl = tt(MX.lo[2 + p][:, qs], b.ap[:, 0:128], MX.hi[2 + p][:, qs].bitcast(FP), ALU.subtract, th, M.f)
                banks.put(b, tl)
                M.att[p] += [th, tl]
                if len(M.att[p]) == 8:
                    MX.th[2 + p] = MX.tl[2 + p] = M.att[p]

            def units():
                M.nsc = M.holds = 0
                n = 0
                for p in range(4):
                    while not M.q[p] or M.v is None or not M.k:
                        yield None
                    yield M.q[p] + M.k
                    for qt in range(4):
                        while M.holds >= HOLD:
                            yield None
                        M.holds += 1
                        spawn(unit(p, qt))
                        n += 1
                        while M.nsc < n:
                            yield None
            M.v = None
            M.att = [[] for _ in range(4)]

            def ev_q(b, t, p):
                spawn(rope2(b[0], t, split_q, q2[p], M.q[p], 2 if p == 0 else NFIX))
                if p == 0:
                    MX.reset()
                    spawn(units())

            def ev_sig(b, t, i):
                def g():
                    if 3 + 2 * i < NFIX:
                        z, t1, wb = yield from fixed(("ln1", l), 3 + 2 * i, b[0], t, TM2)
                        yield [t1]
                        t1 = act(z.ap[:, :], z.ap[:, :], ACT.Sigmoid, t1, bias=wb)
                    else:
                        z = yield from TM2.get()
                        t1 = act(z.ap[:, :], b[0].ap[:, :], ACT.Sigmoid, t, z.free)
                        banks.put(b[0], t1)
                    M.sg[i] = (z, t1)
                spawn(g())

            def ev_a(b, t, i):
                def g():
                    while M.sg[i] is None:
                        yield None
                    z, tz = M.sg[i]
                    if 4 + 2 * i < NFIX:
                        y, t1, wb = yield from fixed(("ln1", l), 4 + 2 * i, b[0], t, TM2)
                        t1 = stt(up[i][:, 15:527], y.ap[:, :], wb, z.ap[:, :], ALU.add, ALU.mult, t1, tz, M.tz)
                        TM2.put(y, t1)
                    else:
                        t1 = tt(up[i][:, 15:527], b[0].ap[:, :], z.ap[:, :], ALU.mult, t, tz, M.tz)
                        banks.put(b[0], t1)
                    TM2.put(z, t1)
                    yield from conv(i, t1)
                spawn(g())
            M.sg = [None] * 2
            M.cv = [None] * 2
            M.cp = [None] * 2


            def conv(i, tu):
                cw = lambda k: col("cc_w", 62 * l + 2 * k + i)
                ta = ts(cacc[i][:, :], up[i][:, NPO:NPO + 512], cw(NPO), col("cc_b", 2 * l + i), ALU.mult, ALU.add, tu, M.f)

                def on_pool():
                    tp = act(cpo[i][:, :], up[i][:, 0:512], ACT.Copy, tu, M.f, scale=cw(0))
                    for k in range(1, NPO):
                        z = yield from cpr.get()
                        yield [z.free]
                        t = act(z.ap[:, :], up[i][:, k:k + 512], ACT.Copy, tu, z.free, scale=cw(k))
                        tp = tt(cpo[i][:, :], cpo[i][:, :], z.ap[:, :], ALU.add, t, tp, q=PO)
                        cpr.put(z, tp)
                    M.cp[i] = tp
                M.cp[i] = None
                spawn(on_pool())
                for k in range(NPO + 1, 31):
                    yield [ta]
                    ta = stt(cacc[i][:, :], up[i][:, k:k + 512], cw(k), cacc[i][:, :], ALU.mult, ALU.add, ta)
                while M.cp[i] is None:
                    yield None
                yield [ta, M.cp[i]]
                ta = tt(cacc[i][:, :], cacc[i][:, :], cpo[i][:, :], ALU.add, ta, M.cp[i])
                M.cv[i] = ta
                if M.cv[1 - i] is not None:
                    yield from cc_norm()

            def cc_norm():
                yield M.cv
                while any(x is None for x in H.tl):
                    yield None
                M.f = fence()
                b = yield from bank()
                for i in range(2):
                    t = mm(b.ap[:, :], ones, cacc[i][:, :], i == 0, i == 1, M.cv[i], b.free, sig=(i == 1))
                yield [t]
                t = act(c_mu[:, :], b.ap[:, :], ACT.Copy, t, M.f, scale=1.0 / 256.0)
                banks.put(b, t)
                yield [t]
                td = [tt(cacc[i][:, :], cacc[i][:, :], c_mu[:, :], ALU.subtract, t) for i in range(2)]
                yield td
                z = yield from TM2.get()
                t0 = act(c_sq[:, :], cacc[0][:, :], ACT.Square, td[0], M.f)
                t1 = act(z.ap[:, :], cacc[1][:, :], ACT.Square, td[1], z.free)
                yield [t1]
                tq = tt(c_sq[:, :], c_sq[:, :], z.ap[:, :], ALU.add, t0, t1)
                TM2.put(z, tq)
                o = {}
                yield from rstd(c_sq, tq, 1.0 / 256.0, EPS_LN, o)
                for i in range(2):
                    td[i] = tt(cacc[i][:, :], cacc[i][:, :], o["bank"].ap[:, :], ALU.mult, o["tok"], td[i])
                banks.put(o["bank"], td[1])
                yield td
                for i in range(2):
                    td[i] = act(cacc[i][:, :], cacc[i][:, :], ACT.Silu, td[i], scale=col("cc_g", 2 * l + i),
                                bias=col("cc_lb", 2 * l + i))
                for i in range(2):
                    th = act(MX.hi[6 + i], cacc[i][:, :], ACT.Copy, td[i], M.f)
                    yield [th]
                    MX.tl[6 + i] = tt(MX.lo[6 + i], cacc[i][:, :], MX.hi[6 + i].bitcast(FP), ALU.subtract, th, M.f)
                    MX.th[6 + i] = th

            M.sc = [None] * 2

            def ev_c(b, t, i):
                def g():
                    z = yield from CN.get()
                    t1 = act(z.ap[:, :], b[0].ap[:, :], ACT.Copy, t, z.free)
                    M.sc[i] = (z, t1)
                    banks.put(b[0], t1)
                spawn(g())

            def ev_h(b, t, i):
                def g():
                    while M.sc[i] is None:
                        yield None
                    z, tz = M.sc[i]
                    t1 = tt(up[2 + i][:, 1:513], b[0].ap[:, :], z.ap[:, :], ALU.mult, t, tz, M.tz)
                    banks.put(b[0], t1)
                    cw = lambda k: col("sc_w", 6 * l + 2 * k + i)
                    t2 = ts(z.ap[:, :], up[2 + i][:, 0:512], cw(0), None, ALU.mult, None, t1)
                    for k in (1, 2):
                        yield [t2]
                        t2 = stt(z.ap[:, :], up[2 + i][:, k:k + 512], cw(k), z.ap[:, :], ALU.mult, ALU.add, t2)
                    M.sd[i] = (z, t2)
                spawn(g())
            M.sd = [None] * 2

            def ev_b(b, t, i):
                def g():
                    while M.sd[i] is None:
                        yield None
                    z, tz = M.sd[i]
                    t1 = tt(z.ap[:, :], b[0].ap[:, :], z.ap[:, :], ALU.mult, t, tz)
                    banks.put(b[0], t1)
                    yield [t1]
                    th = act(MX.hi[i], z.ap[:, :], ACT.Copy, t1, M.f)
                    yield [th]
                    MX.tl[i] = tt(MX.lo[i], z.ap[:, :], MX.hi[i].bitcast(FP), ALU.subtract, th, M.f)
                    MX.th[i] = th
                    CN.put(z, MX.tl[i])
                spawn(g())

            evs = [(10, ev_k), (11, ev_v)]
            evs += [(6, lambda b, t: ev_q(b, t, 0))]
            evs += [(14 + i, lambda b, t, i=i: ev_sig(b, t, i)) if j == 0 else (12 + i, lambda b, t, i=i: ev_a(b, t, i))
                    for i in range(2) for j in range(2)]
            evs += [(6 + i, lambda b, t, i=i: ev_q(b, t, i)) for i in range(1, 4)]
            for i in range(2):
                evs += [(2 + i, lambda b, t, i=i: ev_c(b, t, i)), (4 + i, lambda b, t, i=i: ev_h(b, t, i)),
                        (i, lambda b, t, i=i: ev_b(b, t, i))]
            for n, (tile, ev) in enumerate(evs):
                up_job(a["win2"][l, tile], n, ("ln1", l), ev, before if n == 0 else None)
            order = [0, 1, 2, 3, 6, 7, 4, 5]

            def bef4():
                NS.reserve = 2

            def ev4(b, t):
                NS.reserve = 3
                ln_start()
                for n in range(4):
                    ln_acc(n, b[n], t, ALPHA, "ln2", l, stop == f"b{l}ln2")
            job([(a["wout2"][l, c], 1024, [(4 * i + n, MX, order[2 * c + i], n, c == i == 0, c == 3 and i == 1)
                                           for i in range(2) for n in range(4)]) for c in range(4)], 4, ev4, bef4)
            for n in range(4, 8):
                def ev(b, t, n=n):
                    ln_acc(n, b[0], t, ALPHA, "ln2", l, stop == f"b{l}ln2")
                job([(a["wout2"][l, n], 1024, [(k, MX, k, 0, k == order[0], k == order[-1]) for k in order])], 1, ev)

        stages = [("mix0", lambda: first_block(0)), ("ffn0", lambda: ffn_a(0)), ("mix1", lambda: first_block(1)),
                  ("ffn1", lambda: ffn_a(1)),
                  ("b0ln1", lambda: ffn_b(0, 1)), ("b0ln2", lambda: mixer_b(0)), ("b0ln3", lambda: ffn_b(0, 2)),
                  ("b1ln1", lambda: ffn_b(1, 1)), ("b1ln2", lambda: mixer_b(1)), ("b1ln3", lambda: ffn_b(1, 2))]
        for name, f in stages:
            f()
            if name == stop:
                break
        early_loads()
        spawn(prep(0), first)
        spawn(prep(1), first)
        run_jobs()
        settle()
        s_o = sem()
        for k in range(8):
            t_o = SP.dma(a["out"][:, 512 * k:512 * k + 512], X[k][:, :], s_o, xtok[k])

        block = ctx.enter_context(nc.Block())

        @block.sync
        def _(e):
            SP.emit(e)
            e.wait_ge(t_o[0].h, t_o[1])

        @block.scalar
        def _(e):
            AC.emit(e)

        @block.vector
        def _(e):
            DV.emit(e)

        @block.gpsimd
        def _(e):
            PO.emit(e)

        @block.tensor
        def _(e):
            PE.emit(e)
    return P


SCRATCH = 4096
BASE = (SCRATCH + 97 + 31) // 32 * 32
LIMIT = 229344


def host(inputs):
    f = lambda n: np.asarray(inputs[n])
    col = lambda v: np.ascontiguousarray(v.reshape(-1, 128).T)
    gb = lambda n: np.stack([f(n + "_g_2").reshape(16, 128), f(n + "_b_2").reshape(16, 128)], axis=1)
    parts = [f("attn_norm"), f("ffn_norm"), f("final_norm"), f("da_norm"), f("hg_norm"), f("hg_lb_logits"),
             gb("ln1"), gb("ln2"), gb("ln3"), f("sc_conv_w_2"), f("cc_conv_w_2"), f("cc_conv_b_2"), f("cc_ln_g_2"), f("cc_ln_b_2")]
    cols = [col(p) for p in parts]
    invf = (500000.0 ** (-(np.arange(0, 16, 2, dtype=np.float32) / np.float32(16)))).astype(np.float32)
    iv = np.zeros((128, 1), np.float32)
    for c in range(2):
        for j in range(16):
            iv[64 * c + j, 0] = invf[j % 8]
    sg = np.ones((128, 1), np.float32)
    for c in range(2):
        sg[64 * c:64 * c + 8, 0] = -1.0
    prm = np.concatenate(cols + [iv, sg], axis=1)
    assert prm.shape[1] == NPRM, (prm.shape, NPRM)
    cst = np.concatenate([np.eye(128, dtype=np.float32), np.ones((128, 128), np.float32)], axis=1)
    sel = np.repeat(np.tile(np.eye(4, dtype=np.float32), (2, 1)), 128, axis=1)
    j = np.arange(128)[:, None]
    t = np.arange(128)[None, :]

    ms = []
    for n in (128, 64, 32, 16, 8, 4, 2):
        ms.append((j // n == t // n) & ((j % n < n // 2) != (t % n < n // 2)))
    msk = np.concatenate(ms, axis=1).astype(np.float32)
    c8 = lambda w: np.ascontiguousarray(w.reshape(2, 8, 128, -1, 128).transpose(0, 3, 2, 1, 4)).reshape(2, -1, 128, 1024)
    c4 = lambda w: w.reshape(2, 4, 128, 8, 128).transpose(0, 3, 2, 1, 4)
    gu = lambda g, u: np.ascontiguousarray(np.stack([c8(g), c8(u)], axis=2)).reshape(2, 44, 128, 1024)
    dn = lambda w: np.ascontiguousarray(w.reshape(2, 22, 128, 8, 128).transpose(0, 3, 2, 1, 4)).reshape(2, 8, 128, 2816)
    hd = np.concatenate([np.r_[16 * u:16 * u + 16, 32 + 16 * u:48 + 16 * u] for u in range(2)])
    hq = np.concatenate([np.concatenate([np.arange(64 * i, 64 * i + 64), np.arange(64 * (i + 4), 64 * (i + 4) + 64)])
                         for i in range(4)])
    cols_ = np.arange(2048)
    cols_[768:1280] = 768 + hq.reshape(8, 64)[:, hd].reshape(-1)
    cols_[1280:1408] = 1280 + np.arange(128).reshape(2, 64)[:, hd].reshape(-1)
    rows_ = np.arange(1024)
    rows_[256:768] = 256 + hq
    win2 = f("w_in_2")[:, :, cols_]
    wout2 = f("w_out_2")[:, rows_, :]
    inv2 = (10000.0 ** (-np.arange(32, dtype=np.float32) / np.float32(32))).astype(np.float32)
    ang = np.arange(512, dtype=np.float32)[None, :] * inv2[np.tile(hd, 2) % 32][:, None]
    sg2 = np.where(np.arange(128) % 32 < 16, -1.0, 1.0)[:, None]
    tab2 = np.concatenate([np.cos(ang.astype(np.float64)), sg2 * np.sin(ang.astype(np.float64))], axis=1).astype(np.float32)
    wm = np.concatenate([np.where(t < j, -1e30, 0.0), np.where(t > j, -1e30, 0.0), np.zeros((128, 128))],
                        axis=1).astype(np.float32)
    wo2 = np.array(c8(wout2))
    w8 = wout2.reshape(2, 8, 128, 8, 128)
    for c in range(4):
        for i in range(2):
            for n in range(4):
                wo2[:, c, :, 128 * (4 * i + n):128 * (4 * i + n + 1)] = w8[:, [0, 1, 2, 3, 6, 7, 4, 5][2 * c + i], :, n, :]
    gu2 = lambda w: gu(w[:, :, :2816], w[:, :, 2816:])
    wgu1, wgu2, wi2 = gu2(f("ffn1_w_gu_2")), gu2(f("ffn2_w_gu_2")), c8(win2)
    first = [10, 11, 6, 14, 12, 15, 13][:NFIX]
    nat = lambda w: w.reshape(128, 8, 128).transpose(2, 1, 0).reshape(128, 1024)
    wfix = [[wi2[0, t] for t in first], [wgu2[0, j] for j in range(NFIX)], [wgu1[1, j] for j in range(NFIX)],
            [wi2[1, t] for t in first], [wgu2[1, j] for j in range(NFIX)]]
    wfix = np.stack([np.stack([nat(w) for w in ws]) for ws in wfix])
    gbr = np.stack([np.concatenate([f(n + "_g_2")[l], f(n + "_b_2")[l]]) for n, l in
                    (("ln1", 0), ("ln2", 0), ("ln3", 0), ("ln1", 1), ("ln2", 1))])
    x = f("x")[0]
    arr = {
        "wfix": np.ascontiguousarray(wfix), "gb": np.ascontiguousarray(gbr),
        "xT": np.ascontiguousarray(x.T.reshape(8, 128, 512).transpose(1, 0, 2)).reshape(128, 4096),
        "pos": np.ascontiguousarray(f("positions")).astype(np.int32, copy=False),
        "prm": np.ascontiguousarray(prm),
        "lam": np.ascontiguousarray(f("da_lambda").reshape(1, 512)),
        "cst": np.ascontiguousarray(cst), "sel": sel, "msk": np.ascontiguousarray(msk),
        "win1": c8(f("w_in")),
        "wab": np.ascontiguousarray(np.concatenate([c4(f("w_a")), c4(f("w_b"))], axis=3)).reshape(2, 8, 128, 1024),
        "wo": c8(f("w_o")), "wgu1": gu(f("w_gate"), f("w_up")), "wd1": dn(f("w_down")),
        "sink": np.ascontiguousarray(f("attn_sink_2").reshape(1, 16)), "wmask": wm, "tab2": tab2,
        "wgu2": wgu1, "wd2": dn(f("ffn1_w_down_2")),
        "wgu3": wgu2, "wd3": dn(f("ffn2_w_down_2")),
        "win2": wi2, "wout2": wo2,
    }
    return arr


def kernel(**inputs):
    import concourse.bacc as bacc
    from concourse.bass_utils import run_bass_kernel_spmd as run
    nc = bacc.Bacc("TRN2", target_bir_lowering=False, num_devices=1, dynamic_dma_scratch_size=SCRATCH)
    arr = host(inputs)
    aps = {n: nc.dram_tensor(n, v.shape, mybir.dt.from_np(v.dtype), kind="ExternalInput").ap() for n, v in arr.items()}
    aps["out"] = nc.dram_tensor("out", (128, 4096), FP, kind="ExternalOutput").ap()
    aps["scr"] = nc.dram_tensor("scr", (128, 4096), FP).ap()
    build_program(nc, aps)
    r = run(nc, [arr], core_ids=[0])
    o = r.results[0]["out"]
    return np.ascontiguousarray(o.reshape(128, 8, 512).transpose(1, 0, 2).reshape(1024, 512).T).reshape(1, 512, 1024)
```
